# Optimizing a Trainium2 kernel written in Bass

```python
import math
import jax, jax.numpy as jnp
from jax import lax
import numpy as np

D_MODEL = 2048
BATCH = 1
SEQ = 512
DEPTH = 1

CTX_LEN = 256
GRID_W = 64
W_CONV = 1024
CONV_K = 3
SSM_H = 16
SSM_P = 64
W_SSM = 1024
SSM_G = W_SSM // SSM_H
W_FFT = 1024
FFT_GROUPS = 4
FFT_GW = W_FFT // FFT_GROUPS
N_BRANCH = 3
RMS_EPS = 1e-6
U_OFF = 4 * W_CONV
IN_WIDTH = 4 * W_CONV + 2 * W_SSM + 2 * W_FFT + N_BRANCH * D_MODEL

kernel_name = "hybrid_conv_s5_fnet_parallel_dit_block"

def _split_proj(p):
    idx = [W_CONV, 2 * W_CONV, 3 * W_CONV, 4 * W_CONV,
           4 * W_CONV + W_SSM, 4 * W_CONV + 2 * W_SSM,
           4 * W_CONV + 2 * W_SSM + W_FFT, 4 * W_CONV + 2 * W_SSM + 2 * W_FFT]
    return jnp.split(p, idx, axis=-1)

def _rmsnorm(x, g):
    x32 = x.astype(jnp.float32)
    y = x32 * lax.rsqrt(jnp.mean(x32 * x32, axis=-1, keepdims=True) + RMS_EPS)
    return (y * g.astype(jnp.float32)).astype(x.dtype)

def _short_conv(v, w):
    ch = v.shape[-1]
    return lax.conv_general_dilated(
        v, w[:, None, :].astype(v.dtype), window_strides=(1,), padding=((1, 1),),
        dimension_numbers=('NWC', 'WIO', 'NWC'), feature_group_count=ch)

def _conv_branch(xa, ba, ca, za, w, on_grid):
    v = ca * xa
    if on_grid:
        bn, t, ch = v.shape
        rows = t // GRID_W
        y = _short_conv(v.reshape(bn * rows, GRID_W, ch), w).reshape(bn, t, ch)
    else:
        y = _short_conv(v, w)
    return ba * y * jax.nn.silu(za)

def _fourier_mix(f):
    bn, t, _ = f.shape
    fg = f.astype(jnp.float32).reshape(bn, t, FFT_GROUPS, FFT_GW)
    y = jnp.fft.fft2(fg, axes=(1, 3), norm='ortho').real
    return y.reshape(bn, t, W_FFT).astype(f.dtype)

def _zoh(lam_re, lam_im, log_dt, b_re, b_im):
    lam_re = lam_re.astype(jnp.float32)
    lam_im = lam_im.astype(jnp.float32)
    b_re = b_re.astype(jnp.float32)
    b_im = b_im.astype(jnp.float32)
    dt = jnp.exp(log_dt.astype(jnp.float32))[:, None]
    mag = jnp.exp(lam_re * dt)
    ang = lam_im * dt
    a_re = mag * jnp.cos(ang)
    a_im = mag * jnp.sin(ang)
    n_re = a_re - 1.0
    n_im = a_im
    den = lam_re * lam_re + lam_im * lam_im
    q_re = (n_re * lam_re + n_im * lam_im) / den
    q_im = (n_im * lam_re - n_re * lam_im) / den
    bb_re = q_re[..., None] * b_re - q_im[..., None] * b_im
    bb_im = q_re[..., None] * b_im + q_im[..., None] * b_re
    return a_re, a_im, bb_re, bb_im

def _combine(e1, e2):
    a1r, a1i, b1r, b1i = e1
    a2r, a2i, b2r, b2i = e2
    return (a2r * a1r - a2i * a1i,
            a2r * a1i + a2i * a1r,
            a2r * b1r - a2i * b1i + b2r,
            a2r * b1i + a2i * b1r + b2i)

def _scan_states(u_g, a_re, a_im, bb_re, bb_im, h0, reverse):
    s_re = jnp.einsum('btgh,gph->btgp', u_g, bb_re)
    s_im = jnp.einsum('btgh,gph->btgp', u_g, bb_im)
    if h0 is not None:
        h_re, h_im = h0
        edge = -1 if reverse else 0
        s_re = s_re.at[:, edge].add(a_re * h_re - a_im * h_im)
        s_im = s_im.at[:, edge].add(a_re * h_im + a_im * h_re)
    t = u_g.shape[1]
    ar = jnp.broadcast_to(a_re, (1, t) + a_re.shape)
    ai = jnp.broadcast_to(a_im, (1, t) + a_im.shape)
    _, _, x_re, x_im = lax.associative_scan(_combine, (ar, ai, s_re, s_im), reverse=reverse, axis=1)
    return x_re, x_im

def _readout(x_re, x_im, c_re, c_im):
    y = (jnp.einsum('btgp,ghp->btgh', x_re, c_re.astype(jnp.float32))
         - jnp.einsum('btgp,ghp->btgh', x_im, c_im.astype(jnp.float32)))
    return y.reshape(y.shape[0], y.shape[1], W_SSM)

def _branches_out(s, parts, y_ssm, on_grid, gate, conv_w, ssm_d, glu_wa, glu_wb,
                  fourier_w, proj_a, proj_b, proj_c, w_out, g_post):
    xa, ba, ca, za, u, zb, f, zc, gl = parts
    ya = _conv_branch(xa, ba, ca, za, conv_w, on_grid) @ proj_a
    y = y_ssm.astype(u.dtype) + ssm_d * u
    y = jax.nn.gelu(y)
    y = (y @ glu_wa) * jax.nn.sigmoid(y @ glu_wb) * jax.nn.silu(zb)
    yb = y @ proj_b
    yc = ((_fourier_mix(f) @ fourier_w) * jax.nn.silu(zc)) @ proj_c
    g = jax.nn.sigmoid(gl).reshape(gl.shape[:-1] + (N_BRANCH, D_MODEL))
    m = g[..., 0, :] * ya + g[..., 1, :] * yb + g[..., 2, :] * yc
    o = m @ w_out
    return s + gate * _rmsnorm(o, g_post)

def setup_inputs(seed: int = 0) -> dict:
    key = jax.random.key(seed)
    ks = jax.random.split(key, 26)
    f32 = jnp.float32
    nrm = lambda k, shape, std: jax.random.normal(k, shape, f32) * std
    inp = {}
    inp['x'] = nrm(ks[0], (BATCH, SEQ, D_MODEL), 1.0)
    inp['c'] = nrm(ks[1], (BATCH, D_MODEL), 1.0)
    inp['ctx'] = nrm(ks[2], (BATCH, CTX_LEN, D_MODEL), 1.0)
    inp['c_ctx'] = nrm(ks[3], (D_MODEL,), 1.0)
    inp['w_ada'] = nrm(ks[4], (DEPTH, D_MODEL, 3 * D_MODEL), 0.5 * D_MODEL ** -0.5)
    inp['b_ada'] = nrm(ks[5], (DEPTH, 3 * D_MODEL), 0.01)
    inp['g_pre'] = 1.0 + nrm(ks[6], (DEPTH, D_MODEL), 0.02)
    inp['g_post'] = 1.0 + nrm(ks[7], (DEPTH, D_MODEL), 0.02)
    inp['w_in'] = nrm(ks[8], (DEPTH, D_MODEL, IN_WIDTH), D_MODEL ** -0.5)
    inp['conv_w'] = nrm(ks[9], (DEPTH, CONV_K, W_CONV), CONV_K ** -0.5)
    inp['ssm_lam_re'] = -0.5 + nrm(ks[10], (DEPTH, 2, SSM_G, SSM_P), 0.01)
    inp['ssm_lam_im'] = (math.pi * jnp.arange(SSM_P, dtype=f32)
                         + nrm(ks[11], (DEPTH, 2, SSM_G, SSM_P), 0.01))
    inp['ssm_log_dt'] = jax.random.uniform(ks[12], (DEPTH, 2, SSM_G), f32,
                                           minval=math.log(1e-3), maxval=math.log(1e-1))
    inp['ssm_b_re'] = nrm(ks[13], (DEPTH, 2, SSM_G, SSM_P, SSM_H), (2 * SSM_H) ** -0.5)
    inp['ssm_b_im'] = nrm(ks[14], (DEPTH, 2, SSM_G, SSM_P, SSM_H), (2 * SSM_H) ** -0.5)
    inp['ssm_c_re'] = nrm(ks[15], (DEPTH, 2, SSM_G, SSM_H, SSM_P), SSM_P ** -0.5)
    inp['ssm_c_im'] = nrm(ks[16], (DEPTH, 2, SSM_G, SSM_H, SSM_P), SSM_P ** -0.5)
    inp['ssm_d'] = nrm(ks[17], (DEPTH, W_SSM), 1.0)
    inp['glu_wa'] = nrm(ks[18], (DEPTH, W_SSM, W_SSM), W_SSM ** -0.5)
    inp['glu_wb'] = nrm(ks[19], (DEPTH, W_SSM, W_SSM), W_SSM ** -0.5)
    inp['fourier_w'] = nrm(ks[20], (DEPTH, W_FFT, W_FFT), W_FFT ** -0.5)
    inp['proj_a'] = nrm(ks[21], (DEPTH, W_CONV, D_MODEL), W_CONV ** -0.5)
    inp['proj_b'] = nrm(ks[22], (DEPTH, W_SSM, D_MODEL), W_SSM ** -0.5)
    inp['proj_c'] = nrm(ks[23], (DEPTH, W_FFT, D_MODEL), W_FFT ** -0.5)
    inp['w_out'] = nrm(ks[24], (DEPTH, D_MODEL, D_MODEL), D_MODEL ** -0.5)
    return inp

def reference(x, c, ctx, c_ctx, w_ada, b_ada, g_pre, g_post, w_in, conv_w,
              ssm_lam_re, ssm_lam_im, ssm_log_dt, ssm_b_re, ssm_b_im, ssm_c_re, ssm_c_im,
              ssm_d, glu_wa, glu_wb, fourier_w, proj_a, proj_b, proj_c, w_out):
    bn, t, _ = x.shape
    lc = ctx.shape[1]
    for l in range(DEPTH):
        last = l == DEPTH - 1
        mod_x = jax.nn.silu(c) @ w_ada[l] + b_ada[l]
        sh_x, sc_x, gt_x = jnp.split(mod_x[:, None, :], 3, axis=-1)
        mod_c = jax.nn.silu(c_ctx) @ w_ada[l] + b_ada[l]
        sh_c, sc_c, gt_c = jnp.split(mod_c, 3)
        h_x = _rmsnorm(x, g_pre[l]) * (1 + sc_x) + sh_x
        h_c = _rmsnorm(ctx, g_pre[l]) * (1 + sc_c) + sh_c
        parts_x = _split_proj(h_x @ w_in[l])
        if last:
            parts_c = None
            u_c = h_c @ w_in[l][:, U_OFF:U_OFF + W_SSM]
        else:
            parts_c = _split_proj(h_c @ w_in[l])
            u_c = parts_c[4]
        u_c_g = u_c.astype(jnp.float32).reshape(bn, lc, SSM_G, SSM_H)
        u_x_g = parts_x[4].astype(jnp.float32).reshape(bn, t, SSM_G, SSM_H)
        ys_x = []
        ys_c = []
        for d in range(2):
            rev = d == 1
            disc = _zoh(ssm_lam_re[l, d], ssm_lam_im[l, d], ssm_log_dt[l, d],
                        ssm_b_re[l, d], ssm_b_im[l, d])
            cr, ci = _scan_states(u_c_g, *disc, None, rev)
            edge = 0 if rev else -1
            h0 = (cr[:, edge], ci[:, edge])
            xr, xi = _scan_states(u_x_g, *disc, h0, rev)
            ys_x.append(_readout(xr, xi, ssm_c_re[l, d], ssm_c_im[l, d]))
            if not last:
                ys_c.append(_readout(cr, ci, ssm_c_re[l, d], ssm_c_im[l, d]))
        new_x = _branches_out(x, parts_x, ys_x[0] + ys_x[1], True, gt_x, conv_w[l], ssm_d[l],
                              glu_wa[l], glu_wb[l], fourier_w[l], proj_a[l], proj_b[l],
                              proj_c[l], w_out[l], g_post[l])
        if not last:
            ctx = _branches_out(ctx, parts_c, ys_c[0] + ys_c[1], False, gt_c, conv_w[l], ssm_d[l],
                                glu_wa[l], glu_wb[l], fourier_w[l], proj_a[l], proj_b[l],
                                proj_c[l], w_out[l], g_post[l])
        x = new_x
    return x


_drawn_inputs = setup_inputs


def setup_inputs(seed=0):
    import zlib

    import numpy as np

    out = dict(_drawn_inputs(seed))
    spreads = {}
    factors = {'ctx': 64.0,
     'c_ctx': 64.0,
     'b_ada': 4.727,
     'g_pre': 5.057,
     'g_post': 67.201,
     'ssm_lam_re': 64.0,
     'ssm_lam_im': 37.824,
     'ssm_log_dt': 44.936,
     'ssm_b_re': 55.168,
     'ssm_b_im': 54.864,
     'ssm_c_re': 54.632,
     'ssm_c_im': 52.896,
     'ssm_d': 4.103,
     'glu_wa': 3.598,
     'glu_wb': 5.848,
     'proj_b': 3.57,
     'fourier_w': 2.997,
     'proj_c': 2.998}
    for name, (base, spread) in spreads.items():
        noise = np.random.default_rng([zlib.crc32(name.encode()), seed]).standard_normal(out[name].shape)
        drawn = base * np.exp(spread * noise) if base else spread * noise
        out[name] = __import__('jax').numpy.asarray(drawn.astype(out[name].dtype))
    for name, factor in factors.items():
        out[name] = (out[name] * factor).astype(out[name].dtype)
    return out
```

```python
import math

import numpy as np

import concourse.bass as bass
from concourse import mybir

F32 = mybir.dt.float32
I32 = mybir.dt.int32
ALU = mybir.AluOpType
ACT = mybir.ActivationFunctionType

D = 2048
T = 512
TC = 256
GRID = 64
W = 1024
H, P, G = 16, 64, 64
FG, FGW = 4, 256
EPS = 1e-6
KD, KW = D // 128, W // 128
TT, CT = T // 128, TC // 128
L = 8
NC, NX = TC // L, T // L
NQ = NC + NX
GB = 128 // H
NB = G // GB
PB = GB // 2
COL = dict(xa=0, ba=W, ca=2 * W, za=3 * W, u=4 * W, zb=5 * W, f=6 * W, zc=7 * W, gl=8 * W)
NSLOT = 4
UNIT = 8

V_BADA, V_GPRE, V_CONV, V_SSMD, V_C, V_CC, V_END = 0, 32, 48, 72, 80, 96, 112


class Count:

    def __init__(self, eng, sem):
        self.eng, self.sem, self.n, self.added = eng, sem, 0, 0

    def add(self, ins):
        ins.then_inc(self.sem, 1)
        self.n = self.n + 1
        self.added += 1
        return self.n

    def wait(self, n=None):
        self.eng.wait_ge(self.sem, self.n if n is None else n)

    def link(self, ins):
        self.add(ins)
        self.wait()


def repeat(eng, n, body, counts=(), peel=0):
    starts = [c.n for c, _ in counts]
    if ROLLED:
        for i in range(peel):
            body(i)
        with eng.Fori(peel, n) as i:
            for (c, per), s in zip(counts, starts):
                c.n = i * per + s
                before = c.added
            body(i)
            assert all(c.added - before == per for c, per in counts)
        for (c, per), s in zip(counts, starts):
            c.n = s + n * per
    else:
        for i in range(n):
            body(i)
            for (c, per), s in zip(counts, starts):
                assert c.n == s + (i + 1) * per, (c.n, s, i, per)


ROLLED = True


def sl(i, size):
    return bass.ds(i * size, size)


def program(nc, x, c, ctx, c_ctx, w_ada, b_ada, g_pre, g_post, w_in, conv_w, lam_re, lam_im, log_dt,
            b_re, b_im, c_re, c_im, ssm_d, glu_wa, glu_wb, fourier_w, proj_a, proj_b, proj_c, w_out,
            dft_w, dft_t, out):
    w_ada, w_in, conv_w = w_ada[0], w_in[0], conv_w[0]
    glu_wa, glu_wb, fourier_w = glu_wa[0], glu_wb[0], fourier_w[0]
    proj_a, proj_b, proj_c, w_out = proj_a[0], proj_b[0], proj_c[0], w_out[0]

    base = [(nc.sbuf_base + 31) // 32 * 32]
    top = nc.sbuf_usable_end

    def at(name, shape, off, dt=F32):
        n = int(np.prod(shape[1:])) * 4
        assert off + n <= top, (name, off, n, top)
        return nc.alloc_sbuf_tensor_at(name, shape, dt, offset=off)

    class Region:

        def __init__(self, start):
            self.p = start

        def __call__(self, name, shape, dt=F32):
            t = at(name, shape, self.p, dt)
            self.p += int(np.prod(shape[1:])) * 4
            self.p = (self.p + 31) // 32 * 32
            return t

    keep = Region(base[0])
    ident = keep("ident", [128, 128])
    vecs = keep("vecs", [128, V_END])
    cs = keep("cs", [128, KD, 2])
    small = keep("small", [128, 64])
    ones = keep("ones", [128, 128])
    vmod = keep("vmod", [128, 2, KD, 2])
    vcv = keep("vcv", [128, 24])
    wslot = keep("wslot", [128, NSLOT, UNIT * 128])
    hx = keep("hx", [128, KD, T])
    scan_at = keep.p

    r = Region(scan_at)
    uT = r("uT", [128, NB * (TC + T)])
    Ar = r("Ar", [128, L + 1, 128])
    Ai = r("Ai", [128, L + 1, 128])
    B1 = r("B1", [128, 128, H])
    C1 = r("C1", [128, 128, H])
    PWr = r("PWr", [128, 7, 64])
    PWi = r("PWi", [128, 7, 64])
    R8 = r("R8", [128, 64])
    Abr = r("Abr", [128, KW * T])
    block_at = r.p
    hc = r("hc", [128, KD, TC])
    start_at = r.p
    r = Region(block_at)
    V = r("V", [128, 2, GB, L * H])
    t1 = r("t1", [128, GB * (L + 1) * H * 2])
    Cp = r("Cp", [128, 2, GB, (L + 1) * H])
    VT = r("VT", [128, 2, GB, 128])
    Z = at("Z", [128, 2, 2, PB, NQ], r.p - 2 * GB * 128 * 4)
    M = r("M", [128, GB, 128])
    Tl = r("Tl", [16, GB, 15 * H])
    ut = r("ut", [NQ, GB, L, H])
    yt = at("yt", [NX, L, GB * H], r.p - GB * L * H * 4)
    U = r("U", [128, GB, NQ])
    S = r("S", [128, 2, 2, PB, NQ])
    PH = r("PH", [128, 2, 2, PB, NQ])
    X = r("X", [128, 2, PB, 2, NX])
    B2 = r("B2", [128, 2, GB, H])
    C2 = r("C2", [128, 2, GB, H])
    ucur = r("ucur", [128, TC + T])
    gph = r("gph", [128, 2, 8, 32])
    xas = r("xas", [128, T])
    cv = r("cv", [128, T])
    cy = r("cy", [128, T])
    sg = r("sg", [128, T])

    r = Region(start_at)
    xn = r("xn", [128, TT, D])
    ring = r("ring", [128, 4, 4, 512])
    vrow = r("vrow", [V_END, 128])
    lam = r("lam", [128, 2, P])
    ldt = r("ldt", [128, 1])
    ZN = r("ZN", [128, 7, 2, P])
    q2 = r("q2", [128, 2, 128])
    zt = [r(f"zt{i}", [128, P]) for i in range(8)]
    ei = r("ei", [128, P], I32)
    r = Region(scan_at)
    cn = r("cn", [128, CT, D])
    braw = r("braw", [128, 2, P * H])
    rows = at("rows", [2, 2 * D], block_at - KW * T * 4)
    r = Region(scan_at - KD * T * 4)
    craw = r("craw", [128, H, 2, P])
    Braw = r("Braw", [128, 128, H])
    Brw2 = r("Brw2", [128, 128, H])
    tq = r("tq", [128, 128, H])
    abr_at = block_at - KW * T * 4

    b2nd = at("b2nd", [128, KW * T], scan_at + NB * (TC + T) * 4)
    gacc = at("gacc", [128, D], scan_at + (NB * (TC + T) + KW * T) * 4)
    gwt1_at = abr_at + D * 4
    gwt = [at(f"gwt{i}", [128, D], abr_at + i * D * 4) for i in range(2)]
    r = Region(block_at)
    mT = r("mT", [128, KD * T])
    bact = r("bact", [128, KW * T])
    gsig = r("gsig", [128, T])
    gtm1 = r("gtm1", [128, T])
    gtm2 = r("gtm2", [128, T])
    dftt = r("dftt", [128, 2, TT, T])
    gprod = r("gprod", [128, D])
    r = Region(scan_at)
    pp = r("pp", [128, TT, 512])
    dftw = r("dftw", [128, 2, 512])
    r = Region(scan_at)
    Og = r("Og", [128, TT, D])
    GG = r("GG", [128, D])
    sqj = at("sqj", [128, 512], abr_at)
    ssq = at("ssq", [128, 16], abr_at + 2048)
    grow = at("grow", [1, D], block_at + (KD * T + KW * T + 3 * T + 2 * TT * T) * 4)
    baro = at("baro", [1, D], gwt1_at)
    xr = at("xr", [128, TT, D], block_at + KD * T * 4)

    ss = nc.alloc_psum_tensor("ss", [128, 4, 512], F32)
    ac = nc.alloc_psum_tensor("ac", [128, 4, 512], F32)

    sems = {}

    def sem(name):
        sems[name] = nc.alloc_semaphore(name)
        return sems[name]

    vec_in, x_in, ssm_in, b_in, ada_used = map(sem, ["vec_in", "x_in", "ssm_in", "b_in", "ada_used"])
    ada_in = [sem(f"ada_in{i}") for i in range(4)]
    w_in_s = [sem(f"w_in{i}") for i in range(NSLOT)]
    w_used = sem("w_used")
    dve_s, act_s, pool_s = map(sem, ["dve_steps", "act_steps", "pool_steps"])
    id_done, vec_ps, vec_cp, sg_done, cs_done = map(sem, ["id_done", "vec_ps", "vec_cp", "sg_done", "cs_done"])
    ada_ps, row_cp, col_ps, col_cp = map(sem, ["ada_ps", "row_cp", "col_ps", "col_cp"])
    zn_done, p0_ps, p0_cp, brw_done = map(sem, ["zn_done", "p0_ps", "p0_cp", "brw_done"])
    pw_tab, bb_done, var_done, rt_done, rs_done, y2_done = map(sem, "pw_tab bb_done var_done rt_done rs_done y2_done".split())
    y_done, h_ps, h_done = map(sem, ["y_done", "h_ps", "h_done"])
    ac_done = sem("ac_done")
    ac_free = [sem(f"ac_free{i}") for i in range(4)]
    (u_cur, ut_ps, ut_cp, u_ps, u_cp, v_done, vt_ps, vt_cp, s_ps, s_cp, k_ps, t_cp, t_add, cp_done, m_in,
     x_done, y_ps, yt_cp, yT_ps, y_pre, ph_done, xa_cp, sig_done, bc2) = map(sem, (
        "u_cur ut_ps ut_cp u_ps u_cp v_done vt_ps vt_cp s_ps s_cp k_ps t_cp t_add cp_done m_in "
        "x_done y_ps yt_cp yT_ps y_pre ph_done xa_cp sig_done bc2").split())
    a_done, gs_done, m_done, ge_in, ge_th, ge_done = map(sem, "a_done gs_done m_done ge_in ge_th ge_done".split())
    gl_sig, gl_done, pw_done, f_cp, p_cp, p_ps, f2_cp, dft_in, zc_sig, zc_done = map(
        sem, "gl_sig gl_done pw_done f_cp p_cp p_ps f2_cp dft_in zc_sig zc_done".split())
    gw_in = [sem(f"gw_in{i}") for i in range(2)]
    gw_used, gacc_done, gb_ps, gg_done, gp_in, o_cp, sq_done, o_done, xr_in, out_s, gpr_ps = map(
        sem, "gw_used gacc_done gb_ps gg_done gp_in o_cp sq_done o_done xr_in out_s gpr_ps".split())

    win = lambda col, n: [(w_in, 0, col, n), (w_in, 1024, col, n)]
    phases = []
    ph_u = (KW // 2, lambda i: [q for j in range(2) for q in win(COL["u"], (i, 2, j))])
    ph_conv = (NB, lambda i: [q for k in ("xa", "ca", "ba", "za") for q in win(COL[k], (i, 1, 0))])

    def ph_merge(branch, mat):
        return (KD // 4, lambda i: [q for j in range(4) for q in
                                    win(COL["gl"] + branch * D, (i, 4, j)) + [(mat, 0, 0, (i, 4, j))]])
    ph_glu = (KW // 4, lambda i: [q for j in range(4) for q in win(COL["zb"], (i, 4, j))
                                  + [(glu_wa, 0, 0, (i, 4, j)), (glu_wb, 0, 0, (i, 4, j))]])
    ph_f = (KW // 4, lambda i: [q for j in range(4) for q in win(COL["f"], (i, 4, j))])
    ph_fw = (KW // 4, lambda i: [q for j in range(4) for q in win(COL["zc"], (i, 4, j))
                                 + [(fourier_w, 0, 0, (i, 4, j))]])
    stream = [ph_u, ph_conv, ph_merge(0, proj_a), ph_glu, ph_merge(1, proj_b), ph_f, ph_fw, ph_merge(2, proj_c)]
    U0, A0 = [0], [0]
    ACCS = (4, 4, 8, 12, 8, 4, 8, 8)
    for (n, units), accs in zip(stream, ACCS):
        U0.append(U0[-1] + n * len(units(0)))
        A0.append(A0[-1] + n * accs)

    MIX = FG

    def freed(eng, k, i, a):
        eng.wait_ge(ac_free[a % 4], i * (ACCS[k] // 4) + ((A0[k] + a) // 4 + 1
                                                         + (MIX if k >= 6 and a % 4 < 2 else 0)))

    block = nc.Block()
    blk = block.__enter__()

    @blk.sync
    def _(sp):
        for rr, src in ((V_BADA, b_ada[0:1, 0:2 * D]), (V_GPRE, g_pre[0:1, :]), (V_CONV, conv_w),
                        (V_SSMD, ssm_d[0:1, :]), (V_C, c[0:1, :]), (V_CC, c_ctx.rearrange("(a n) -> a n", a=1))):
            n = src.shape[0] * src.shape[1] // 128
            sp.dma_start(vrow[rr:rr + n, :], src.rearrange("a (r p) -> (a r) p", p=128)).then_inc(vec_in, 16)
        for i, src in enumerate((lam_re, lam_im)):
            sp.dma_start(lam[:, i, :], src[0].rearrange("d g p -> (d g) p")).then_inc(ssm_in, 16)
        sp.dma_start(ldt[:, :], log_dt[0].rearrange("d (g a) -> (d g) a", a=1)).then_inc(ssm_in, 16)
        for i, src in enumerate((b_re, b_im)):
            sp.dma_start(braw[:, i, :], src[0].rearrange("d g p h -> (d g) (p h)")).then_inc(b_in, 16)
        for i, src in enumerate((c_re, c_im)):
            sp.dma_start(craw[:, :, i, :], src[0].rearrange("d g h p -> (d g) h p")).then_inc(b_in, 16)

        def ada_unit(n):
            q, k = n // 4, n % 4
            col = D + q * 512 if q < 4 else (q - 4) * 512
            if n >= 4:
                sp.wait_ge(ada_used, n - 3)
            sp.dma_start(ring[:, n % 4], w_ada[k * 512:(k + 1) * 512, col:col + 512]
                         .rearrange("(k p) c -> p k c", p=128)).then_inc(ada_in[n % 4], 16)
        for n in range(4):
            ada_unit(n)
        for t in range(TT):
            sp.dma_start(xn[:, t, :], x[0, t * 128:(t + 1) * 128, :]).then_inc(x_in, 16)
        for t in range(CT):
            sp.dma_start(cn[:, t, :], ctx[0, t * 128:(t + 1) * 128, :]).then_inc(x_in, 16)
        for n in range(4, 32):
            ada_unit(n)

        for k, (turns, units) in enumerate(stream):
            per = len(units(0))

            def body(i):
                for j, (mat, row, col, (ii, m, jj)) in enumerate(units(i)):
                    u = i * per + (U0[k] + j)
                    s = (U0[k] + j) % NSLOT
                    cc = (ii * m + jj) * 128 + col
                    if not isinstance(cc, int):
                        sp.compute_val(cc * 4)
                    if not isinstance(u, int) or u >= NSLOT:
                        sp.wait_ge(w_used, u - (NSLOT - 1))
                    cc = (ii * m + jj) * 128 + col
                    sp.dma_start(wslot[:, s, :].rearrange("p (k c) -> p k c", k=UNIT),
                                 mat[row:row + 1024, bass.ds(cc, 128)]
                                 .rearrange("(k p) c -> p k c", p=128)).then_inc(w_in_s[s], 16)
            repeat(sp, turns, body, peel=(1 if k == 0 else 0))
            if k == 4:
                sp.wait_ge(ge_done, 8)
                sp.dma_start(dftw[:, :, :], dft_w.rearrange("(k p) c -> p k c", p=128)).then_inc(dft_in, 16)
                sp.dma_start(dftt[:, :, :, :], dft_t.rearrange("a (k p) c -> p a k c", p=128)).then_inc(dft_in, 16)
        sp.wait_ge(gacc_done, 1)
        sp.dma_start(grow[0:1, :], g_post[0:1, :]).then_inc(gp_in, 16)
        sp.dma_start(baro[0:1, :], b_ada[0:1, 2 * D:3 * D]).then_inc(gp_in, 16)
        for cb in range(4):
            for j in range(8):
                u = U0[-1] + cb * 8 + j
                sp.wait_ge(w_used, u - (NSLOT - 1))
                sp.dma_start(wslot[:, u % NSLOT, :].rearrange("p (k c) -> p k c", k=2),
                             w_out[j * 256:(j + 1) * 256, cb * 512:(cb + 1) * 512]
                             .rearrange("(k p) c -> p k c", p=128)).then_inc(w_in_s[u % NSLOT], 16)
            if cb == 0:
                sp.wait_ge(m_done, 32)
                sp.wait_ge(gg_done, 2)
                for t in range(TT):
                    sp.dma_start(xr[:, t, :], x[0, t * 128:(t + 1) * 128, :]).then_inc(xr_in, 16)
        for t in range(TT):
            sp.wait_ge(o_done, t + 1)
            sp.dma_start(out[0, t * 128:(t + 1) * 128, :], Og[:, t, :]).then_inc(out_s, 16)
        sp.wait_ge(out_s, 16 * TT)

    @blk.gpsimd
    def _(pool):
        st = Count(pool, pool_s)
        g = nc.gpsimd
        st.link(g.memset(ident[:, :], 0.0))
        g.affine_select(out=ident[:, :], in_=ident[:, :], compare_op=ALU.not_equal, fill=1.0, base=0,
                        pattern=[[-1, 128]], channel_multiplier=1).then_inc(id_done, 1)
        pool.wait_ge(pw_tab, 6)
        pool.wait_ge(h_done, KD)

        def phases_of(b):
            pool.wait_ge(x_done, b) if not (isinstance(b, int) and b == 0) else None
            re, im = (PH[:, ri].rearrange("p d l q -> p (d l) q") for ri in range(2))
            n, lev = 1, 0
            while n < NQ:
                m = min(n, NQ - n)
                pr, pi = (w[:, lev, sl(b, 8)].unsqueeze(2).to_broadcast([128, 8, m]) for w in (PWr, PWi))
                g.tensor_tensor(re[:, :, n:n + m], re[:, :, 0:m], pr, ALU.mult)
                g.tensor_tensor(im[:, :, n:n + m], re[:, :, 0:m], pi, ALU.mult)
                ta = gph[:, 0, :, 0:m]
                tb = gph[:, 1, :, 0:m]
                g.tensor_tensor(ta, im[:, :, 0:m], pi, ALU.mult)
                st.link(g.tensor_tensor(tb, im[:, :, 0:m], pr, ALU.mult))
                g.tensor_tensor(re[:, :, n:n + m], re[:, :, n:n + m], ta, ALU.subtract)
                last = g.tensor_tensor(im[:, :, n:n + m], im[:, :, n:n + m], tb, ALU.add)
                n, lev = n + m, lev + 1
                if n < NQ:
                    st.link(last)
            last.then_inc(ph_done, 1)
        g.memset(PH[:, 0, :, :, 0:1].rearrange("p d l q -> p (d l) q"), 1.0)
        st.link(g.memset(PH[:, 1, :, :, 0:1].rearrange("p d l q -> p (d l) q"), 0.0))
        repeat(pool, NB, phases_of, [(st, 13)])

        for t in (5, 7):
            freed(pool, 2, 3, t)
        def load(k):
            pool.dma_start(gwt[k % 2][:, :], w_ada[k * 128:(k + 1) * 128, 2 * D:3 * D]).then_inc(gw_in[k % 2], 16)
        load(0)
        load(1)
        for k in range(KD):
            pool.wait_ge(gw_in[k % 2], 16 * (k // 2 + 1))
            if k == 0:
                st.link(g.tensor_scalar(gacc[:, :], gwt[0][:, :], cs[:, 0, 0:1], 0.0, ALU.mult, ALU.add))
            else:
                st.link(g.tensor_scalar(gprod[:, :], gwt[k % 2][:, :], cs[:, k, 0:1], 0.0, ALU.mult, ALU.add))
            if k + 2 < KD:
                load(k + 2)
            if k:
                st.link(g.tensor_tensor(gacc[:, :], gacc[:, :], gprod[:, :], ALU.add))
        g.memset(ones[:, :], 1.0).then_inc(gacc_done, 1)

    @blk.tensor
    def _(pe):
        mm, tr = nc.tensor.matmul, nc.tensor.transpose
        pe.wait_ge(id_done, 1)
        pe.wait_ge(vec_in, 96)
        tr(ss[:, 0, 0:V_END], vrow[:, :], ident[0:V_END, 0:V_END]).then_inc(vec_ps, 1)
        pe.wait_ge(cs_done, 1)

        def ada_half(h):
            for q in range(4 * h, 4 * h + 4):
                if q >= 4:
                    pe.wait_ge(row_cp, q - 3)
                for k in range(4):
                    n = 4 * q + k
                    pe.wait_ge(ada_in[n % 4], 16 * (n // 4 + 1))
                    for j in range(4):
                        last = mm(ac[0:2, q % 4, :], cs[:, 4 * k + j, :], ring[:, n % 4, j, :],
                                  start=(k == 0 and j == 0), stop=(k == 3 and j == 3))
                    last.then_inc(ada_used, 1)

        def cols_half(h):
            pe.wait_ge(row_cp, 4 * h + 4)
            for k in range(KD):
                n = h * KD + k
                last = tr(ss[:, 0, 2 * n:2 * n + 2], rows[:, n * 128:(n + 1) * 128], ident[0:2, 0:2])
            last.then_inc(col_ps, 1)

        ada_half(0)
        pe.wait_ge(zn_done, 1)
        for n in range(7):
            last = tr(ss[:, n // 4, (n % 4) * 128:(n % 4 + 1) * 128],
                      ZN[:, n].rearrange("q a p -> q (a p)"), ident[:, :])
        last.then_inc(p0_ps, 1)
        pe.wait_ge(b_in, 64)
        pe.wait_ge(p0_cp, 1)
        for h in range(H):
            last = tr(ss[:, h // 4, (h % 4) * 128:(h % 4 + 1) * 128],
                      braw[:, :, :].rearrange("q r (p h) -> q (r p) h", h=H)[:, :, h], ident[:, :])
        last.then_inc(p0_ps, 1)
        pe.wait_ge(p0_cp, 2)
        for h in range(H):
            last = tr(ss[:, h // 4, (h % 4) * 128:(h % 4 + 1) * 128],
                      craw[:, h].rearrange("q r p -> q (r p)"), ident[:, :])
        last.then_inc(p0_ps, 1)
        ada_half(1)
        pe.wait_ge(p0_cp, 3)
        cols_half(0)
        cols_half(1)
        pe.wait_ge(col_cp, 1)
        pe.wait_ge(y_done, 6)
        for k in range(KD):
            b = 2 * (k % 2)
            if k >= 2:
                pe.wait_ge(h_done, k - 1)
            for t in range(TT):
                tr(ss[:, b, t * 128:(t + 1) * 128], xn[:, t, k * 128:(k + 1) * 128], ident[:, :])
            for t in range(CT):
                last = tr(ss[:, b + 1, t * 128:(t + 1) * 128], cn[:, t, k * 128:(k + 1) * 128], ident[:, :])
            last.then_inc(h_ps, 1)

        def product(k, i, j, nu, a, rhs, wait_free=True):
            per, accs = len(stream[k][1](0)), (4, 4, 8, 12, 8, 4, 8, 8)[k]
            bank = a % 4
            n = i * accs + (A0[k] + a)
            if A0[k] + a >= 4 or not isinstance(n, int) or n >= 4:
                pe.wait_ge(ac_free[bank], (n - bank) // 4 if isinstance(n, int)
                           else i * (accs // 4) + (A0[k] + a - bank) // 4)
            for v in range(nu):
                u = i * per + (U0[k] + j + v)
                s = (U0[k] + j + v) % NSLOT
                pe.wait_ge(w_in_s[s], i * (per * 16 // NSLOT) + ((U0[k] + j + v) // NSLOT + 1) * 16)
                for q in range(UNIT):
                    last = mm(ac[:, bank, :], wslot[:, s, q * 128:(q + 1) * 128], rhs(v * UNIT + q),
                              start=(v == 0 and q == 0), stop=(v == nu - 1 and q == UNIT - 1))
                last.then_inc(w_used, 1)

        pe.wait_ge(h_done, KD)
        x_of = lambda q: hx[:, q, :]

        def u_turn(i):
            for j in range(2):
                for a in (2 * j, 2 * j + 1):
                    n = i * 4 + a
                    if a >= 4 or not isinstance(n, int) or n >= 4:
                        pe.wait_ge(ac_free[a], i)
                for v in range(2):
                    s = 2 * j + v
                    pe.wait_ge(w_in_s[s], i * 16 + 16)
                    for q in range(UNIT):
                        f = dict(start=(v == 0 and q == 0), stop=(v == 1 and q == UNIT - 1))
                        w = wslot[:, s, q * 128:(q + 1) * 128]
                        lx = mm(ac[:, 2 * j, :], w, hx[:, v * UNIT + q, :], **f)
                        last = mm(ac[:, 2 * j + 1, 0:TC], w, hc[:, v * UNIT + q, :], **f)
                    last.then_inc(w_used, 1)
        repeat(pe, KW // 2, u_turn)

        def conv_turn(b):
            pe.wait_ge(u_cur, b + 1)
            if not (isinstance(b, int) and b == 0):
                pe.wait_ge(y_pre, b)
            for j in range(L):
                last = tr(ss[0:NQ, j // 4, (j % 4) * 128:(j % 4 + 1) * 128], ucur[:, j::L], ident[:, :])
            last.then_inc(ut_ps, 1)
            product(1, b, 0, 2, 0, x_of)
            pe.wait_ge(ut_cp, b + 1)
            for g in range(GB):
                last = tr(ss[:, 2 + g // 4, (g % 4) * NQ:(g % 4 + 1) * NQ],
                          ut[:, g].rearrange("c j h -> c (j h)"), ident[0:NQ, 0:NQ])
            last.then_inc(u_ps, 1)
            pe.wait_ge(v_done, b + 1)
            pe.wait_ge(u_cp, b + 1)
            for d in range(2):
                for g in range(GB):
                    last = tr(ss[:, 2 * d + g // 4, (g % 4) * 128:(g % 4 + 1) * 128], V[:, d, g, :], ident[:, :])
                last.then_inc(vt_ps, 1)
            product(1, b, 2, 2, 1, x_of)
            for d in range(2):
                pe.wait_ge(vt_cp, 2 * b + 1 + d)
                for g in range(GB):
                    last = mm(ss[:, 2 * d + g // 4, (g % 4) * NQ:(g % 4 + 1) * NQ], VT[:, d, g, :], U[:, g, :],
                              start=True, stop=True)
                last.then_inc(s_ps, 1)
            product(1, b, 4, 2, 2, x_of)
            pe.wait_ge(s_cp, 2 * b + 2)
            pe.wait_ge(cp_done, b + 1)
            for d in range(2):
                for g in range(GB):
                    at0 = (L - 1) * H if d == 0 else 0
                    cp0 = 0 if d == 0 else H
                    last = mm(ss[0:H, 2 * d + g // 4, (g % 4) * 128:(g % 4 + 1) * 128],
                              V[:, d, g, at0:at0 + H], Cp[:, d, g, cp0:cp0 + L * H], start=True, stop=True)
            last.then_inc(k_ps, 1)
            product(1, b, 6, 2, 3, x_of)
            pe.wait_ge(t_add, b + 1)
            pe.wait_ge(x_done, b + 1)
            pe.wait_ge(m_in, b * 128 + 128)
            for g in range(GB):
                o = ss[0:NX, g // 4, (g % 4) * 128:(g % 4 + 1) * 128]
                mm(o, U[:, g, NC:NQ], M[:, g, :], start=True, stop=False)
                mm(o, X[:, 0, g // 2, g % 2, :], Cp[:, 0, g, H:(L + 1) * H], start=False, stop=False)
                last = mm(o, X[:, 1, g // 2, g % 2, :], Cp[:, 1, g, 0:L * H], start=False, stop=True)
            last.then_inc(y_ps, 1)
            pe.wait_ge(yt_cp, 1)
            pe.wait_ge(yt_cp, b + 1)
            for i in range(L):
                last = tr(ss[:, 2, i * NX:(i + 1) * NX], yt[:, i, :], ident[0:NX, 0:NX])
            last.then_inc(yT_ps, 1)
        repeat(pe, NB, conv_turn)

        def merge(k, branch, ready):
            def body(i):
                for j in range(4):
                    product(k, i, 3 * j, 2, 2 * j, x_of)
                    if j == 0 and isinstance(i, int) and i == 0 or (j == 0 and not isinstance(i, int)):
                        pe.wait_ge(*ready)
                    product(k, i, 3 * j + 2, 1, 2 * j + 1, lambda q: branch[:, q * T:(q + 1) * T])
            repeat(pe, KD // 4, body)
        merge(2, Abr, (a_done, NB))

        def glu_turn(i):
            for j in range(4):
                product(3, i, 4 * j, 2, 3 * j, x_of)
                if j == 0:
                    pe.wait_ge(ge_done, 8)
                for w in range(2):
                    product(3, i, 4 * j + 2 + w, 1, 3 * j + 1 + w, lambda q: b2nd[:, q * T:(q + 1) * T])
        repeat(pe, KW // 4, glu_turn)
        merge(4, bact, (gl_done, KW))

        def f_turn(i):
            for j in range(4):
                product(5, i, 2 * j, 2, j, x_of)
        repeat(pe, KW // 4, f_turn)
        for a in range(4):
            freed(pe, 5, 1, a)
        pe.wait_ge(dft_in, 32)
        for gr in range(FG):
            for t in range(TT):
                if gr:
                    pe.wait_ge(p_cp, 4 * (gr - 1) + t + 1)
                for q in range(2):
                    kk = 2 * gr + q
                    last = mm(ss[:, t, :], bact[:, kk * T + t * 128:kk * T + (t + 1) * 128], dftw[:, q, :],
                              start=(q == 0), stop=(q == 1))
                last.then_inc(p_ps, 1)
            pe.wait_ge(p_cp, 4 * gr + 4)
            for wt in range(2):
                n = 2 * gr + wt
                pe.wait_ge(ac_free[n % 2], A0[6] // 4 + n // 2)
                for t in range(TT):
                    for a in range(2):
                        last = mm(ac[:, n % 2, :], pp[:, t, a * 256 + wt * 128:a * 256 + (wt + 1) * 128],
                                  dftt[:, a, t, :], start=(t == 0 and a == 0), stop=(t == 3 and a == 1))
                last.then_inc(pw_done, 1)

        def fw_turn(i):
            for j in range(4):
                prod6(i, 3 * j, 2, 2 * j, x_of)
                if j == 0:
                    pe.wait_ge(ac_free[0], A0[6] // 4 + MIX)
                    pe.wait_ge(ac_free[1], A0[6] // 4 + MIX)
                prod6(i, 3 * j + 2, 1, 2 * j + 1, lambda q: b2nd[:, q * T:(q + 1) * T])
        DF = MIX

        def prod(k, i, j, nu, a, rhs):
            per, accs = len(stream[k][1](0)), 8
            bank = a % 4
            pe.wait_ge(ac_free[bank], i * 2 + (A0[k] + a - bank) // 4 + (DF if bank < 2 else 0))
            for v in range(nu):
                s = (U0[k] + j + v) % NSLOT
                pe.wait_ge(w_in_s[s], i * (per * 16 // NSLOT) + ((U0[k] + j + v) // NSLOT + 1) * 16)
                for q in range(UNIT):
                    last = mm(ac[:, bank, :], wslot[:, s, q * 128:(q + 1) * 128], rhs(v * UNIT + q),
                              start=(v == 0 and q == 0), stop=(v == nu - 1 and q == UNIT - 1))
                last.then_inc(w_used, 1)
        prod6 = lambda *a: prod(6, *a)
        repeat(pe, KW // 4, fw_turn)

        def c_turn(i):
            for j in range(4):
                prod(7, i, 3 * j, 2, 2 * j, x_of)
                if j == 0:
                    for t in (5, 7):
                        freed(pe, 6, 1, t)
                prod(7, i, 3 * j + 2, 1, 2 * j + 1, lambda q: bact[:, q * T:(q + 1) * T])
        repeat(pe, KD // 4, c_turn)
        pe.wait_ge(gacc_done, 1)
        pe.wait_ge(gp_in, 32)
        for q in range(4):
            mm(ss[:, q, :], ones[:, :], gacc[:, q * 512:(q + 1) * 512], start=True, stop=False)
            last = mm(ss[:, q, :], ones[0:1, :], baro[0:1, q * 512:(q + 1) * 512], start=False, stop=True)
        last.then_inc(gb_ps, 1)
        pe.wait_ge(gg_done, 1)
        for q in range(4):
            last = mm(ss[:, q, :], ones[0:1, :], grow[0:1, q * 512:(q + 1) * 512], start=True, stop=True)
        last.then_inc(gpr_ps, 1)
        pe.wait_ge(m_done, 32)
        for cb in range(4):
            for t in range(TT):
                pe.wait_ge(ac_free[t], A0[8] // 4 + cb + (DF if t < 2 else 0))
            for j in range(8):
                u = U0[-1] + cb * 8 + j
                pe.wait_ge(w_in_s[u % NSLOT], (u // NSLOT + 1) * 16)
                for t in range(TT):
                    for q in range(2):
                        kk = 2 * j + q
                        last = mm(ac[:, t, :], mT[:, kk * T + t * 128:kk * T + (t + 1) * 128],
                                  wslot[:, u % NSLOT, q * 512:(q + 1) * 512],
                                  start=(kk == 0), stop=(kk == KD - 1))
                    if j == 7 and t < 3:
                        last.then_inc(ac_done, 1)
                last.then_inc(w_used, 1)

    @blk.scalar
    def _(act):
        st = Count(act, act_s)
        a = nc.scalar.activation
        cp = lambda o, i, scale=1.0: nc.scalar.activation(o, i, ACT.Copy, scale=scale)
        act.wait_ge(vec_cp, 1)
        a(small[:, 0:32], vecs[:, V_C:V_END], ACT.Sigmoid).then_inc(sg_done, 1)
        act.wait_ge(x_in, 96)
        junk = hc[:, 0:8, :].rearrange("p a b -> p (a b)")
        toks = [xn[:, t, :] for t in range(TT)] + [cn[:, t, :] for t in range(CT)]
        for t, tok in enumerate(toks):
            st.link(a(junk, tok, ACT.Square, accum_out=small[:, 32 + t:33 + t]))
        act.wait_ge(var_done, 1)
        a(small[:, 46:52], small[:, 40:46], ACT.Sqrt).then_inc(rt_done, 1)
        act.wait_ge(rs_done, 1)
        for t, tok in enumerate(toks):
            cp(tok, tok, small[:, 52 + t:53 + t]).then_inc(y_done, 1)

        def rows_half(h):
            for q in range(4 * h, 4 * h + 4):
                act.wait_ge(ada_used, 4 * q + 4)
                cp(rows[:, q * 512:(q + 1) * 512], ac[0:2, q % 4, :]).then_inc(row_cp, 1)
        rows_half(0)
        act.wait_ge(p0_ps, 2)
        for h in range(H):
            last = cp(Braw[:, :, h].rearrange("p (b d g) -> p d b g", b=NB, d=2),
                      ss[:, h // 4, (h % 4) * 128:(h % 4 + 1) * 128].rearrange("p (d b g) -> p d b g", b=NB, d=2))
        last.then_inc(p0_cp, 1)
        act.wait_ge(p0_cp, 2)
        cp(Brw2[0:64, :, :], Braw[64:128, :, :], -1.0)
        cp(Brw2[64:128, :, :], Braw[0:64, :, :]).then_inc(brw_done, 1)
        act.wait_ge(p0_ps, 3)
        for h in range(H):
            for ri in range(2):
                pr = slice(64 * ri, 64 * ri + 64)
                last = cp(C1[pr, :, h].rearrange("p (b d g) -> p d b g", b=NB, d=2),
                          ss[pr, h // 4, (h % 4) * 128:(h % 4 + 1) * 128]
                          .rearrange("p (d b g) -> p d b g", b=NB, d=2), 1.0 - 2.0 * ri)
        last.then_inc(p0_cp, 1)
        rows_half(1)

        def u_turn(i):
            for j in range(2):
                act.wait_ge(w_used, i * 4 + (2 * j + 2))
                o = i * (2 * (TC + T)) + j * (TC + T)
                cp(uT[:, bass.ds(o, TC)], ac[:, 2 * j + 1, 0:TC]).then_inc(ac_free[2 * j + 1], 1)
                cp(uT[:, bass.ds(o + TC, T)], ac[:, 2 * j, :]).then_inc(ac_free[2 * j], 1)
        repeat(act, KW // 2, u_turn)
        act.wait_ge(p0_cp, 3)
        act.wait_ge(bb_done, 1)
        for j in range(4):
            act.wait_ge(ac_free[j], 4)

        def conv_turn(b):
            first = isinstance(b, int) and b == 0
            if not first:
                act.wait_ge(ut_ps, b)
                act.wait_ge(v_done, b)
                act.wait_ge(cp_done, b)
            cp(ucur[:, :], uT[:, sl(b, TC + T)]).then_inc(u_cur, 1)
            for T2, T1, sign in ((B2, B1, -1.0), (C2, C1, 1.0)):
                s1, s2 = T1[64:128, sl(b, 16), :], T1[0:64, sl(b, 16), :]
                cp(T2[0:64].rearrange("p d g h -> p (d g) h"), s1, sign)
                last = cp(T2[64:128].rearrange("p d g h -> p (d g) h"), s2, 1.0 if sign < 0 else -1.0)
            last.then_inc(bc2, 1)
            act.wait_ge(ut_ps, b + 1)
            for q in range(2):
                last = cp(ut[:, :, 4 * q:4 * q + 4, :].rearrange("c g j h -> c j g h"),
                          ss[0:NQ, q, :].rearrange("c (j g h) -> c j g h", j=4, g=GB))
            last.then_inc(ut_cp, 1)
            act.wait_ge(w_used, b * 8 + (U0[1] + 2))
            cp(xas[:, :], ac[:, 0, :]).then_inc(ac_free[0], 1)
            act.wait_ge(u_ps, b + 1)
            for q in range(2):
                last = cp(U[:, 4 * q:4 * q + 4, :], ss[:, 2 + q, 0:4 * NQ].rearrange("p (g c) -> p g c", g=4))
            last.then_inc(u_cp, 1)
            if not first:
                act.wait_ge(x_done, b)
            for d in range(2):
                act.wait_ge(vt_ps, 2 * b + (d + 1))
                for q in range(2):
                    last = cp(VT[:, d, 4 * q:4 * q + 4, :], ss[:, 2 * d + q, :].rearrange("p (g c) -> p g c", g=4))
                last.then_inc(vt_cp, 1)
            for d in range(2):
                act.wait_ge(s_ps, 2 * b + (d + 1))
                for q in range(2):
                    for ri in range(2):
                        for s in range(2):
                            src = ss[64 * ri:64 * ri + 64, 2 * d + q, 0:4 * NQ].rearrange(
                                "p (l s c) -> p l s c", l=2, s=2)[:, :, s, :]
                            dst = S[64 * s:64 * s + 64, ri, d, 2 * q:2 * q + 2, :]
                            if d == 0:
                                last = cp(dst, src)
                            else:
                                cp(dst[:, :, 0:NC], src[:, :, NC - 1::-1])
                                last = cp(dst[:, :, NC:NQ], src[:, :, NQ - 1:NC - 1:-1])
                last.then_inc(s_cp, 1)
            act.wait_ge(k_ps, b + 1)
            if not first:
                act.wait_ge(m_in, b * 128)
            for q in range(2):
                back = ss[0:H, 2 + q, :].rearrange("p (g c) -> p g c", g=4)
                forth = ss[0:H, q, :].rearrange("p (g c) -> p g c", g=4)
                cp(Tl[:, 4 * q:4 * q + 4, 0:128], back)
                last = cp(Tl[:, 4 * q:4 * q + 4, 128:240], forth[:, :, H:128])
            last.then_inc(t_cp, 1)
            act.wait_ge(t_add, b + 1)
            if not first:
                act.wait_ge(y_ps, b)
            for j in range(L):
                act.dma_start(M[H * j:H * j + H, :, :], Tl[:, :, (L - 1 - j) * H:(L - 1 - j) * H + 128])\
                   .then_inc(m_in, 16)
            act.wait_ge(w_used, b * 8 + (U0[1] + 8))
            if not first:
                act.wait_ge(a_done, b)
            a(sg[:, :], ac[:, 3, :], ACT.Sigmoid).then_inc(sig_done, 1)
            act.wait_ge(y_ps, b + 1)
            for q in range(2):
                last = cp(yt[:, :, 64 * q:64 * q + 64].rearrange("c i (g h) -> c g i h", g=4),
                          ss[0:NX, q, :].rearrange("c (g i h) -> c g i h", g=4, i=L))
            last.then_inc(yt_cp, 1)
        repeat(act, NB, conv_turn)
        act.wait_ge(y_pre, NB)

        def tanhs():
            for b in range(NB):
                act.wait_ge(ge_in, b + 1)
                a(gtm1[:, :], gtm1[:, :], ACT.Tanh, scale=math.sqrt(2.0 / math.pi)).then_inc(ge_th, 1)
        tanhs()

        def merge(k):
            def body(i):
                for j in range(4):
                    act.wait_ge(w_used, i * 12 + (U0[k] + 3 * j + 2))
                    if j:
                        freed(act, k, i, 2 * j - 1)
                    elif not isinstance(i, int) or i:
                        freed(act, k, i - 1, 7)
                    a(gsig[:, :], ac[:, (2 * j) % 4, :], ACT.Sigmoid).then_inc(ac_free[(2 * j) % 4], 1)
            repeat(act, KD // 4, body, peel=1)
        merge(2)

        def glu_turn(i):
            for j in range(4):
                act.wait_ge(w_used, i * 16 + (U0[3] + 4 * j + 2))
                if j or not isinstance(i, int) or i:
                    act.wait_ge(gl_done, i * 4 + j)
                a(gsig[:, :], ac[:, (3 * j) % 4, :], ACT.Sigmoid).then_inc(gl_sig, 1)
                act.wait_ge(w_used, i * 16 + (U0[3] + 4 * j + 4))
                a(gtm1[:, :], ac[:, (3 * j + 2) % 4, :], ACT.Sigmoid).then_inc(ac_free[(3 * j + 2) % 4], 1)
        freed(act, 2, 3, 7)
        repeat(act, KW // 4, glu_turn)
        act.wait_ge(gl_done, 8)
        merge(4)

        def f_turn(i):
            for j in range(4):
                act.wait_ge(w_used, i * 8 + (U0[5] + 2 * j + 2))
                cp(bact[:, bass.ds(i * (4 * T) + j * T, T)], ac[:, j, :]).then_inc(ac_free[j], 1)
        repeat(act, KW // 4, f_turn)
        for gr in range(FG):
            for t in range(TT):
                act.wait_ge(p_ps, 4 * gr + t + 1)
                if gr:
                    act.wait_ge(pw_done, 2 * gr)
                cp(pp[:, t, :], ss[:, t, :]).then_inc(p_cp, 1)

        def fw_turn(i):
            for j in range(4):
                act.wait_ge(w_used, i * 12 + (U0[6] + 3 * j + 2))
                if j:
                    freed(act, 6, i, 2 * j - 2)
                elif not isinstance(i, int) or i:
                    freed(act, 6, i - 1, 6)
                a(gsig[:, :], ac[:, (2 * j) % 4, :], ACT.Sigmoid).then_inc(zc_sig, 1)
        freed(act, 4, 3, 7)
        repeat(act, KW // 4, fw_turn, peel=1)
        freed(act, 6, 1, 6)
        merge(7)
        act.wait_ge(gg_done, 2)
        for cb in range(4):
            for t in range(TT):
                if t < 3:
                    act.wait_ge(ac_done, 3 * cb + t + 1)
                else:
                    act.wait_ge(w_used, U0[-1] + 8 * cb + 8)
                if cb or t:
                    act.wait_ge(sq_done, 4 * cb + t)
                a(sqj[:, :], ac[:, t, :], ACT.Square, accum_out=ssq[:, 4 * t + cb:4 * t + cb + 1])\
                    .then_inc(sq_done, 1)
        act.wait_ge(var_done, 2)
        a(small[:, 46:50], small[:, 40:44], ACT.Sqrt).then_inc(rt_done, 1)

    @blk.vector
    def _(dve):
        st = Count(dve, dve_s)
        v = nc.vector
        tt, ts_, stt, cpy = v.tensor_tensor, v.tensor_scalar, v.scalar_tensor_tensor, v.tensor_copy
        link = st.link
        st.link(v.memset(small[:, :], 0.0))
        dve.wait_ge(vec_ps, 1)
        cpy(vecs[:, :], ss[:, 0, 0:V_END]).then_inc(vec_cp, 1)
        dve.wait_ge(vec_cp, 1)
        dve.wait_ge(sg_done, 1)
        tt(cs[:, :, :].rearrange("p k two -> p two k"), vecs[:, V_C:V_END].rearrange("p (two k) -> p two k", two=2),
           small[:, 0:32].rearrange("p (two k) -> p two k", two=2), ALU.mult).then_inc(cs_done, 1)

        MAGIC = 1.5 * 2.0 ** 23

        def nearest(o, i, scale):
            link(ts_(o, i, scale, MAGIC, ALU.mult, ALU.add))
            link(ts_(o, o, MAGIC, None, ALU.subtract))

        def exp(o, i, n, rr, p, q, e):
            link(ts_(q, i, 88.0, -87.0, ALU.min, ALU.max))
            nearest(n, q, 1.0 / math.log(2.0))
            link(stt(rr, n, -0.693145751953125, q, ALU.mult, ALU.add))
            link(stt(rr, n, -1.42860682030941723e-6, rr, ALU.mult, ALU.add))
            link(ts_(p, rr, 1.0 / 5040, 1.0 / 720, ALU.mult, ALU.add))
            for cc in (1.0 / 120, 1.0 / 24, 1.0 / 6, 0.5, 1.0, 1.0):
                link(tt(p, p, rr, ALU.mult))
                link(ts_(p, p, cc, None, ALU.add))
            link(ts_(e, n, 127.0, 8388608.0, ALU.add, ALU.mult))
            link(ts_(q, i, -87.0, None, ALU.is_ge))
            link(tt(p, p, q, ALU.mult))
            link(tt(o, p, e.bitcast(F32), ALU.mult))

        dve.wait_ge(ssm_in, 48)
        a0, a1, a2, a3, a4, a5, a6, a7 = [z[:, :] for z in zt]
        lre, lim = lam[:, 0, :], lam[:, 1, :]
        exp(a7[:, 0:1], ldt[:, :], a1[:, 0:1], a2[:, 0:1], a3[:, 0:1], a4[:, 0:1], ei[:, 0:1])
        link(ts_(a0, lre, a7[:, 0:1], None, ALU.mult))
        exp(a6, a0, a1, a2, a3, a4, ei[:, :])
        link(ts_(a0, lim, a7[:, 0:1], None, ALU.mult))
        nearest(a1, a0, 1.0 / math.pi)
        link(stt(a2, a1, -3.140625, a0, ALU.mult, ALU.add))
        link(stt(a2, a1, -9.67502593994140625e-4, a2, ALU.mult, ALU.add))
        link(stt(a2, a1, -1.509957990978376432e-7, a2, ALU.mult, ALU.add))
        nearest(a3, a1, 0.5)
        link(stt(a3, a3, -2.0, a1, ALU.mult, ALU.add))
        link(tt(a3, a3, a3, ALU.mult))
        link(ts_(a3, a3, -2.0, 1.0, ALU.mult, ALU.add))
        link(tt(a1, a2, a2, ALU.mult))
        fact = [1.0 / math.factorial(n) for n in range(16)]
        link(ts_(a4, a1, fact[13], -fact[11], ALU.mult, ALU.add))
        for cc in (fact[9], -fact[7], fact[5], -fact[3], 1.0):
            link(tt(a4, a4, a1, ALU.mult))
            link(ts_(a4, a4, cc, None, ALU.add))
        link(tt(a4, a4, a2, ALU.mult))
        link(tt(a4, a4, a3, ALU.mult))
        link(ts_(a5, a1, -fact[14], fact[12], ALU.mult, ALU.add))
        for cc in (-fact[10], fact[8], -fact[6], fact[4], -fact[2], 1.0):
            link(tt(a5, a5, a1, ALU.mult))
            link(ts_(a5, a5, cc, None, ALU.add))
        link(tt(a5, a5, a3, ALU.mult))
        z = lambda n: ZN[:, n, 0, :]
        link(tt(z(0), a6, a5, ALU.mult))
        link(tt(z(1), a6, a4, ALU.mult))
        link(ts_(a0, z(0), 1.0, None, ALU.subtract))
        link(tt(a1, lre, lre, ALU.mult))
        link(tt(a2, lim, lim, ALU.mult))
        link(tt(a1, a1, a2, ALU.add))
        link(v.reciprocal(a1, a1))
        link(tt(a2, a0, lre, ALU.mult))
        link(tt(a3, z(1), lim, ALU.mult))
        link(tt(a2, a2, a3, ALU.add))
        link(tt(z(2), a2, a1, ALU.mult))
        link(tt(a2, z(1), lre, ALU.mult))
        link(tt(a3, a0, lim, ALU.mult))
        link(tt(a2, a2, a3, ALU.subtract))
        link(tt(z(3), a2, a1, ALU.mult))

        def square(re, im, s, t):
            link(tt(s, re, re, ALU.mult))
            link(tt(t, im, im, ALU.mult))
            link(tt(im, re, im, ALU.mult))
            link(tt(re, s, t, ALU.subtract))
            link(ts_(im, im, 2.0, None, ALU.mult))
        for _ in range(3):
            square(a5, a4, a0, a1)
            link(tt(a6, a6, a6, ALU.mult))
        cpy(z(4), a5)
        cpy(z(5), a4)
        link(cpy(z(6), a6))
        cpy(ZN[:, :, 1, :], ZN[:, :, 0, :]).then_inc(zn_done, 1)
        dve.wait_ge(act_s, 6)
        ts_(small[:, 40:46], small[:, 32:38], 1.0 / D, EPS, ALU.mult, ALU.add).then_inc(var_done, 1)
        dve.wait_ge(var_done, 1)

        def rsqrt(n, rt):
            dve.wait_ge(rt_done, rt)
            s40, s46, s52 = small[:, 40:40 + n], small[:, 46:46 + n], small[:, 52:52 + n]
            link(v.reciprocal(s52, s46))
            link(tt(s46, s52, s52, ALU.mult))
            link(tt(s46, s46, s40, ALU.mult))
            link(ts_(s46, s46, -0.5, 1.5, ALU.mult, ALU.add))
            return tt(s52, s52, s46, ALU.mult)
        rsqrt(6, 1).then_inc(rs_done, 1)

        dve.wait_ge(p0_ps, 1)
        col = lambda n: ss[:, n // 4, (n % 4) * 128:(n % 4 + 1) * 128]
        dbg = lambda ap: ap.rearrange("p (d b g) -> p d b g", b=NB, d=2)
        bdg = lambda ap: ap.rearrange("p (b d g) -> p d b g", b=NB, d=2)
        cpy(bdg(Ar[:, 1, :]), dbg(col(0)))
        cpy(bdg(Ai[:, 1, :]), dbg(col(1)))
        cpy(bdg(q2[:, 0, :]), dbg(col(2)))
        cpy(bdg(q2[:, 1, :]), dbg(col(3)))
        for n, dst in ((4, PWr[:, 0, :]), (5, PWi[:, 0, :]), (6, R8[:, :])):
            for s in range(2):
                pr = slice(64 * s, 64 * s + 64)
                last = cpy(dst[pr].rearrange("p (b d l) -> p d b l", b=NB, d=2),
                           col(n)[pr].rearrange("p (d b l s) -> p d b l s", b=NB, d=2, s=2)[:, :, :, :, s])
        last.then_inc(p0_cp, 1)
        dve.wait_ge(p0_cp, 1)
        v.memset(Ar[:, 0, :], 1.0)
        link(v.memset(Ai[:, 0, :], 0.0))
        for n0, m in ((1, 1), (2, 2), (4, 4)):
            mr, mi = (A[:, n0:n0 + 1, :].to_broadcast([128, m, 128]) for A in (Ar, Ai))
            sr, si = Ar[:, 1:1 + m, :], Ai[:, 1:1 + m, :]
            dr, di = Ar[:, n0 + 1:n0 + 1 + m, :], Ai[:, n0 + 1:n0 + 1 + m, :]
            ta = tq[:, 0:8 * m, :].rearrange("p (m a) h -> p m (a h)", m=m)
            tb = tq[:, 32:32 + 8 * m, :].rearrange("p (m a) h -> p m (a h)", m=m)
            tt(dr, sr, mr, ALU.mult)
            tt(di, sr, mi, ALU.mult)
            tt(ta, si, mi, ALU.mult)
            link(tt(tb, si, mr, ALU.mult))
            tt(dr, dr, ta, ALU.subtract)
            link(tt(di, di, tb, ALU.add))
        for n in range(6):
            re, im = PWr[:, n, :], PWi[:, n, :]
            tt(PWr[:, n + 1, :], re, re, ALU.mult)
            tt(a0, im, im, ALU.mult)
            link(tt(a1, re, im, ALU.mult))
            tt(PWr[:, n + 1, :], PWr[:, n + 1, :], a0, ALU.subtract)
            ts_(PWi[:, n + 1, :], a1, 2.0, None, ALU.mult).then_inc(pw_tab, 1)
            dve.wait_ge(pw_tab, n + 1)
        dve.wait_ge(brw_done, 1)
        qb = lambda n: q2[:, n, :].unsqueeze(2).to_broadcast([128, 128, H])
        tt(tq[:, :, :], Brw2[:, :, :], qb(1), ALU.mult)
        link(tt(B1[:, :, :], Braw[:, :, :], qb(0), ALU.mult))
        tt(B1[:, :, :], B1[:, :, :], tq[:, :, :], ALU.add).then_inc(bb_done, 1)
        dve.wait_ge(col_ps, 2)
        mod = vmod
        for h, vb in ((0, 16), (1, 0)):
            last = tt(mod[:, h], ss[:, 0, 32 * h:32 * h + 32].rearrange("p (k two) -> p k two", two=2),
                      vecs[:, V_BADA + vb:V_BADA + vb + 16].unsqueeze(2).to_broadcast([128, KD, 2]), ALU.add)
        link(last)
        stt(mod[:, 0], mod[:, 0], 1.0, vecs[:, V_GPRE:V_GPRE + 16].unsqueeze(2).to_broadcast([128, KD, 2]),
            ALU.add, ALU.mult).then_inc(col_cp, 1)
        dve.wait_ge(col_cp, 1)
        for k in range(KD):
            dve.wait_ge(h_ps, k + 1)
            b = 2 * (k % 2)
            ts_(hx[:, k, :], ss[:, b, :], mod[:, 0, k, 0:1], mod[:, 1, k, 0:1], ALU.mult, ALU.add)
            ts_(hc[:, k, :], ss[:, b + 1, 0:TC], mod[:, 0, k, 1:2], mod[:, 1, k, 1:2], ALU.mult, ALU.add)\
                .then_inc(h_done, 1)

        def powers(dst, A, e0, n, rev, b, d, T1, T2, tmp):
            shape = [128, GB, n, H]
            cols = bass.ds(b * 16 + d * 8, 8)
            es = slice(e0, e0 + n)
            br, bi = (A_[:, es, cols].rearrange("p e g -> p g e").unsqueeze(3).to_broadcast(shape) for A_ in A)
            o = dst.rearrange("p g (m h) -> p g m h", h=H)
            if rev:
                o, tmp = o[:, :, ::-1, :], tmp[:, :, ::-1, :]
            w1, w2 = (q.unsqueeze(2).to_broadcast(shape) for q in (T1, T2))
            tt(o, br, w1, ALU.mult)
            return tt(tmp, bi, w2, ALU.mult), o

        def conv_turn(b):
            dyn = not isinstance(b, int)
            dve.wait_ge(bc2, b + 1)
            if dyn or b:
                dve.wait_ge(k_ps, b)
                dve.wait_ge(y_ps, b)
            for d in range(2):
                tmp = t1[:, d * 1152:d * 1152 + 1024].rearrange("p (g m h) -> p g m h", g=GB, m=L)
                last, o = powers(V[:, d], (Ar, Ai), 0, L, d == 0, b, d, B1[:, bass.ds(b * 16 + d * 8, 8), :],
                                 B2[:, d], tmp)
            link(last)
            for d in range(2):
                tmp = t1[:, d * 1152:d * 1152 + 1024]
                o = V[:, d].rearrange("p g m -> p (g m)")
                last = tt(o, o, tmp, ALU.add)
            last.then_inc(v_done, 1)
            dve.wait_ge(v_done, b + 1)
            for d in range(2):
                tmp = t1[:, d * 1152:d * 1152 + 1152].rearrange("p (g m h) -> p g m h", g=GB, m=L + 1)
                last, o = powers(Cp[:, d], (Ar, Ai), 0, L + 1, d == 1, b, d,
                                 C1[:, bass.ds(b * 16 + d * 8, 8), :], C2[:, d], tmp)
            link(last)
            for d in range(2):
                o = Cp[:, d].rearrange("p g m -> p (g m)")
                last = tt(o, o, t1[:, d * 1152:(d + 1) * 1152], ALU.add)
            last.then_inc(cp_done, 1)
            dve.wait_ge(cp_done, b + 1)
            dve.wait_ge(w_used, b * 8 + (U0[1] + 4))
            freed(dve, 1, b, 0)
            tt(cv[:, :], ac[:, 1, :], xas[:, :], ALU.mult).then_inc(ac_free[1], 1)
            freed(dve, 1, b, 1)
            cw = lambda k: vcv[:, bass.ds(b * 3 + k, 1)]
            rows_of = lambda q: q[:, :].rearrange("p (r c) -> p r c", c=GRID)
            link(ts_(cy[:, :], cv[:, :], cw(1), None, ALU.mult))
            y3, c3 = rows_of(cy), rows_of(cv)
            link(stt(y3[:, :, 1:], c3[:, :, :GRID - 1], cw(0), y3[:, :, 1:], ALU.mult, ALU.add))
            link(stt(y3[:, :, :GRID - 1], c3[:, :, 1:], cw(2), y3[:, :, :GRID - 1], ALU.mult, ALU.add))
            dve.wait_ge(s_cp, 2 * b + 2)
            dve.wait_ge(ph_done, b + 1)
            f = lambda q: q.rearrange("p d l c -> p (d l c)")
            sr, si, pr, pi, zr, zi = (f(q[:, ri]) for q in (S, PH, Z) for ri in range(2))
            n = 2 * PB * NQ
            tt(zr, pr, sr, ALU.mult)
            tt(zi, pr, si, ALU.mult)
            tt(t1[:, 0:n], pi, si, ALU.mult)
            link(tt(t1[:, n:2 * n], pi, sr, ALU.mult))
            tt(zr, zr, t1[:, 0:n], ALU.add)
            link(tt(zi, zi, t1[:, n:2 * n], ALU.subtract))
            for ri in range(2):
                for d in range(2):
                    for l in range(PB):
                        q = Z[:, ri, d, l, :]
                        rr = R8[:, bass.ds(b * 8 + d * 4 + l, 1)]
                        last = v.tensor_tensor_scan(S[:, ri, d, l, :], rr.to_broadcast([128, NQ]), q, 0.0,
                                                    ALU.mult, ALU.add)
            link(last)
            w = slice(NC - 1, NQ - 1)
            ta, tb = (t1[:, n * i:n * i + 512].rearrange("p (d l c) -> p d l c", d=2, l=PB) for i in range(2))
            g3 = lambda q: q.rearrange("p d l c -> p (d l) c")
            P_, S_ = (lambda ri: g3(PH[:, ri])[:, :, w]), (lambda ri: g3(S[:, ri])[:, :, w])
            xs = []
            for ri in range(2):
                oa, ob = (t1[:, (2 * ri + k) * 512:(2 * ri + k + 1) * 512] for k in range(2))
                oa3, ob3 = (q.rearrange("p (m c) -> p m c", c=NX) for q in (oa, ob))
                tt(oa3, P_(0), S_(ri), ALU.mult)
                last = tt(ob3, P_(1), S_(1 - ri), ALU.mult)
            link(last)
            for ri in range(2):
                op = ALU.subtract if ri == 0 else ALU.add
                for s in range(2):
                    for d in range(2):
                        oa, ob = (t1[64 * s:64 * s + 64, (2 * ri + k) * 512 + d * 256:(2 * ri + k) * 512 + d * 256 + 256]
                                  .rearrange("p (l c) -> p l c", l=PB) for k in range(2))
                        dst = X[64 * ri:64 * ri + 64, d, :, s, :]
                        last = tt(dst if d == 0 else dst[:, :, ::-1], oa, ob, op)
            last.then_inc(x_done, 1)
            dve.wait_ge(t_cp, b + 1)
            for q in range(2):
                o = Tl[:, 4 * q:4 * q + 4, 112:128]
                last = tt(o, o, ss[0:H, q, :].rearrange("p (g c) -> p g c", g=4)[:, :, 0:H], ALU.add)
            last.then_inc(t_add, 1)
            dve.wait_ge(w_used, b * 8 + (U0[1] + 8))
            dve.wait_ge(sig_done, b + 1)
            tt(cy[:, :], cy[:, :], ac[:, 2, :], ALU.mult).then_inc(ac_free[2], 1)
            tt(sg[:, :], sg[:, :], ac[:, 3, :], ALU.mult).then_inc(ac_free[3], 1)
            freed(dve, 1, b, 2)
            freed(dve, 1, b, 3)
            tt(Abr[:, sl(b, T)], cy[:, :], sg[:, :], ALU.mult).then_inc(a_done, 1)
            dve.wait_ge(yT_ps, b + 1)
            uo = uT[:, bass.ds(b * (TC + T) + TC, T)].rearrange("p (c i) -> p c i", i=L)
            stt(uo, uo, vecs[:, bass.ds(b + V_SSMD, 1)], ss[:, 2, :].rearrange("p (i c) -> p c i", i=L),
                ALU.mult, ALU.add).then_inc(y_pre, 1)
        st.add(cpy(vcv[:, :].rearrange("p (b k) -> p k b", k=3),
                   vecs[:, V_CONV:V_CONV + 24].rearrange("p (k b) -> p k b", k=3)))
        st.wait()
        repeat(dve, NB, conv_turn, [(st, CONV_STEPS)])
        dve.wait_ge(a_done, NB)
        dve.wait_ge(y_pre, NB)
        for b in range(NB):
            y = uT[:, b * (TC + T) + TC:(b + 1) * (TC + T)]
            link(tt(gtm1[:, :], y, y, ALU.mult))
            link(ts_(gtm1[:, :], gtm1[:, :], 0.044715, 1.0, ALU.mult, ALU.add))
            tt(gtm1[:, :], gtm1[:, :], y, ALU.mult).then_inc(ge_in, 1)
            o = b2nd[:, b * T:(b + 1) * T]
            dve.wait_ge(ge_th, b + 1)
            link(stt(o, gtm1[:, :], 1.0, y, ALU.add, ALU.mult))
            ts_(o, o, 0.5, None, ALU.mult).then_inc(ge_done, 1)

        def merge(k, br):
            def body(i):
                for j in range(4):
                    o = mT[:, bass.ds(i * (4 * T) + j * T, T)]
                    freed(dve, k, i, 2 * j)
                    dve.wait_ge(w_used, i * 12 + (U0[k] + 3 * j + 3))
                    free = ac_free[(2 * j + 1) % 4]
                    if br and (j or not isinstance(i, int) or i):
                        dve.wait_ge(m_done, i * 4 + (16 * (br - 1) + j))
                    tt(o if br == 0 else gtm2[:, :], ac[:, (2 * j + 1) % 4, :], gsig[:, :], ALU.mult)\
                        .then_inc(free, 1)
                    if br:
                        freed(dve, k, i, 2 * j + 1)
                        tt(o, o, gtm2[:, :], ALU.add).then_inc(m_done, 1)
            repeat(dve, KD // 4, body)
        merge(2, 0)
        freed(dve, 2, 3, 5)
        freed(dve, 2, 3, 7)

        def glu_turn(i):
            for j in range(4):
                za, wa, wb = ((3 * j + q) % 4 for q in range(3))
                dve.wait_ge(gl_sig, i * 4 + (j + 1))
                dve.wait_ge(w_used, i * 16 + (U0[3] + 4 * j + 4))
                tt(gtm2[:, :], ac[:, za, :], gsig[:, :], ALU.mult).then_inc(ac_free[za], 1)
                freed(dve, 3, i, 3 * j + 2)
                tt(gtm1[:, :], ac[:, wa, :], gtm1[:, :], ALU.mult).then_inc(ac_free[wa], 1)
                freed(dve, 3, i, 3 * j)
                freed(dve, 3, i, 3 * j + 1)
                tt(bact[:, bass.ds(i * (4 * T) + j * T, T)], gtm1[:, :], gtm2[:, :], ALU.mult).then_inc(gl_done, 1)
        repeat(dve, KW // 4, glu_turn)
        merge(4, 1)
        for n in range(2 * FG):
            dve.wait_ge(pw_done, n + 1)
            cpy(b2nd[:, n * T:(n + 1) * T], ac[:, n % 2, :]).then_inc(ac_free[n % 2], 1)

        def fw_turn(i):
            for j in range(4):
                zc, fw = (2 * j) % 4, (2 * j + 1) % 4
                dve.wait_ge(zc_sig, i * 4 + (j + 1))
                tt(gtm2[:, :], ac[:, zc, :], gsig[:, :], ALU.mult).then_inc(ac_free[zc], 1)
                freed(dve, 6, i, 2 * j)
                dve.wait_ge(w_used, i * 12 + (U0[6] + 3 * j + 3))
                tt(bact[:, bass.ds(i * (4 * T) + j * T, T)], ac[:, fw, :], gtm2[:, :], ALU.mult)\
                    .then_inc(ac_free[fw], 1)
                freed(dve, 6, i, 2 * j + 1)
        repeat(dve, KW // 4, fw_turn)
        merge(7, 2)
        flat = ss[:, :, :].rearrange("p q c -> p (q c)")
        dve.wait_ge(gb_ps, 1)
        cpy(GG[:, :], flat).then_inc(gg_done, 1)
        dve.wait_ge(gg_done, 1)
        dve.wait_ge(gpr_ps, 1)
        tt(GG[:, :], GG[:, :], flat, ALU.mult).then_inc(gg_done, 1)
        dve.wait_ge(gg_done, 2)
        for cb in range(4):
            for t in range(TT):
                dve.wait_ge(sq_done, 4 * cb + t + 1)
                w = slice(cb * 512, cb * 512 + 512)
                tt(Og[:, t, w], ac[:, t, :], GG[:, w], ALU.mult).then_inc(ac_free[t], 1)
        link(v.tensor_reduce(small[:, 40:44], ssq[:, :].rearrange("p (t c) -> p t c", t=TT),
                             mybir.AxisListType.X, ALU.add))
        ts_(small[:, 40:44], small[:, 40:44], 1.0 / D, EPS, ALU.mult, ALU.add).then_inc(var_done, 1)
        dve.wait_ge(var_done, 2)
        link(rsqrt(4, 2))
        for t in range(TT):
            dve.wait_ge(ac_free[t], A0[8] // 4 + 4 + (4 if t < 2 else 0))
        dve.wait_ge(xr_in, 64)
        for t in range(TT):
            stt(Og[:, t, :], Og[:, t, :], small[:, 52 + t:53 + t], xr[:, t, :], ALU.mult, ALU.add).then_inc(o_done, 1)

    block.__exit__(None, None, None)


CONV_STEPS = 9

NAMES = ['x', 'c', 'ctx', 'c_ctx', 'w_ada', 'b_ada', 'g_pre', 'g_post', 'w_in', 'conv_w', 'ssm_lam_re',
         'ssm_lam_im', 'ssm_log_dt', 'ssm_b_re', 'ssm_b_im', 'ssm_c_re', 'ssm_c_im', 'ssm_d', 'glu_wa', 'glu_wb',
         'fourier_w', 'proj_a', 'proj_b', 'proj_c', 'w_out']


def fourier_tables():
    k = np.arange(FGW)
    w = 2 * np.pi * (np.outer(k, k) % FGW) / FGW
    dft_w = np.concatenate([np.cos(w), np.sin(w)], 1) / np.sqrt(FGW)
    k = np.arange(T)
    w = 2 * np.pi * (np.outer(k, k) % T) / T
    dft_t = np.stack([np.cos(w), -np.sin(w)]) / np.sqrt(T)
    return dft_w.astype(np.float32), dft_t.astype(np.float32)


def kernel(**inputs):
    import concourse.bacc as bacc
    from concourse.bass_utils import run_bass_kernel_spmd

    nc = bacc.Bacc("TRN2", target_bir_lowering=False, num_devices=1)
    dft_w, dft_t = fourier_tables()
    arrays, args = {}, []
    for name in NAMES:
        arrays[name] = np.ascontiguousarray(inputs[name])
    arrays["dft_w"], arrays["dft_t"] = dft_w, dft_t
    for name, a in arrays.items():
        args.append(nc.dram_tensor(name, a.shape, mybir.dt.from_np(a.dtype), kind="ExternalInput").ap())
    args.append(nc.dram_tensor("out", (1, T, D), F32, kind="ExternalOutput").ap())
    program(nc, *args)
    r = run_bass_kernel_spmd(nc, [arrays], core_ids=[0])
    return r.results[0]["out"]
```

```python
import math

import numpy as np

import concourse.bass as bass
from concourse import mybir

F32 = mybir.dt.float32
F32R = mybir.dt.float32r
I32 = mybir.dt.int32
ALU = mybir.AluOpType
ACT = mybir.ActivationFunctionType

D = 2048
T = 512
TC = 256
GRID = 64
W = 1024
H, P, G = 16, 64, 64
FG, FGW = 4, 256
EPS = 1e-6
KD, KW = D // 128, W // 128
TT, CT = T // 128, TC // 128
L = 8
NC, NX = TC // L, T // L
NQ = NC + NX
GB = 128 // H
NB = G // GB
PB = GB // 2
COL = dict(xa=0, ba=W, ca=2 * W, za=3 * W, u=4 * W, zb=5 * W, f=6 * W, zc=7 * W, gl=8 * W)
NSLOT = 4
GC = 256
UNIT = 8

V_BADA, V_GPRE, V_CONV, V_SSMD, V_C, V_CC, V_END = 0, 32, 48, 72, 80, 96, 112


class Count:

    def __init__(self, eng, sem):
        self.eng, self.sem, self.n, self.added = eng, sem, 0, 0

    def add(self, ins):
        ins.then_inc(self.sem, 1)
        self.n = self.n + 1
        self.added += 1
        return self.n

    def wait(self, n=None):
        self.eng.wait_ge(self.sem, self.n if n is None else n)

    def link(self, ins):
        self.add(ins)
        self.wait()


def repeat(eng, n, body, counts=(), peel=0):
    starts = [c.n for c, _ in counts]
    if ROLLED:
        for i in range(peel):
            body(i)
        with eng.Fori(peel, n) as i:
            for (c, per), s in zip(counts, starts):
                c.n = i * per + s
                before = c.added
            body(i)
            assert all(c.added - before == per for c, per in counts)
        for (c, per), s in zip(counts, starts):
            c.n = s + n * per
    else:
        for i in range(n):
            body(i)
            for (c, per), s in zip(counts, starts):
                assert c.n == s + (i + 1) * per, (c.n, s, i, per)


ROLLED = True


def sl(i, size):
    return bass.ds(i * size, size)


def program(nc, x, c, ctx, c_ctx, w_ada, b_ada, g_pre, g_post, w_in, conv_w, lam_re, lam_im, log_dt,
            b_re, b_im, c_re, c_im, ssm_d, glu_wa, glu_wb, fourier_w, proj_a, proj_b, proj_c, w_out,
            dft_w, dft_t, out):
    w_ada, w_in, conv_w = w_ada[0], w_in[0], conv_w[0]
    glu_wa, glu_wb, fourier_w = glu_wa[0], glu_wb[0], fourier_w[0]
    proj_a, proj_b, proj_c, w_out = proj_a[0], proj_b[0], proj_c[0], w_out[0]

    base = [(nc.sbuf_base + 31) // 32 * 32]
    top = nc.sbuf_usable_end

    def at(name, shape, off, dt=F32):
        n = int(np.prod(shape[1:])) * 4
        assert off + n <= top, (name, off, n, top)
        return nc.alloc_sbuf_tensor_at(name, shape, dt, offset=off)

    class Region:

        def __init__(self, start):
            self.p = start

        def __call__(self, name, shape, dt=F32):
            t = at(name, shape, self.p, dt)
            self.p += int(np.prod(shape[1:])) * 4
            self.p = (self.p + 31) // 32 * 32
            return t

    keep = Region(base[0])
    ident = keep("ident", [128, 128])
    vecs = keep("vecs", [128, V_END])
    cs = keep("cs", [128, KD, 2])
    small = keep("small", [128, 64])
    ones = keep("ones", [128, 128])
    vmod = keep("vmod", [128, 2, KD, 2])
    vcv = keep("vcv", [128, 24])
    wslot_at = keep.p
    wslot = keep("wslot", [128, NSLOT, UNIT * 128])
    hx_at = keep.p
    hx = keep("hx", [128, KD, T])
    scan_at = keep.p

    r = Region(scan_at)
    Ar = r("Ar", [128, L + 1, 128])
    Ai = r("Ai", [128, L + 1, 128])
    B1 = r("B1", [128, 128, H])
    C1 = r("C1", [128, 128, H])
    PWr = r("PWr", [128, 7, 64])
    PWi = r("PWi", [128, 7, 64])
    R8 = r("R8", [128, 64])
    u_at = r.p
    uT = r("uT", [128, NB * (TC + T)])
    abr_at = r.p
    Abr = r("Abr", [128, KW * T])
    block_at = r.p
    hc = r("hc", [128, KD, TC])
    start_at = r.p
    r = Region(block_at)
    V = r("V", [128, 2, GB, L * H])
    t1 = r("t1", [128, GB * (L + 1) * H * 2])
    Cp = r("Cp", [128, 2, GB, (L + 1) * H])
    VT = r("VT", [128, 2, GB, 128])
    Z = at("Z", [128, 2, 2, PB, NQ], r.p - 2 * GB * 128 * 4)
    M = r("M", [128, GB, 128])
    Tl = r("Tl", [16, GB, 15 * H])
    ut = r("ut", [NQ, GB, L, H])
    yt = at("yt", [NX, L, GB * H], r.p - GB * L * H * 4)
    U = r("U", [128, GB, NQ])
    S = r("S", [128, 2, 2, PB, NQ])
    PH = r("PH", [128, 2, 2, PB, NQ])
    X = r("X", [128, 2, PB, 2, NX])
    B2 = r("B2", [128, 2, GB, H])
    C2 = r("C2", [128, 2, GB, H])
    ucur = r("ucur", [128, TC + T])
    gph = r("gph", [128, 2, 8, 32])
    xas = r("xas", [128, T])
    cv = r("cv", [128, T])
    cy = r("cy", [128, T])
    sg = r("sg", [128, T])

    r = Region(start_at)
    xn = r("xn", [128, TT, D])
    ring = r("ring", [128, 4, 4, 512])
    vrow = r("vrow", [V_END, 128])
    lam = r("lam", [128, 2, P])
    ldt = r("ldt", [128, 1])
    ZN = r("ZN", [128, 7, 2, P])
    q2 = r("q2", [128, 2, 128])
    zt = [r(f"zt{i}", [128, P]) for i in range(8)]
    ei = r("ei", [128, P], I32)
    r = Region(u_at)
    cn = r("cn", [128, CT, D])
    braw = r("braw", [128, 2, P * H])
    rows = at("rows", [2, 2 * D], abr_at)
    r = Region(scan_at - KD * T * 4)
    craw = r("craw", [128, H, 2, P])
    Braw = r("Braw", [128, 128, H])
    Brw2 = r("Brw2", [128, 128, H])
    tq = r("tq", [128, 128, H])

    wlo = at("wlo", [128, NSLOT, UNIT * 128], wslot_at, F32R)
    hxh = at("hxh", [128, KD, T], hx_at, F32R)
    r = Region(scan_at)
    whi = r("whi", [128, 2, UNIT * 128], F32R)
    hit = at("hit", [128, 4, T], r.p, F32R)
    gsig = r("gsig", [128, T])
    gtm1 = r("gtm1", [128, T])
    gtm2 = r("gtm2", [128, T])
    gt = r("gt", [128, T])
    dftw = r("dftw", [128, 2, 512])
    b2_at = u_at - KW * T * 4 // 2
    assert r.p <= b2_at
    b2nd = at("b2nd", [128, KW, 2, T], b2_at, F32R)
    mlo = at("mlo", [128, KD, T], b2_at, F32R)
    bah = at("bah", [128, KW, T], abr_at, F32R)
    fT = at("fT", [128, KW * T], abr_at)
    r = Region(block_at)
    bal_at = r.p
    bal = r("bal", [128, KW, T], F32R)
    dftt = at("dftt", [128, 2, TT, T], bal_at)
    mT_at = r.p
    mT = r("mT", [128, KD * T])
    mhi = at("mhi", [128, KD, T], mT_at, F32R)
    hxl_at = r.p
    hxl = r("hxl", [128, KD, T], F32R)
    pp = at("pp", [128, TT, 512], r.p)
    gwt = r("gwt", [128, 4, GC])
    gacc = r("gacc", [128, GC])
    ssq = at("ssq", [128, 16], hxl_at + (KD + TT) * T * 4)
    xr = at("xr", [128, TT, D], hx_at)
    Og = at("Og", [128, TT, D], hxl_at)
    r = Region(abr_at)
    GG = r("GG", [128, D])
    gpart = r("gpart", [128, D])
    grow = r("grow", [1, D])
    baro = r("baro", [1, D])
    gate_dram = nc.dram_tensor("gate_dram", (128, D), F32, kind="Internal").ap()

    ss = nc.alloc_psum_tensor("ss", [128, 4, 512], F32)
    ac = nc.alloc_psum_tensor("ac", [128, 4, 512], F32)

    sems = {}

    def sem(name):
        sems[name] = nc.alloc_semaphore(name)
        return sems[name]

    vec_in, x_in, ssm_in, b_in, ada_used = map(sem, ["vec_in", "x_in", "ssm_in", "b_in", "ada_used"])
    ada_in = [sem(f"ada_in{i}") for i in range(4)]
    w_in_s = [sem(f"w_in{i}") for i in range(NSLOT)]
    w_used = sem("w_used")
    dve_s, act_s, pool_s = map(sem, ["dve_steps", "act_steps", "pool_steps"])
    id_done, vec_ps, vec_cp, sg_done, cs_done = map(sem, ["id_done", "vec_ps", "vec_cp", "sg_done", "cs_done"])
    ada_ps, row_cp, col_ps, col_cp = map(sem, ["ada_ps", "row_cp", "col_ps", "col_cp"])
    zn_done, p0_ps, p0_cp, brw_done = map(sem, ["zn_done", "p0_ps", "p0_cp", "brw_done"])
    pw_tab, bb_done, var_done, rt_done, rs_done, y2_done = map(sem, "pw_tab bb_done var_done rt_done rs_done y2_done".split())
    y_done, h_ps, h_done = map(sem, ["y_done", "h_ps", "h_done"])
    ac_done = sem("ac_done")
    ac_free = [sem(f"ac_free{i}") for i in range(4)]
    (u_cur, ut_ps, ut_cp, u_ps, u_cp, v_done, vt_ps, vt_cp, s_ps, s_cp, k_ps, t_cp, t_add, cp_done, m_in,
     x_done, y_ps, yt_cp, yT_ps, y_pre, ph_done, xa_cp, sig_done, bc2) = map(sem, (
        "u_cur ut_ps ut_cp u_ps u_cp v_done vt_ps vt_cp s_ps s_cp k_ps t_cp t_add cp_done m_in "
        "x_done y_ps yt_cp yT_ps y_pre ph_done xa_cp sig_done bc2").split())
    w_hi, w_lo, hit_done, hl_done, hs_done, b2_done, ba_done, ml_done, o_free, gate_used, gate_out = map(
        sem, "w_hi w_lo hit_done hl_done hs_done b2_done ba_done ml_done o_free gate_used gate_out".split())
    a_done, gs_done, m_done, ge_in, ge_th, ge_done = map(sem, "a_done gs_done m_done ge_in ge_th ge_done".split())
    gl_sig, gl_done, pw_done, f_cp, p_cp, p_ps, f2_cp, dft_in, zc_sig, zc_done = map(
        sem, "gl_sig gl_done pw_done f_cp p_cp p_ps f2_cp dft_in zc_sig zc_done".split())
    gw_in = [sem(f"gw_in{i}") for i in range(4)]
    gb_ps, gg_done, gp_in, o_cp, sq_done, o_done, xr_in, out_s, gpr_ps = map(
        sem, "gb_ps gg_done gp_in o_cp sq_done o_done xr_in out_s gpr_ps".split())

    win = lambda col, n: [(w_in, 0, col, n), (w_in, 1024, col, n)]
    phases = []
    ph_u = (KW // 2, lambda i: [q for j in range(2) for q in win(COL["u"], (i, 2, j))])
    ph_conv = (NB, lambda i: [q for k in ("xa", "ca", "ba", "za") for q in win(COL[k], (i, 1, 0))])

    def ph_merge(branch, mat):
        return (KD // 4, lambda i: [q for j in range(4) for q in
                                    win(COL["gl"] + branch * D, (i, 4, j)) + [(mat, 0, 0, (i, 4, j))]])
    ph_glu = (KW // 4, lambda i: [q for j in range(4) for q in win(COL["zb"], (i, 4, j))
                                  + [(glu_wa, 0, 0, (i, 4, j)), (glu_wb, 0, 0, (i, 4, j))]])
    ph_f = (KW // 4, lambda i: [q for j in range(4) for q in win(COL["f"], (i, 4, j))])
    ph_fw = (KW // 4, lambda i: [q for j in range(4) for q in win(COL["zc"], (i, 4, j))
                                 + [(fourier_w, 0, 0, (i, 4, j))]])
    stream = [ph_u, ph_conv, ph_merge(0, proj_a), ph_glu, ph_merge(1, proj_b), ph_f, ph_fw, ph_merge(2, proj_c)]
    U0, A0 = [0], [0]
    ACCS = (4, 4, 8, 12, 8, 4, 8, 8)
    for (n, units), accs in zip(stream, ACCS):
        U0.append(U0[-1] + n * len(units(0)))
        A0.append(A0[-1] + n * accs)

    MIX = FG

    def freed(eng, k, i, a):
        eng.wait_ge(ac_free[a % 4], i * (ACCS[k] // 4) + ((A0[k] + a) // 4 + 1
                                                         + (MIX if k >= 6 and a % 4 < 2 else 0)))

    def unit(k, i, j):
        per = len(stream[k][1](0)) if k < 8 else 8
        return i * per + (U0[k] + j), (U0[k] + j) % NSLOT, \
            i * (per * 16 // NSLOT) + ((U0[k] + j) // NSLOT + 1) * 16

    block = nc.Block()
    blk = block.__enter__()

    @blk.sync
    def _(sp):
        for rr, src in ((V_BADA, b_ada[0:1, 0:2 * D]), (V_GPRE, g_pre[0:1, :]), (V_CONV, conv_w),
                        (V_SSMD, ssm_d[0:1, :]), (V_C, c[0:1, :]), (V_CC, c_ctx.rearrange("(a n) -> a n", a=1))):
            n = src.shape[0] * src.shape[1] // 128
            sp.dma_start(vrow[rr:rr + n, :], src.rearrange("a (r p) -> (a r) p", p=128)).then_inc(vec_in, 16)
        for i, src in enumerate((lam_re, lam_im)):
            sp.dma_start(lam[:, i, :], src[0].rearrange("d g p -> (d g) p")).then_inc(ssm_in, 16)
        sp.dma_start(ldt[:, :], log_dt[0].rearrange("d (g a) -> (d g) a", a=1)).then_inc(ssm_in, 16)
        for i, src in enumerate((b_re, b_im)):
            sp.dma_start(braw[:, i, :], src[0].rearrange("d g p h -> (d g) (p h)")).then_inc(b_in, 16)
        for i, src in enumerate((c_re, c_im)):
            sp.dma_start(craw[:, :, i, :], src[0].rearrange("d g h p -> (d g) h p")).then_inc(b_in, 16)

        def ada_unit(n):
            q, k = n // 4, n % 4
            col = D + q * 512 if q < 4 else (q - 4) * 512
            if n >= 4:
                sp.wait_ge(ada_used, n - 3)
            sp.dma_start(ring[:, n % 4], w_ada[k * 512:(k + 1) * 512, col:col + 512]
                         .rearrange("(k p) c -> p k c", p=128)).then_inc(ada_in[n % 4], 16)
        for n in range(4):
            ada_unit(n)
        for t in range(TT):
            sp.dma_start(xn[:, t, :], x[0, t * 128:(t + 1) * 128, :]).then_inc(x_in, 16)
        for t in range(CT):
            sp.dma_start(cn[:, t, :], ctx[0, t * 128:(t + 1) * 128, :]).then_inc(x_in, 16)
        for n in range(4, 32):
            ada_unit(n)

        def gate_loads(br, i, j):
            if j == 0 and (br or not isinstance(i, int)):
                col = i * GC + (br * 4 - 1) * GC
                if not isinstance(col, int):
                    sp.compute_val(col * 4)
                sp.wait_ge(gate_used, i * KD + br * 4 * KD)
                sp.dma_start(gate_dram[:, bass.ds(i * GC + (br * 4 - 1) * GC, GC)], gacc[:, :]).then_inc(gate_out, 16)
            if j == 0 and br == 0 and isinstance(i, int):
                sp.wait_ge(a_done, NB)
                sp.wait_ge(y_pre, NB)
            for r in range(4 * j, 4 * j + 4):
                if not isinstance(i, int):
                    sp.compute_val((i * GC + (2 * D + br * 4 * GC)) * 4)
                if br or not isinstance(i, int) or r > 3:
                    sp.wait_ge(gate_used, i * KD + (br * 4 * KD + r - 3))
                sp.dma_start(gwt[:, r % 4, :],
                             w_ada[r * 128:(r + 1) * 128, bass.ds(i * GC + (2 * D + br * 4 * GC), GC)])\
                    .then_inc(gw_in[r % 4], 16)

        for k, (turns, units) in enumerate(stream):
            per = len(units(0))

            def body(i):
                for j, (mat, row, col, (ii, m, jj)) in enumerate(units(i)):
                    u = i * per + (U0[k] + j)
                    s = (U0[k] + j) % NSLOT
                    cc = (ii * m + jj) * 128 + col
                    if not isinstance(cc, int):
                        sp.compute_val(cc * 4)
                    if not isinstance(u, int) or u >= NSLOT:
                        sp.wait_ge(w_used, u - (NSLOT - 1))
                    cc = (ii * m + jj) * 128 + col
                    sp.dma_start(wslot[:, s, :].rearrange("p (k c) -> p k c", k=UNIT),
                                 mat[row:row + 1024, bass.ds(cc, 128)]
                                 .rearrange("(k p) c -> p k c", p=128)).then_inc(w_in_s[s], 16)
                    if k in (2, 4) and j % 3 == 2:
                        gate_loads(k // 2 - 1, i, j // 3)
            repeat(sp, turns, body, peel=(1 if k in (0, 2) else 0))
            if k == 4:
                sp.wait_ge(gate_used, D // GC * KD)
                sp.dma_start(gate_dram[:, D - GC:D], gacc[:, :]).then_inc(gate_out, 16)
            if k == 5:
                sp.wait_ge(w_used, U0[5])
                sp.dma_start(dftw[:, :, :], dft_w.rearrange("(k p) c -> p k c", p=128)).then_inc(dft_in, 16)
                sp.dma_start(dftt[:, :, :, :], dft_t.rearrange("a (k p) c -> p a k c", p=128)).then_inc(dft_in, 16)
        for cb in range(4):
            for j in range(8):
                u = U0[-1] + cb * 8 + j
                sp.wait_ge(w_used, u - (NSLOT - 1))
                sp.dma_start(wslot[:, u % NSLOT, :].rearrange("p (k c) -> p k c", k=2),
                             w_out[j * 256:(j + 1) * 256, cb * 512:(cb + 1) * 512]
                             .rearrange("(k p) c -> p k c", p=128)).then_inc(w_in_s[u % NSLOT], 16)
                if cb == 0 and j == 3:
                    sp.wait_ge(w_used, U0[-1])
                    sp.wait_ge(gate_out, 16 * (D // GC))
                    sp.dma_start(grow[0:1, :], g_post[0:1, :]).then_inc(gp_in, 16)
                    sp.dma_start(baro[0:1, :], b_ada[0:1, 2 * D:3 * D]).then_inc(gp_in, 16)
                    sp.dma_start(gpart[:, :], gate_dram[:, :]).then_inc(gp_in, 16)
            if cb == 1:
                for t in range(TT):
                    sp.dma_start(xr[:, t, :], x[0, t * 128:(t + 1) * 128, :]).then_inc(xr_in, 16)
        for t in range(TT):
            sp.wait_ge(o_done, t + 1)
            sp.dma_start(out[0, t * 128:(t + 1) * 128, :], Og[:, t, :]).then_inc(out_s, 16)
        sp.wait_ge(out_s, 16 * TT)

    @blk.gpsimd
    def _(pool):
        st = Count(pool, pool_s)
        g = nc.gpsimd
        g.memset(ones[:, :], 1.0)
        st.link(g.memset(ident[:, :], 0.0))
        g.affine_select(out=ident[:, :], in_=ident[:, :], compare_op=ALU.not_equal, fill=1.0, base=0,
                        pattern=[[-1, 128]], channel_multiplier=1).then_inc(id_done, 1)
        pool.wait_ge(pw_tab, 6)
        pool.wait_ge(h_done, KD)

        def phases_of(b):
            pool.wait_ge(x_done, b) if not (isinstance(b, int) and b == 0) else None
            re, im = (PH[:, ri].rearrange("p d l q -> p (d l) q") for ri in range(2))
            n, lev = 1, 0
            while n < NQ:
                m = min(n, NQ - n)
                pr, pi = (w[:, lev, sl(b, 8)].unsqueeze(2).to_broadcast([128, 8, m]) for w in (PWr, PWi))
                g.tensor_tensor(re[:, :, n:n + m], re[:, :, 0:m], pr, ALU.mult)
                g.tensor_tensor(im[:, :, n:n + m], re[:, :, 0:m], pi, ALU.mult)
                ta = gph[:, 0, :, 0:m]
                tb = gph[:, 1, :, 0:m]
                g.tensor_tensor(ta, im[:, :, 0:m], pi, ALU.mult)
                st.link(g.tensor_tensor(tb, im[:, :, 0:m], pr, ALU.mult))
                g.tensor_tensor(re[:, :, n:n + m], re[:, :, n:n + m], ta, ALU.subtract)
                last = g.tensor_tensor(im[:, :, n:n + m], im[:, :, n:n + m], tb, ALU.add)
                n, lev = n + m, lev + 1
                if n < NQ:
                    st.link(last)
            last.then_inc(ph_done, 1)
        g.memset(PH[:, 0, :, :, 0:1].rearrange("p d l q -> p (d l) q"), 1.0)
        st.link(g.memset(PH[:, 1, :, :, 0:1].rearrange("p d l q -> p (d l) q"), 0.0))
        repeat(pool, NB, phases_of, [(st, 13)])

        def lo(k, i, j):
            u, s, _ = unit(k, i, j)
            pool.wait_ge(w_hi, u - (U0[2] - 1))
            g.tensor_tensor(wlo[:, s, :], wslot[:, s, :], whi[:, (U0[k] + j) % 2, :].bitcast(F32), ALU.subtract)\
                .then_inc(w_lo, 1)

        def gate_tile(br, i, r):
            n = i * KD + (br * 4 * KD + r)
            pool.wait_ge(gw_in[r % 4], i * 64 + (br * 256 + r // 4 * 16 + 16))
            scale = cs[:, r, 0:1].to_broadcast([128, GC])
            if r == 0:
                if br or not isinstance(i, int):
                    pool.wait_ge(gate_out, i * 16 + br * 64)
                g.tensor_tensor(gacc[:, :], gwt[:, 0, :], scale, ALU.mult).then_inc(gate_used, 1)
            else:
                st.link(g.tensor_tensor(gwt[:, r % 4, :], gwt[:, r % 4, :], scale, ALU.mult))
                pool.wait_ge(gate_used, n)
                g.tensor_tensor(gacc[:, :], gacc[:, :], gwt[:, r % 4, :], ALU.add).then_inc(gate_used, 1)

        def merge_turn(k):
            def body(i):
                for j in range(4):
                    lo(k, i, 3 * j)
                    lo(k, i, 3 * j + 1)
                    for r in (0, 1):
                        gate_tile(k // 2 - 1, i, 4 * j + r)
                    lo(k, i, 3 * j + 2)
                    for r in (2, 3):
                        gate_tile(k // 2 - 1, i, 4 * j + r)
            return body
        pool.wait_ge(y_pre, NB)
        pool.wait_ge(a_done, NB)
        for k in range(2, 9):
            turns = stream[k][0] if k < 8 else 4
            per = len(stream[k][1](0)) if k < 8 else 8
            if k in (2, 4):
                repeat(pool, turns, merge_turn(k), [(st, KD - 1)], peel=(1 if k == 2 else 0))
            else:
                repeat(pool, turns, lambda i: [lo(k, i, j) for j in range(per)])

    @blk.tensor
    def _(pe):
        mm, tr = nc.tensor.matmul, nc.tensor.transpose
        pe.wait_ge(id_done, 1)
        pe.wait_ge(vec_in, 96)
        tr(ss[:, 0, 0:V_END], vrow[:, :], ident[0:V_END, 0:V_END]).then_inc(vec_ps, 1)
        pe.wait_ge(cs_done, 1)

        def ada_half(h):
            for q in range(4 * h, 4 * h + 4):
                if q >= 4:
                    pe.wait_ge(row_cp, q - 3)
                for k in range(4):
                    n = 4 * q + k
                    pe.wait_ge(ada_in[n % 4], 16 * (n // 4 + 1))
                    for j in range(4):
                        last = mm(ac[0:2, q % 4, :], cs[:, 4 * k + j, :], ring[:, n % 4, j, :],
                                  start=(k == 0 and j == 0), stop=(k == 3 and j == 3))
                    last.then_inc(ada_used, 1)

        def cols_half(h):
            pe.wait_ge(row_cp, 4 * h + 4)
            for k in range(KD):
                n = h * KD + k
                last = tr(ss[:, 0, 2 * n:2 * n + 2], rows[:, n * 128:(n + 1) * 128], ident[0:2, 0:2])
            last.then_inc(col_ps, 1)

        ada_half(0)
        pe.wait_ge(zn_done, 1)
        for n in range(7):
            last = tr(ss[:, n // 4, (n % 4) * 128:(n % 4 + 1) * 128],
                      ZN[:, n].rearrange("q a p -> q (a p)"), ident[:, :])
        last.then_inc(p0_ps, 1)
        pe.wait_ge(b_in, 64)
        pe.wait_ge(p0_cp, 1)
        for h in range(H):
            last = tr(ss[:, h // 4, (h % 4) * 128:(h % 4 + 1) * 128],
                      braw[:, :, :].rearrange("q r (p h) -> q (r p) h", h=H)[:, :, h], ident[:, :])
        last.then_inc(p0_ps, 1)
        pe.wait_ge(p0_cp, 2)
        for h in range(H):
            last = tr(ss[:, h // 4, (h % 4) * 128:(h % 4 + 1) * 128],
                      craw[:, h].rearrange("q r p -> q (r p)"), ident[:, :])
        last.then_inc(p0_ps, 1)
        ada_half(1)
        pe.wait_ge(p0_cp, 3)
        cols_half(0)
        cols_half(1)
        pe.wait_ge(col_cp, 1)
        pe.wait_ge(y_done, 6)
        for k in range(KD):
            b = 2 * (k % 2)
            if k >= 2:
                pe.wait_ge(h_done, k - 1)
            for t in range(TT):
                tr(ss[:, b, t * 128:(t + 1) * 128], xn[:, t, k * 128:(k + 1) * 128], ident[:, :])
            for t in range(CT):
                last = tr(ss[:, b + 1, t * 128:(t + 1) * 128], cn[:, t, k * 128:(k + 1) * 128], ident[:, :])
            last.then_inc(h_ps, 1)

        def product(k, i, j, nu, a, rhs, ready=None):
            bank = a % 4
            mix = MIX if k >= 6 and bank < 2 else 0
            if A0[k] + a >= 4 or not isinstance(i, int) or i:
                pe.wait_ge(ac_free[bank], i * (ACCS[k] // 4) + ((A0[k] + a) // 4 + mix))
            for v in range(nu):
                u, s, arrived = unit(k, i, j + v)
                h = (U0[k] + j + v) % 2
                ends = lambda q: dict(start=(v == 0 and q == 0), stop=(v == nu - 1 and q == UNIT - 1))
                if k < 2:
                    pe.wait_ge(w_in_s[s], arrived)
                    for q in range(UNIT):
                        last = mm(ac[:, bank, :], wslot[:, s, q * 128:(q + 1) * 128], rhs(v * UNIT + q), **ends(q))
                    last.then_inc(w_used, 1)
                    continue
                pe.wait_ge(w_hi, u - (U0[2] - 1))
                for q in range(UNIT):
                    if ready:
                        ready(v * UNIT + q)
                    w = whi[:, h, q * 128:(q + 1) * 128]
                    xh, xl = rhs(v * UNIT + q)
                    mm(ac[:, bank, :], w, xh, start=(v == 0 and q == 0), stop=False)
                    mm(ac[:, bank, :], w, xl, start=False, stop=False)
                pe.wait_ge(w_lo, u - (U0[2] - 1))
                for q in range(UNIT):
                    last = mm(ac[:, bank, :], wlo[:, s, q * 128:(q + 1) * 128], rhs(v * UNIT + q)[0],
                              start=False, stop=(v == nu - 1 and q == UNIT - 1))
                last.then_inc(w_used, 1)

        pe.wait_ge(h_done, KD)
        x_of = lambda q: hx[:, q, :]
        xs_of = lambda q: (hxh[:, q, :], hxl[:, q, :])
        ba_of = lambda q: (bah[:, q, :], bal[:, q, :])
        b2_of = lambda q: (b2nd[:, q, 0, :], b2nd[:, q, 1, :])

        def u_turn(i):
            for j in range(2):
                for a in (2 * j, 2 * j + 1):
                    n = i * 4 + a
                    if a >= 4 or not isinstance(n, int) or n >= 4:
                        pe.wait_ge(ac_free[a], i)
                for v in range(2):
                    s = 2 * j + v
                    pe.wait_ge(w_in_s[s], i * 16 + 16)
                    for q in range(UNIT):
                        f = dict(start=(v == 0 and q == 0), stop=(v == 1 and q == UNIT - 1))
                        w = wslot[:, s, q * 128:(q + 1) * 128]
                        lx = mm(ac[:, 2 * j, :], w, hx[:, v * UNIT + q, :], **f)
                        last = mm(ac[:, 2 * j + 1, 0:TC], w, hc[:, v * UNIT + q, :], **f)
                    last.then_inc(w_used, 1)
        repeat(pe, KW // 2, u_turn)

        def conv_turn(b):
            pe.wait_ge(u_cur, b + 1)
            if not (isinstance(b, int) and b == 0):
                pe.wait_ge(y_pre, b)
            for j in range(L):
                last = tr(ss[0:NQ, j // 4, (j % 4) * 128:(j % 4 + 1) * 128], ucur[:, j::L], ident[:, :])
            last.then_inc(ut_ps, 1)
            product(1, b, 0, 2, 0, x_of)
            pe.wait_ge(ut_cp, b + 1)
            for g in range(GB):
                last = tr(ss[:, 2 + g // 4, (g % 4) * NQ:(g % 4 + 1) * NQ],
                          ut[:, g].rearrange("c j h -> c (j h)"), ident[0:NQ, 0:NQ])
            last.then_inc(u_ps, 1)
            pe.wait_ge(v_done, b + 1)
            pe.wait_ge(u_cp, b + 1)
            for d in range(2):
                for g in range(GB):
                    last = tr(ss[:, 2 * d + g // 4, (g % 4) * 128:(g % 4 + 1) * 128], V[:, d, g, :], ident[:, :])
                last.then_inc(vt_ps, 1)
            product(1, b, 2, 2, 1, x_of)
            for d in range(2):
                pe.wait_ge(vt_cp, 2 * b + 1 + d)
                for g in range(GB):
                    last = mm(ss[:, 2 * d + g // 4, (g % 4) * NQ:(g % 4 + 1) * NQ], VT[:, d, g, :], U[:, g, :],
                              start=True, stop=True)
                last.then_inc(s_ps, 1)
            product(1, b, 4, 2, 2, x_of)
            pe.wait_ge(s_cp, 2 * b + 2)
            pe.wait_ge(cp_done, b + 1)
            for d in range(2):
                for g in range(GB):
                    at0 = (L - 1) * H if d == 0 else 0
                    cp0 = 0 if d == 0 else H
                    last = mm(ss[0:H, 2 * d + g // 4, (g % 4) * 128:(g % 4 + 1) * 128],
                              V[:, d, g, at0:at0 + H], Cp[:, d, g, cp0:cp0 + L * H], start=True, stop=True)
            last.then_inc(k_ps, 1)
            product(1, b, 6, 2, 3, x_of)
            pe.wait_ge(t_add, b + 1)
            pe.wait_ge(x_done, b + 1)
            pe.wait_ge(m_in, b * 128 + 128)
            for g in range(GB):
                o = ss[0:NX, g // 4, (g % 4) * 128:(g % 4 + 1) * 128]
                mm(o, U[:, g, NC:NQ], M[:, g, :], start=True, stop=False)
                mm(o, X[:, 0, g // 2, g % 2, :], Cp[:, 0, g, H:(L + 1) * H], start=False, stop=False)
                last = mm(o, X[:, 1, g // 2, g % 2, :], Cp[:, 1, g, 0:L * H], start=False, stop=True)
            last.then_inc(y_ps, 1)
            pe.wait_ge(yt_cp, 1)
            pe.wait_ge(yt_cp, b + 1)
            for i in range(L):
                last = tr(ss[:, 2, i * NX:(i + 1) * NX], yt[:, i, :], ident[0:NX, 0:NX])
            last.then_inc(yT_ps, 1)
        repeat(pe, NB, conv_turn)

        def merge(k, ready, peel=0):
            def body(i):
                first = isinstance(i, int) and i == 0
                for j in range(4):
                    product(k, i, 3 * j, 2, 2 * j, xs_of,
                            (lambda q: pe.wait_ge(hs_done, q + 1)) if k == 2 and first and j == 0 else None)
                    if j == 0:
                        pe.wait_ge(*ready)
                    product(k, i, 3 * j + 2, 1, 2 * j + 1, ba_of)
            repeat(pe, KD // 4, body, peel=peel)
        merge(2, (hs_done, KD + KW), peel=1)

        def glu_turn(i):
            for j in range(4):
                product(3, i, 4 * j, 2, 3 * j, xs_of)
                if j == 0:
                    pe.wait_ge(b2_done, KW)
                for w in range(2):
                    product(3, i, 4 * j + 2 + w, 1, 3 * j + 1 + w, b2_of)
        repeat(pe, KW // 4, glu_turn)
        merge(4, (ba_done, KW))

        def f_turn(i):
            for j in range(4):
                product(5, i, 2 * j, 2, j, xs_of)
        repeat(pe, KW // 4, f_turn)
        for a in range(4):
            freed(pe, 5, 1, a)
        pe.wait_ge(dft_in, 32)
        for gr in range(FG):
            for t in range(TT):
                if gr:
                    pe.wait_ge(p_cp, 4 * (gr - 1) + t + 1)
                for q in range(2):
                    kk = 2 * gr + q
                    last = mm(ss[:, t, :], fT[:, kk * T + t * 128:kk * T + (t + 1) * 128], dftw[:, q, :],
                              start=(q == 0), stop=(q == 1))
                last.then_inc(p_ps, 1)
            pe.wait_ge(p_cp, 4 * gr + 4)
            for wt in range(2):
                n = 2 * gr + wt
                pe.wait_ge(ac_free[n % 2], A0[6] // 4 + n // 2)
                for t in range(TT):
                    for a in range(2):
                        last = mm(ac[:, n % 2, :], pp[:, t, a * 256 + wt * 128:a * 256 + (wt + 1) * 128],
                                  dftt[:, a, t, :], start=(t == 0 and a == 0), stop=(t == 3 and a == 1))
                last.then_inc(pw_done, 1)

        def fw_turn(i):
            for j in range(4):
                product(6, i, 3 * j, 2, 2 * j, xs_of)
                if j == 0:
                    pe.wait_ge(ac_free[0], A0[6] // 4 + MIX)
                    pe.wait_ge(ac_free[1], A0[6] // 4 + MIX)
                product(6, i, 3 * j + 2, 1, 2 * j + 1, b2_of)
        repeat(pe, KW // 4, fw_turn)
        merge(7, (ba_done, 2 * KW))

        for cb in range(4):
            acc = (ac, ss)[cb % 2]
            if cb == 1:
                pe.wait_ge(gg_done, 2)
            for j in range(8):
                u, s, _ = unit(8, cb, j)
                pe.wait_ge(w_hi, u - (U0[2] - 1))
                pe.wait_ge(w_lo, u - (U0[2] - 1))
                if cb == 0:
                    pe.wait_ge(ml_done, 2 * j + 2)
                for t in range(TT):
                    if j == 0 and cb == 0:
                        pe.wait_ge(ac_free[t], A0[8] // 4 + (MIX if t < 2 else 0))
                    if j == 0 and cb > 1:
                        pe.wait_ge(o_free, 4 * (cb - 2) + t + 1)
                    for q in range(2):
                        kk = 2 * j + q
                        mh, ml = (m[:, kk, t * 128:(t + 1) * 128] for m in (mhi, mlo))
                        wh, wl = whi[:, u % 2, q * 512:(q + 1) * 512], wlo[:, s, q * 512:(q + 1) * 512]
                        mm(acc[:, t, :], mh, wh, start=(kk == 0), stop=False)
                        mm(acc[:, t, :], mh, wl, start=False, stop=False)
                        last = mm(acc[:, t, :], ml, wh, start=False, stop=(kk == KD - 1))
                    if j == 7 and t < 3:
                        last.then_inc(ac_done, 1)
                last.then_inc(w_used, 1)
                if cb == 0 and j == 5:
                    pe.wait_ge(gp_in, 48)
                    for q in range(4):
                        mm(ss[:, q, :], ones[:, :], gpart[:, q * 512:(q + 1) * 512], start=True, stop=False)
                        last = mm(ss[:, q, :], ones[0:1, :], baro[0:1, q * 512:(q + 1) * 512], start=False, stop=True)
                    last.then_inc(gb_ps, 1)
                if cb == 0 and j == 6:
                    pe.wait_ge(gg_done, 1)
                    for q in range(4):
                        last = mm(ss[:, q, :], ones[0:1, :], grow[0:1, q * 512:(q + 1) * 512], start=True, stop=True)
                    last.then_inc(gpr_ps, 1)

    @blk.scalar
    def _(act):
        st = Count(act, act_s)
        a = nc.scalar.activation
        cp = lambda o, i, scale=1.0: nc.scalar.activation(o, i, ACT.Copy, scale=scale)
        act.wait_ge(vec_cp, 1)
        a(small[:, 0:32], vecs[:, V_C:V_END], ACT.Sigmoid).then_inc(sg_done, 1)
        act.wait_ge(x_in, 96)
        junk = hc[:, 0:8, :].rearrange("p a b -> p (a b)")
        toks = [xn[:, t, :] for t in range(TT)] + [cn[:, t, :] for t in range(CT)]
        for t, tok in enumerate(toks):
            st.link(a(junk, tok, ACT.Square, accum_out=small[:, 32 + t:33 + t]))
        act.wait_ge(var_done, 1)
        a(small[:, 46:52], small[:, 40:46], ACT.Sqrt).then_inc(rt_done, 1)
        act.wait_ge(rs_done, 1)
        for t, tok in enumerate(toks):
            cp(tok, tok, small[:, 52 + t:53 + t]).then_inc(y_done, 1)

        def rows_half(h):
            for q in range(4 * h, 4 * h + 4):
                act.wait_ge(ada_used, 4 * q + 4)
                cp(rows[:, q * 512:(q + 1) * 512], ac[0:2, q % 4, :]).then_inc(row_cp, 1)
        rows_half(0)
        act.wait_ge(p0_ps, 2)
        for h in range(H):
            last = cp(Braw[:, :, h].rearrange("p (b d g) -> p d b g", b=NB, d=2),
                      ss[:, h // 4, (h % 4) * 128:(h % 4 + 1) * 128].rearrange("p (d b g) -> p d b g", b=NB, d=2))
        last.then_inc(p0_cp, 1)
        act.wait_ge(p0_cp, 2)
        cp(Brw2[0:64, :, :], Braw[64:128, :, :], -1.0)
        cp(Brw2[64:128, :, :], Braw[0:64, :, :]).then_inc(brw_done, 1)
        act.wait_ge(p0_ps, 3)
        for h in range(H):
            for ri in range(2):
                pr = slice(64 * ri, 64 * ri + 64)
                last = cp(C1[pr, :, h].rearrange("p (b d g) -> p d b g", b=NB, d=2),
                          ss[pr, h // 4, (h % 4) * 128:(h % 4 + 1) * 128]
                          .rearrange("p (d b g) -> p d b g", b=NB, d=2), 1.0 - 2.0 * ri)
        last.then_inc(p0_cp, 1)
        rows_half(1)

        def u_turn(i):
            for j in range(2):
                act.wait_ge(w_used, i * 4 + (2 * j + 2))
                o = i * (2 * (TC + T)) + j * (TC + T)
                cp(uT[:, bass.ds(o, TC)], ac[:, 2 * j + 1, 0:TC]).then_inc(ac_free[2 * j + 1], 1)
                cp(uT[:, bass.ds(o + TC, T)], ac[:, 2 * j, :]).then_inc(ac_free[2 * j], 1)
        repeat(act, KW // 2, u_turn)
        act.wait_ge(p0_cp, 3)
        act.wait_ge(bb_done, 1)
        for j in range(4):
            act.wait_ge(ac_free[j], 4)

        def conv_turn(b):
            first = isinstance(b, int) and b == 0
            if not first:
                act.wait_ge(ut_ps, b)
                act.wait_ge(v_done, b)
                act.wait_ge(cp_done, b)
            cp(ucur[:, :], uT[:, sl(b, TC + T)]).then_inc(u_cur, 1)
            for T2, T1, sign in ((B2, B1, -1.0), (C2, C1, 1.0)):
                s1, s2 = T1[64:128, sl(b, 16), :], T1[0:64, sl(b, 16), :]
                cp(T2[0:64].rearrange("p d g h -> p (d g) h"), s1, sign)
                last = cp(T2[64:128].rearrange("p d g h -> p (d g) h"), s2, 1.0 if sign < 0 else -1.0)
            last.then_inc(bc2, 1)
            act.wait_ge(ut_ps, b + 1)
            for q in range(2):
                last = cp(ut[:, :, 4 * q:4 * q + 4, :].rearrange("c g j h -> c j g h"),
                          ss[0:NQ, q, :].rearrange("c (j g h) -> c j g h", j=4, g=GB))
            last.then_inc(ut_cp, 1)
            act.wait_ge(w_used, b * 8 + (U0[1] + 2))
            cp(xas[:, :], ac[:, 0, :]).then_inc(ac_free[0], 1)
            act.wait_ge(u_ps, b + 1)
            for q in range(2):
                last = cp(U[:, 4 * q:4 * q + 4, :], ss[:, 2 + q, 0:4 * NQ].rearrange("p (g c) -> p g c", g=4))
            last.then_inc(u_cp, 1)
            if not first:
                act.wait_ge(x_done, b)
            for d in range(2):
                act.wait_ge(vt_ps, 2 * b + (d + 1))
                for q in range(2):
                    last = cp(VT[:, d, 4 * q:4 * q + 4, :], ss[:, 2 * d + q, :].rearrange("p (g c) -> p g c", g=4))
                last.then_inc(vt_cp, 1)
            for d in range(2):
                act.wait_ge(s_ps, 2 * b + (d + 1))
                for q in range(2):
                    for ri in range(2):
                        for s in range(2):
                            src = ss[64 * ri:64 * ri + 64, 2 * d + q, 0:4 * NQ].rearrange(
                                "p (l s c) -> p l s c", l=2, s=2)[:, :, s, :]
                            dst = S[64 * s:64 * s + 64, ri, d, 2 * q:2 * q + 2, :]
                            if d == 0:
                                last = cp(dst, src)
                            else:
                                cp(dst[:, :, 0:NC], src[:, :, NC - 1::-1])
                                last = cp(dst[:, :, NC:NQ], src[:, :, NQ - 1:NC - 1:-1])
                last.then_inc(s_cp, 1)
            act.wait_ge(k_ps, b + 1)
            if not first:
                act.wait_ge(m_in, b * 128)
            for q in range(2):
                back = ss[0:H, 2 + q, :].rearrange("p (g c) -> p g c", g=4)
                forth = ss[0:H, q, :].rearrange("p (g c) -> p g c", g=4)
                cp(Tl[:, 4 * q:4 * q + 4, 0:128], back)
                last = cp(Tl[:, 4 * q:4 * q + 4, 128:240], forth[:, :, H:128])
            last.then_inc(t_cp, 1)
            act.wait_ge(t_add, b + 1)
            if not first:
                act.wait_ge(y_ps, b)
            for j in range(L):
                act.dma_start(M[H * j:H * j + H, :, :], Tl[:, :, (L - 1 - j) * H:(L - 1 - j) * H + 128])\
                   .then_inc(m_in, 16)
            act.wait_ge(w_used, b * 8 + (U0[1] + 8))
            if not first:
                act.wait_ge(a_done, b)
            a(sg[:, :], ac[:, 3, :], ACT.Sigmoid).then_inc(sig_done, 1)
            act.wait_ge(y_ps, b + 1)
            for q in range(2):
                last = cp(yt[:, :, 64 * q:64 * q + 64].rearrange("c i (g h) -> c g i h", g=4),
                          ss[0:NX, q, :].rearrange("c (g i h) -> c g i h", g=4, i=L))
            last.then_inc(yt_cp, 1)
        repeat(act, NB, conv_turn)
        def hi(k, i, j, first=False):
            u, s, arrived = unit(k, i, j)
            if not first:
                act.wait_ge(w_used, u - 1)
            act.wait_ge(w_in_s[s], arrived)
            cp(whi[:, (U0[k] + j) % 2, :], wslot[:, s, :]).then_inc(w_hi, 1)
        act.wait_ge(cp_done, NB)
        hi(2, 0, 0, True)
        hi(2, 0, 1, True)
        for n in range(KD + KW):
            if n == KD:
                act.wait_ge(a_done, NB)
            if n >= 4:
                act.wait_ge(hl_done, n - 3)
            cp(hit[:, n % 4, :], hx[:, n, :] if n < KD else Abr[:, sl(n - KD, T)]).then_inc(hit_done, 1)
        act.wait_ge(hl_done, KD + KW)

        def merge(k):
            def body(i):
                for j in range(4):
                    hi(k, i, 3 * j + 2)
                    hi(k, i, 3 * j + 3)
                    act.wait_ge(w_used, i * 12 + (U0[k] + 3 * j + 2))
                    if j:
                        freed(act, k, i, 2 * j - 1)
                    elif not isinstance(i, int) or i:
                        freed(act, k, i - 1, 7)
                    a(gsig[:, :], ac[:, (2 * j) % 4, :], ACT.Sigmoid).then_inc(ac_free[(2 * j) % 4], 1)
                    hi(k, i, 3 * j + 4)
                    if k == 2 and j % 2:
                        act.wait_ge(ge_in, i * 2 + (j + 1) // 2)
                        a(gtm1[:, :], gtm1[:, :], ACT.Tanh, scale=math.sqrt(2.0 / math.pi)).then_inc(ge_th, 1)
            repeat(act, KD // 4, body, peel=1)
        merge(2)

        def glu_turn(i):
            for j in range(4):
                hi(3, i, 4 * j + 2)
                hi(3, i, 4 * j + 3)
                act.wait_ge(w_used, i * 16 + (U0[3] + 4 * j + 2))
                if j or not isinstance(i, int) or i:
                    act.wait_ge(gl_done, i * 4 + j)
                a(gsig[:, :], ac[:, (3 * j) % 4, :], ACT.Sigmoid).then_inc(gl_sig, 1)
                hi(3, i, 4 * j + 4)
                hi(3, i, 4 * j + 5)
                act.wait_ge(w_used, i * 16 + (U0[3] + 4 * j + 4))
                a(gtm1[:, :], ac[:, (3 * j + 2) % 4, :], ACT.Sigmoid).then_inc(ac_free[(3 * j + 2) % 4], 1)
        freed(act, 2, 3, 7)
        act.wait_ge(b2_done, KW)
        repeat(act, KW // 4, glu_turn, peel=1)
        act.wait_ge(gl_done, 8)
        merge(4)

        def f_turn(i):
            for j in range(4):
                hi(5, i, 2 * j + 2)
                hi(5, i, 2 * j + 3)
                act.wait_ge(w_used, i * 8 + (U0[5] + 2 * j + 2))
                cp(fT[:, bass.ds(i * (4 * T) + j * T, T)], ac[:, j, :]).then_inc(ac_free[j], 1)
        repeat(act, KW // 4, f_turn)
        act.wait_ge(gate_out, 16 * (D // GC))
        for gr in range(FG):
            for t in range(TT):
                act.wait_ge(p_ps, 4 * gr + t + 1)
                if gr:
                    act.wait_ge(pw_done, 2 * gr)
                cp(pp[:, t, :], ss[:, t, :]).then_inc(p_cp, 1)

        def fw_turn(i):
            for j in range(4):
                hi(6, i, 3 * j + 2)
                hi(6, i, 3 * j + 3)
                act.wait_ge(w_used, i * 12 + (U0[6] + 3 * j + 2))
                if j:
                    freed(act, 6, i, 2 * j - 2)
                elif not isinstance(i, int) or i:
                    freed(act, 6, i - 1, 6)
                a(gsig[:, :], ac[:, (2 * j) % 4, :], ACT.Sigmoid).then_inc(zc_sig, 1)
                hi(6, i, 3 * j + 4)
        freed(act, 4, 3, 7)
        repeat(act, KW // 4, fw_turn, peel=1)
        freed(act, 6, 1, 6)
        merge(7)
        for cb in range(4):
            for j in range(2, 10):
                if cb * 8 + j < 32:
                    hi(8, cb, j)
            if cb == 0:
                act.wait_ge(ml_done, KD)
            for t in range(TT):
                if t < 3:
                    act.wait_ge(ac_done, 3 * cb + t + 1)
                else:
                    act.wait_ge(w_used, U0[-1] + 8 * cb + 8)
                if cb or t:
                    act.wait_ge(sq_done, 4 * cb + t)
                a(gtm2[:, :], (ac, ss)[cb % 2][:, t, :], ACT.Square, accum_out=ssq[:, 4 * t + cb:4 * t + cb + 1])\
                    .then_inc(sq_done, 1)
        act.wait_ge(var_done, 2)
        a(small[:, 46:50], small[:, 40:44], ACT.Sqrt).then_inc(rt_done, 1)

    @blk.vector
    def _(dve):
        st = Count(dve, dve_s)
        v = nc.vector
        tt, ts_, stt, cpy = v.tensor_tensor, v.tensor_scalar, v.scalar_tensor_tensor, v.tensor_copy
        link = st.link
        st.link(v.memset(small[:, :], 0.0))
        dve.wait_ge(vec_ps, 1)
        cpy(vecs[:, :], ss[:, 0, 0:V_END]).then_inc(vec_cp, 1)
        dve.wait_ge(vec_cp, 1)
        dve.wait_ge(sg_done, 1)
        tt(cs[:, :, :].rearrange("p k two -> p two k"), vecs[:, V_C:V_END].rearrange("p (two k) -> p two k", two=2),
           small[:, 0:32].rearrange("p (two k) -> p two k", two=2), ALU.mult).then_inc(cs_done, 1)

        MAGIC = 1.5 * 2.0 ** 23

        def nearest(o, i, scale):
            link(ts_(o, i, scale, MAGIC, ALU.mult, ALU.add))
            link(ts_(o, o, MAGIC, None, ALU.subtract))

        def exp(o, i, n, rr, p, q, e):
            link(ts_(q, i, 88.0, -87.0, ALU.min, ALU.max))
            nearest(n, q, 1.0 / math.log(2.0))
            link(stt(rr, n, -0.693145751953125, q, ALU.mult, ALU.add))
            link(stt(rr, n, -1.42860682030941723e-6, rr, ALU.mult, ALU.add))
            link(ts_(p, rr, 1.0 / 5040, 1.0 / 720, ALU.mult, ALU.add))
            for cc in (1.0 / 120, 1.0 / 24, 1.0 / 6, 0.5, 1.0, 1.0):
                link(tt(p, p, rr, ALU.mult))
                link(ts_(p, p, cc, None, ALU.add))
            link(ts_(e, n, 127.0, 8388608.0, ALU.add, ALU.mult))
            link(ts_(q, i, -87.0, None, ALU.is_ge))
            link(tt(p, p, q, ALU.mult))
            link(tt(o, p, e.bitcast(F32), ALU.mult))

        dve.wait_ge(ssm_in, 48)
        a0, a1, a2, a3, a4, a5, a6, a7 = [z[:, :] for z in zt]
        lre, lim = lam[:, 0, :], lam[:, 1, :]
        exp(a7[:, 0:1], ldt[:, :], a1[:, 0:1], a2[:, 0:1], a3[:, 0:1], a4[:, 0:1], ei[:, 0:1])
        link(ts_(a0, lre, a7[:, 0:1], None, ALU.mult))
        exp(a6, a0, a1, a2, a3, a4, ei[:, :])
        link(ts_(a0, lim, a7[:, 0:1], None, ALU.mult))
        nearest(a1, a0, 1.0 / math.pi)
        link(stt(a2, a1, -3.140625, a0, ALU.mult, ALU.add))
        link(stt(a2, a1, -9.67502593994140625e-4, a2, ALU.mult, ALU.add))
        link(stt(a2, a1, -1.509957990978376432e-7, a2, ALU.mult, ALU.add))
        nearest(a3, a1, 0.5)
        link(stt(a3, a3, -2.0, a1, ALU.mult, ALU.add))
        link(tt(a3, a3, a3, ALU.mult))
        link(ts_(a3, a3, -2.0, 1.0, ALU.mult, ALU.add))
        link(tt(a1, a2, a2, ALU.mult))
        fact = [1.0 / math.factorial(n) for n in range(16)]
        link(ts_(a4, a1, fact[13], -fact[11], ALU.mult, ALU.add))
        for cc in (fact[9], -fact[7], fact[5], -fact[3], 1.0):
            link(tt(a4, a4, a1, ALU.mult))
            link(ts_(a4, a4, cc, None, ALU.add))
        link(tt(a4, a4, a2, ALU.mult))
        link(tt(a4, a4, a3, ALU.mult))
        link(ts_(a5, a1, -fact[14], fact[12], ALU.mult, ALU.add))
        for cc in (-fact[10], fact[8], -fact[6], fact[4], -fact[2], 1.0):
            link(tt(a5, a5, a1, ALU.mult))
            link(ts_(a5, a5, cc, None, ALU.add))
        link(tt(a5, a5, a3, ALU.mult))
        z = lambda n: ZN[:, n, 0, :]
        link(tt(z(0), a6, a5, ALU.mult))
        link(tt(z(1), a6, a4, ALU.mult))
        link(ts_(a0, z(0), 1.0, None, ALU.subtract))
        link(tt(a1, lre, lre, ALU.mult))
        link(tt(a2, lim, lim, ALU.mult))
        link(tt(a1, a1, a2, ALU.add))
        link(v.reciprocal(a1, a1))
        link(tt(a2, a0, lre, ALU.mult))
        link(tt(a3, z(1), lim, ALU.mult))
        link(tt(a2, a2, a3, ALU.add))
        link(tt(z(2), a2, a1, ALU.mult))
        link(tt(a2, z(1), lre, ALU.mult))
        link(tt(a3, a0, lim, ALU.mult))
        link(tt(a2, a2, a3, ALU.subtract))
        link(tt(z(3), a2, a1, ALU.mult))

        def square(re, im, s, t):
            link(tt(s, re, re, ALU.mult))
            link(tt(t, im, im, ALU.mult))
            link(tt(im, re, im, ALU.mult))
            link(tt(re, s, t, ALU.subtract))
            link(ts_(im, im, 2.0, None, ALU.mult))
        for _ in range(3):
            square(a5, a4, a0, a1)
            link(tt(a6, a6, a6, ALU.mult))
        cpy(z(4), a5)
        cpy(z(5), a4)
        link(cpy(z(6), a6))
        cpy(ZN[:, :, 1, :], ZN[:, :, 0, :]).then_inc(zn_done, 1)
        dve.wait_ge(act_s, 6)
        ts_(small[:, 40:46], small[:, 32:38], 1.0 / D, EPS, ALU.mult, ALU.add).then_inc(var_done, 1)
        dve.wait_ge(var_done, 1)

        def rsqrt(n, rt):
            dve.wait_ge(rt_done, rt)
            s40, s46, s52 = small[:, 40:40 + n], small[:, 46:46 + n], small[:, 52:52 + n]
            link(v.reciprocal(s52, s46))
            link(tt(s46, s52, s52, ALU.mult))
            link(tt(s46, s46, s40, ALU.mult))
            link(ts_(s46, s46, -0.5, 1.5, ALU.mult, ALU.add))
            return tt(s52, s52, s46, ALU.mult)
        rsqrt(6, 1).then_inc(rs_done, 1)

        dve.wait_ge(p0_ps, 1)
        col = lambda n: ss[:, n // 4, (n % 4) * 128:(n % 4 + 1) * 128]
        dbg = lambda ap: ap.rearrange("p (d b g) -> p d b g", b=NB, d=2)
        bdg = lambda ap: ap.rearrange("p (b d g) -> p d b g", b=NB, d=2)
        cpy(bdg(Ar[:, 1, :]), dbg(col(0)))
        cpy(bdg(Ai[:, 1, :]), dbg(col(1)))
        cpy(bdg(q2[:, 0, :]), dbg(col(2)))
        cpy(bdg(q2[:, 1, :]), dbg(col(3)))
        for n, dst in ((4, PWr[:, 0, :]), (5, PWi[:, 0, :]), (6, R8[:, :])):
            for s in range(2):
                pr = slice(64 * s, 64 * s + 64)
                last = cpy(dst[pr].rearrange("p (b d l) -> p d b l", b=NB, d=2),
                           col(n)[pr].rearrange("p (d b l s) -> p d b l s", b=NB, d=2, s=2)[:, :, :, :, s])
        last.then_inc(p0_cp, 1)
        dve.wait_ge(p0_cp, 1)
        v.memset(Ar[:, 0, :], 1.0)
        link(v.memset(Ai[:, 0, :], 0.0))
        for n0, m in ((1, 1), (2, 2), (4, 4)):
            mr, mi = (A[:, n0:n0 + 1, :].to_broadcast([128, m, 128]) for A in (Ar, Ai))
            sr, si = Ar[:, 1:1 + m, :], Ai[:, 1:1 + m, :]
            dr, di = Ar[:, n0 + 1:n0 + 1 + m, :], Ai[:, n0 + 1:n0 + 1 + m, :]
            ta = tq[:, 0:8 * m, :].rearrange("p (m a) h -> p m (a h)", m=m)
            tb = tq[:, 32:32 + 8 * m, :].rearrange("p (m a) h -> p m (a h)", m=m)
            tt(dr, sr, mr, ALU.mult)
            tt(di, sr, mi, ALU.mult)
            tt(ta, si, mi, ALU.mult)
            link(tt(tb, si, mr, ALU.mult))
            tt(dr, dr, ta, ALU.subtract)
            link(tt(di, di, tb, ALU.add))
        for n in range(6):
            re, im = PWr[:, n, :], PWi[:, n, :]
            tt(PWr[:, n + 1, :], re, re, ALU.mult)
            tt(a0, im, im, ALU.mult)
            link(tt(a1, re, im, ALU.mult))
            tt(PWr[:, n + 1, :], PWr[:, n + 1, :], a0, ALU.subtract)
            ts_(PWi[:, n + 1, :], a1, 2.0, None, ALU.mult).then_inc(pw_tab, 1)
            dve.wait_ge(pw_tab, n + 1)
        dve.wait_ge(brw_done, 1)
        qb = lambda n: q2[:, n, :].unsqueeze(2).to_broadcast([128, 128, H])
        tt(tq[:, :, :], Brw2[:, :, :], qb(1), ALU.mult)
        link(tt(B1[:, :, :], Braw[:, :, :], qb(0), ALU.mult))
        tt(B1[:, :, :], B1[:, :, :], tq[:, :, :], ALU.add).then_inc(bb_done, 1)
        dve.wait_ge(col_ps, 2)
        mod = vmod
        for h, vb in ((0, 16), (1, 0)):
            last = tt(mod[:, h], ss[:, 0, 32 * h:32 * h + 32].rearrange("p (k two) -> p k two", two=2),
                      vecs[:, V_BADA + vb:V_BADA + vb + 16].unsqueeze(2).to_broadcast([128, KD, 2]), ALU.add)
        link(last)
        stt(mod[:, 0], mod[:, 0], 1.0, vecs[:, V_GPRE:V_GPRE + 16].unsqueeze(2).to_broadcast([128, KD, 2]),
            ALU.add, ALU.mult).then_inc(col_cp, 1)
        dve.wait_ge(col_cp, 1)
        for k in range(KD):
            dve.wait_ge(h_ps, k + 1)
            b = 2 * (k % 2)
            ts_(hx[:, k, :], ss[:, b, :], mod[:, 0, k, 0:1], mod[:, 1, k, 0:1], ALU.mult, ALU.add)
            ts_(hc[:, k, :], ss[:, b + 1, 0:TC], mod[:, 0, k, 1:2], mod[:, 1, k, 1:2], ALU.mult, ALU.add)\
                .then_inc(h_done, 1)

        def powers(dst, A, e0, n, rev, b, d, T1, T2, tmp):
            shape = [128, GB, n, H]
            cols = bass.ds(b * 16 + d * 8, 8)
            es = slice(e0, e0 + n)
            br, bi = (A_[:, es, cols].rearrange("p e g -> p g e").unsqueeze(3).to_broadcast(shape) for A_ in A)
            o = dst.rearrange("p g (m h) -> p g m h", h=H)
            if rev:
                o, tmp = o[:, :, ::-1, :], tmp[:, :, ::-1, :]
            w1, w2 = (q.unsqueeze(2).to_broadcast(shape) for q in (T1, T2))
            tt(o, br, w1, ALU.mult)
            return tt(tmp, bi, w2, ALU.mult), o

        def conv_turn(b):
            dyn = not isinstance(b, int)
            dve.wait_ge(bc2, b + 1)
            if dyn or b:
                dve.wait_ge(k_ps, b)
                dve.wait_ge(y_ps, b)
            for d in range(2):
                tmp = t1[:, d * 1152:d * 1152 + 1024].rearrange("p (g m h) -> p g m h", g=GB, m=L)
                last, o = powers(V[:, d], (Ar, Ai), 0, L, d == 0, b, d, B1[:, bass.ds(b * 16 + d * 8, 8), :],
                                 B2[:, d], tmp)
            link(last)
            for d in range(2):
                tmp = t1[:, d * 1152:d * 1152 + 1024]
                o = V[:, d].rearrange("p g m -> p (g m)")
                last = tt(o, o, tmp, ALU.add)
            last.then_inc(v_done, 1)
            dve.wait_ge(v_done, b + 1)
            for d in range(2):
                tmp = t1[:, d * 1152:d * 1152 + 1152].rearrange("p (g m h) -> p g m h", g=GB, m=L + 1)
                last, o = powers(Cp[:, d], (Ar, Ai), 0, L + 1, d == 1, b, d,
                                 C1[:, bass.ds(b * 16 + d * 8, 8), :], C2[:, d], tmp)
            link(last)
            for d in range(2):
                o = Cp[:, d].rearrange("p g m -> p (g m)")
                last = tt(o, o, t1[:, d * 1152:(d + 1) * 1152], ALU.add)
            last.then_inc(cp_done, 1)
            dve.wait_ge(cp_done, b + 1)
            dve.wait_ge(w_used, b * 8 + (U0[1] + 4))
            freed(dve, 1, b, 0)
            tt(cv[:, :], ac[:, 1, :], xas[:, :], ALU.mult).then_inc(ac_free[1], 1)
            freed(dve, 1, b, 1)
            cw = lambda k: vcv[:, bass.ds(b * 3 + k, 1)]
            rows_of = lambda q: q[:, :].rearrange("p (r c) -> p r c", c=GRID)
            link(ts_(cy[:, :], cv[:, :], cw(1), None, ALU.mult))
            y3, c3 = rows_of(cy), rows_of(cv)
            link(stt(y3[:, :, 1:], c3[:, :, :GRID - 1], cw(0), y3[:, :, 1:], ALU.mult, ALU.add))
            link(stt(y3[:, :, :GRID - 1], c3[:, :, 1:], cw(2), y3[:, :, :GRID - 1], ALU.mult, ALU.add))
            dve.wait_ge(s_cp, 2 * b + 2)
            dve.wait_ge(ph_done, b + 1)
            f = lambda q: q.rearrange("p d l c -> p (d l c)")
            sr, si, pr, pi, zr, zi = (f(q[:, ri]) for q in (S, PH, Z) for ri in range(2))
            n = 2 * PB * NQ
            tt(zr, pr, sr, ALU.mult)
            tt(zi, pr, si, ALU.mult)
            tt(t1[:, 0:n], pi, si, ALU.mult)
            link(tt(t1[:, n:2 * n], pi, sr, ALU.mult))
            tt(zr, zr, t1[:, 0:n], ALU.add)
            link(tt(zi, zi, t1[:, n:2 * n], ALU.subtract))
            for ri in range(2):
                for d in range(2):
                    for l in range(PB):
                        q = Z[:, ri, d, l, :]
                        rr = R8[:, bass.ds(b * 8 + d * 4 + l, 1)]
                        last = v.tensor_tensor_scan(S[:, ri, d, l, :], rr.to_broadcast([128, NQ]), q, 0.0,
                                                    ALU.mult, ALU.add)
            link(last)
            w = slice(NC - 1, NQ - 1)
            ta, tb = (t1[:, n * i:n * i + 512].rearrange("p (d l c) -> p d l c", d=2, l=PB) for i in range(2))
            g3 = lambda q: q.rearrange("p d l c -> p (d l) c")
            P_, S_ = (lambda ri: g3(PH[:, ri])[:, :, w]), (lambda ri: g3(S[:, ri])[:, :, w])
            xs = []
            for ri in range(2):
                oa, ob = (t1[:, (2 * ri + k) * 512:(2 * ri + k + 1) * 512] for k in range(2))
                oa3, ob3 = (q.rearrange("p (m c) -> p m c", c=NX) for q in (oa, ob))
                tt(oa3, P_(0), S_(ri), ALU.mult)
                last = tt(ob3, P_(1), S_(1 - ri), ALU.mult)
            link(last)
            for ri in range(2):
                op = ALU.subtract if ri == 0 else ALU.add
                for s in range(2):
                    for d in range(2):
                        oa, ob = (t1[64 * s:64 * s + 64, (2 * ri + k) * 512 + d * 256:(2 * ri + k) * 512 + d * 256 + 256]
                                  .rearrange("p (l c) -> p l c", l=PB) for k in range(2))
                        dst = X[64 * ri:64 * ri + 64, d, :, s, :]
                        last = tt(dst if d == 0 else dst[:, :, ::-1], oa, ob, op)
            last.then_inc(x_done, 1)
            dve.wait_ge(t_cp, b + 1)
            for q in range(2):
                o = Tl[:, 4 * q:4 * q + 4, 112:128]
                last = tt(o, o, ss[0:H, q, :].rearrange("p (g c) -> p g c", g=4)[:, :, 0:H], ALU.add)
            last.then_inc(t_add, 1)
            dve.wait_ge(w_used, b * 8 + (U0[1] + 8))
            dve.wait_ge(sig_done, b + 1)
            tt(cy[:, :], cy[:, :], ac[:, 2, :], ALU.mult).then_inc(ac_free[2], 1)
            tt(sg[:, :], sg[:, :], ac[:, 3, :], ALU.mult).then_inc(ac_free[3], 1)
            freed(dve, 1, b, 2)
            freed(dve, 1, b, 3)
            tt(Abr[:, sl(b, T)], cy[:, :], sg[:, :], ALU.mult).then_inc(a_done, 1)
            dve.wait_ge(yT_ps, b + 1)
            uo = uT[:, bass.ds(b * (TC + T) + TC, T)].rearrange("p (c i) -> p c i", i=L)
            stt(uo, uo, vecs[:, bass.ds(b + V_SSMD, 1)], ss[:, 2, :].rearrange("p (i c) -> p c i", i=L),
                ALU.mult, ALU.add).then_inc(y_pre, 1)
        st.add(cpy(vcv[:, :].rearrange("p (b k) -> p k b", k=3),
                   vecs[:, V_CONV:V_CONV + 24].rearrange("p (k b) -> p k b", k=3)))
        st.wait()
        repeat(dve, NB, conv_turn, [(st, CONV_STEPS)])
        dve.wait_ge(a_done, NB)
        dve.wait_ge(y_pre, NB)
        dve.wait_ge(y_ps, NB)
        dve.wait_ge(yt_cp, NB)
        dve.wait_ge(yT_ps, NB)
        dve.wait_ge(w_used, U0[2])
        for n in range(KD + KW):
            src = hx[:, n, :] if n < KD else Abr[:, sl(n - KD, T)]
            hi, lo = (hxh[:, n, :], hxl[:, n, :]) if n < KD else (bah[:, n - KD, :], bal[:, n - KD, :])
            dve.wait_ge(hit_done, n + 1)
            tt(lo, src, hit[:, n % 4, :].bitcast(F32), ALU.subtract).then_inc(hl_done, 1)
            cpy(hi, src).then_inc(hs_done, 1)

        def split(hi, lo):
            link(cpy(hi, gt[:, :]))
            return tt(lo, gt[:, :], hi.bitcast(F32), ALU.subtract)

        def gelu_in(b):
            y = uT[:, bass.ds(b * (TC + T) + TC, T)]
            link(tt(gtm1[:, :], y, y, ALU.mult))
            link(ts_(gtm1[:, :], gtm1[:, :], 0.044715, 1.0, ALU.mult, ALU.add))
            tt(gtm1[:, :], gtm1[:, :], y, ALU.mult).then_inc(ge_in, 1)

        def gelu_out(b):
            y = uT[:, bass.ds(b * (TC + T) + TC, T)]
            dve.wait_ge(ge_th, b + 1)
            link(stt(gt[:, :], gtm1[:, :], 1.0, y, ALU.add, ALU.mult))
            link(ts_(gt[:, :], gt[:, :], 0.5, None, ALU.mult))
            o = b2nd[:, bass.ds(b, 1), :, :].rearrange("p a h t -> p (a h) t")
            split(o[:, 0, :], o[:, 1, :]).then_inc(b2_done, 1)

        def merge(k, br):
            def body(i):
                for j in range(4):
                    o = mT[:, bass.ds(i * (4 * T) + j * T, T)]
                    freed(dve, k, i, 2 * j)
                    dve.wait_ge(w_used, i * 12 + (U0[k] + 3 * j + 3))
                    free = ac_free[(2 * j + 1) % 4]
                    if br and (j or not isinstance(i, int) or i):
                        dve.wait_ge(m_done, i * 4 + (16 * (br - 1) + j))
                    tt(o if br == 0 else gtm2[:, :], ac[:, (2 * j + 1) % 4, :], gsig[:, :], ALU.mult)\
                        .then_inc(free, 1)
                    if br == 0 and j % 2:
                        gelu_in(i * 2 + j // 2)
                        gelu_out(i * 2 + j // 2)
                    if br:
                        freed(dve, k, i, 2 * j + 1)
                        tt(o if br == 1 else gt[:, :], o, gtm2[:, :], ALU.add).then_inc(m_done, 1)
                    if br == 2:
                        dve.wait_ge(m_done, i * 4 + (16 + j + 1))
                        n = bass.ds(i * 4 + j, 1)
                        split(mhi[:, n, :].rearrange("p a t -> p (a t)"),
                              mlo[:, n, :].rearrange("p a t -> p (a t)")).then_inc(ml_done, 1)
            repeat(dve, KD // 4, body, [(st, (10, 0, 4)[br])])
        merge(2, 0)
        freed(dve, 2, 3, 5)
        freed(dve, 2, 3, 7)

        def glu_turn(i):
            for j in range(4):
                za, wa, wb = ((3 * j + q) % 4 for q in range(3))
                dve.wait_ge(gl_sig, i * 4 + (j + 1))
                dve.wait_ge(w_used, i * 16 + (U0[3] + 4 * j + 4))
                tt(gtm2[:, :], ac[:, za, :], gsig[:, :], ALU.mult).then_inc(ac_free[za], 1)
                freed(dve, 3, i, 3 * j + 2)
                tt(gtm1[:, :], ac[:, wa, :], gtm1[:, :], ALU.mult).then_inc(ac_free[wa], 1)
                freed(dve, 3, i, 3 * j)
                freed(dve, 3, i, 3 * j + 1)
                tt(gt[:, :], gtm1[:, :], gtm2[:, :], ALU.mult).then_inc(gl_done, 1)
                dve.wait_ge(gl_done, i * 4 + (j + 1))
                n = bass.ds(i * 4 + j, 1)
                split(bah[:, n, :].rearrange("p a t -> p (a t)"),
                      bal[:, n, :].rearrange("p a t -> p (a t)")).then_inc(ba_done, 1)
        repeat(dve, KW // 4, glu_turn, [(st, 4)])
        merge(4, 1)
        for n in range(2 * FG):
            dve.wait_ge(pw_done, n + 1)
            link(cpy(b2nd[:, n, 0, :], ac[:, n % 2, :]))
            tt(b2nd[:, n, 1, :], ac[:, n % 2, :], b2nd[:, n, 0, :].bitcast(F32), ALU.subtract)\
                .then_inc(ac_free[n % 2], 1)

        def fw_turn(i):
            for j in range(4):
                zc, fw = (2 * j) % 4, (2 * j + 1) % 4
                dve.wait_ge(zc_sig, i * 4 + (j + 1))
                tt(gtm2[:, :], ac[:, zc, :], gsig[:, :], ALU.mult).then_inc(ac_free[zc], 1)
                freed(dve, 6, i, 2 * j)
                dve.wait_ge(w_used, i * 12 + (U0[6] + 3 * j + 3))
                tt(gt[:, :], ac[:, fw, :], gtm2[:, :], ALU.mult).then_inc(ac_free[fw], 1)
                freed(dve, 6, i, 2 * j + 1)
                n = bass.ds(i * 4 + j, 1)
                split(bah[:, n, :].rearrange("p a t -> p (a t)"),
                      bal[:, n, :].rearrange("p a t -> p (a t)")).then_inc(ba_done, 1)
        repeat(dve, KW // 4, fw_turn, [(st, 4)])
        merge(7, 2)
        flat = ss[:, :, :].rearrange("p q c -> p (q c)")
        dve.wait_ge(gb_ps, 1)
        cpy(GG[:, :], flat).then_inc(gg_done, 1)
        dve.wait_ge(gg_done, 1)
        dve.wait_ge(gpr_ps, 1)
        tt(GG[:, :], GG[:, :], flat, ALU.mult).then_inc(gg_done, 1)
        dve.wait_ge(gg_done, 2)
        for cb in range(4):
            for t in range(TT):
                dve.wait_ge(sq_done, 4 * cb + t + 1)
                w = slice(cb * 512, cb * 512 + 512)
                tt(Og[:, t, w], (ac, ss)[cb % 2][:, t, :], GG[:, w], ALU.mult).then_inc(o_free, 1)
        link(v.tensor_reduce(small[:, 40:44], ssq[:, :].rearrange("p (t c) -> p t c", t=TT),
                             mybir.AxisListType.X, ALU.add))
        ts_(small[:, 40:44], small[:, 40:44], 1.0 / D, EPS, ALU.mult, ALU.add).then_inc(var_done, 1)
        dve.wait_ge(var_done, 2)
        link(rsqrt(4, 2))
        dve.wait_ge(o_free, 4 * TT)
        dve.wait_ge(xr_in, 64)
        for t in range(TT):
            stt(Og[:, t, :], Og[:, t, :], small[:, 52 + t:53 + t], xr[:, t, :], ALU.mult, ALU.add).then_inc(o_done, 1)

    block.__exit__(None, None, None)


CONV_STEPS = 9

NAMES = ['x', 'c', 'ctx', 'c_ctx', 'w_ada', 'b_ada', 'g_pre', 'g_post', 'w_in', 'conv_w', 'ssm_lam_re',
         'ssm_lam_im', 'ssm_log_dt', 'ssm_b_re', 'ssm_b_im', 'ssm_c_re', 'ssm_c_im', 'ssm_d', 'glu_wa', 'glu_wb',
         'fourier_w', 'proj_a', 'proj_b', 'proj_c', 'w_out']


def fourier_tables():
    k = np.arange(FGW)
    w = 2 * np.pi * (np.outer(k, k) % FGW) / FGW
    dft_w = np.concatenate([np.cos(w), np.sin(w)], 1) / np.sqrt(FGW)
    k = np.arange(T)
    w = 2 * np.pi * (np.outer(k, k) % T) / T
    dft_t = np.stack([np.cos(w), -np.sin(w)]) / np.sqrt(T)
    return dft_w.astype(np.float32), dft_t.astype(np.float32)


def kernel(**inputs):
    import concourse.bacc as bacc
    from concourse.bass_utils import run_bass_kernel_spmd

    nc = bacc.Bacc("TRN2", target_bir_lowering=False, num_devices=1)
    dft_w, dft_t = fourier_tables()
    arrays, args = {}, []
    for name in NAMES:
        arrays[name] = np.ascontiguousarray(inputs[name])
    arrays["dft_w"], arrays["dft_t"] = dft_w, dft_t
    for name, a in arrays.items():
        args.append(nc.dram_tensor(name, a.shape, mybir.dt.from_np(a.dtype), kind="ExternalInput").ap())
    args.append(nc.dram_tensor("out", (1, T, D), F32, kind="ExternalOutput").ap())
    program(nc, *args)
    r = run_bass_kernel_spmd(nc, [arrays], core_ids=[0])
    return r.results[0]["out"]
```

```python
import math

import numpy as np

import concourse.bass as bass
from concourse import mybir

F32 = mybir.dt.float32
F32R = mybir.dt.float32r
I32 = mybir.dt.int32
ALU = mybir.AluOpType
ACT = mybir.ActivationFunctionType

D = 2048
T = 512
TC = 256
GRID = 64
W = 1024
H, P, G = 16, 64, 64
FG, FGW = 4, 256
EPS = 1e-6
KD, KW = D // 128, W // 128
TT, CT = T // 128, TC // 128
L = 8
NC, NX = TC // L, T // L
NQ = NC + NX
TU = TC + T
GB = 128 // H
NB = G // GB
PB = GB // 2
COL = dict(xa=0, ba=W, ca=2 * W, za=3 * W, u=4 * W, zb=5 * W, f=6 * W, zc=7 * W, gl=8 * W)
NSLOT = 4
TAB = 2 * (L + 1) * 2 * GB + 2 * 2 * GB * H
GC = 256
UNIT = 8

V_BADA, V_GPRE, V_CONV, V_C, V_CC, V_END = 0, 32, 48, 72, 88, 104


class Count:

    def __init__(self, eng, sem):
        self.eng, self.sem, self.n, self.added = eng, sem, 0, 0

    def add(self, ins):
        ins.then_inc(self.sem, 1)
        self.n = self.n + 1
        self.added += 1
        return self.n

    def wait(self, n=None):
        self.eng.wait_ge(self.sem, self.n if n is None else n)

    def link(self, ins):
        self.add(ins)
        self.wait()


def repeat(eng, n, body, counts=(), peel=0):
    starts = [c.n for c, _ in counts]
    for i in range(peel):
        body(i)
    if peel < n:
        with eng.Fori(peel, n) as i:
            for (c, per), s in zip(counts, starts):
                c.n = i * per + s
            body(i)
    for (c, per), s in zip(counts, starts):
        c.n = s + n * per


def sl(i, size):
    return bass.ds(i * size, size)


def program(nc, x, c, ctx, c_ctx, w_ada, b_ada, g_pre, g_post, w_in, conv_w, lam_re, lam_im, log_dt,
            b_re, b_im, c_re, c_im, ssm_d, glu_wa, glu_wb, fourier_w, proj_a, proj_b, proj_c, w_out,
            dft_w, dft_t, out):
    w_ada, w_in, conv_w = w_ada[0], w_in[0], conv_w[0]
    glu_wa, glu_wb, fourier_w = glu_wa[0], glu_wb[0], fourier_w[0]
    proj_a, proj_b, proj_c, w_out = proj_a[0], proj_b[0], proj_c[0], w_out[0]

    base = [(nc.sbuf_base + 31) // 32 * 32]
    top = nc.sbuf_usable_end

    def at(name, shape, off, dt=F32):
        n = int(np.prod(shape[1:])) * 4
        assert off + n <= top, (name, off, n, top)
        return nc.alloc_sbuf_tensor_at(name, shape, dt, offset=off)

    class Region:

        def __init__(self, start):
            self.p = start

        def __call__(self, name, shape, dt=F32):
            t = at(name, shape, self.p, dt)
            self.p += int(np.prod(shape[1:])) * 4
            self.p = (self.p + 31) // 32 * 32
            return t

    keep = Region(base[0])
    ident = keep("ident", [128, 128])
    vecs = keep("vecs", [128, V_END])
    cs = keep("cs", [128, KD, 2])
    small = keep("small", [128, 64])
    vmod = keep("vmod", [128, 2, KD, 2])
    vcv = keep("vcv", [128, 24])
    dtab = keep("dtab", [128, G])
    wslot_at = keep.p
    wslot = keep("wslot", [128, NSLOT, UNIT * 128])
    hx_at = keep.p
    wlo = at("wlo", [128, NSLOT, UNIT * 128], wslot_at, F32R)
    hx_at = keep.p
    hxh = keep("hxh", [128, KD, T], F32R)
    whi_at = keep.p
    whi = keep("whi", [128, 2, UNIT * 128], F32R)
    hxl_at = keep.p
    hxl = keep("hxl", [128, KD, T], F32R)
    abr_at = keep.p

    r = Region(abr_at)
    Abr = r("Abr", [128, KW * T])
    PWr = r("PWr", [128, 7, 64])
    PWi = r("PWi", [128, 7, 64])
    R8 = r("R8", [128, 64])
    tab_at = r.p
    tab = r("tab", [128, TAB])
    tAr, tAi = (tab[:, n * (L + 1) * 16:(n + 1) * (L + 1) * 16].rearrange("p (e c) -> p e c", c=16) for n in range(2))
    tB1, tC1 = (tab[:, 2 * (L + 1) * 16 + n * 256:2 * (L + 1) * 16 + (n + 1) * 256]
                .rearrange("p (c h) -> p c h", h=H) for n in range(2))
    ys = r("ys", [128, GB, NX])
    block_at = r.p
    V = r("V", [128, 2, GB, L * H])
    t1 = r("t1", [128, GB * (L + 1) * H * 2])
    Cp = r("Cp", [128, 2, GB, (L + 1) * H])
    VT = r("VT", [128, 2, GB, 128])
    Z = at("Z", [128, 2, 2, PB, NQ], r.p - 2 * GB * 128 * 4)
    M = r("M", [128, GB, 128])
    Tl = r("Tl", [16, GB, 15 * H])
    U = r("U", [128, GB, NQ])
    S = r("S", [128, 2, 2, PB, NQ])
    PH = r("PH", [128, 2, 2, PB, NQ])
    X = r("X", [128, 2, PB, 2, NX])
    B2 = r("B2", [128, 2, GB, H])
    C2 = r("C2", [128, 2, GB, H])
    gph = r("gph", [128, 2, 8, 32])
    xas = r("xas", [128, T])
    cv = r("cv", [128, T])
    cy = r("cy", [128, T])
    sg = r("sg", [128, T])

    hch = at("hch", [128, KD, TC], abr_at, F32R)
    htmp = at("htmp", [128, 3, TU], tab_at)
    r = Region(tab_at + 3 * TU * 4)
    hcl_at = r.p
    hcl = r("hcl", [128, KD, TC], F32R)
    xn = r("xn", [128, TT, D])
    uS = at("uS", [128, 2, TU], r.p - TT * D * 4)
    cn = r("cn", [128, CT, D])
    Ar = r("Ar", [128, L + 1, 128])
    Ai = r("Ai", [128, L + 1, 128])
    B1 = r("B1", [128, 128, H])
    C1 = r("C1", [128, 128, H])
    drow = at("drow", [G, L, H], abr_at)
    braw = at("braw", [128, 2, P * H], hcl_at)
    junk = at("junk", [128, D], hcl_at + 2 * P * H * 4)
    rows = at("rows", [2, 2 * D], abr_at)
    r = Region(hx_at)
    craw = r("craw", [128, H, 2, P])
    Braw = r("Braw", [128, 128, H])
    Brw2 = r("Brw2", [128, 128, H])
    tq = r("tq", [128, 128, H])
    ring = at("ring", [128, 4, 4, 512], hxl_at)
    r = Region(whi_at)
    vrow = r("vrow", [V_END, 128])
    lam = r("lam", [128, 2, P])
    ldt = r("ldt", [128, 1])
    ZN = r("ZN", [128, 7, 2, P])
    q2 = r("q2", [128, 2, 128])
    zt = [r(f"zt{i}", [128, P]) for i in range(8)]
    ei = r("ei", [128, P], I32)
    assert r.p <= hxl_at

    bah = at("bah", [128, KW, T], abr_at, F32R)
    fT = at("fT", [128, KW * T], abr_at)
    r = Region(abr_at + KW * T * 4)
    bal_at = r.p
    bal = r("bal", [128, KW, T], F32R)
    dftt = at("dftt", [128, 2, TT, T], bal_at)
    mT_at = r.p
    mT = r("mT", [128, KD * T])
    mhi = at("mhi", [128, KD, T], mT_at, F32R)
    b2_at = r.p
    b2nd = r("b2nd", [128, KW, 2, T], F32R)
    yin = at("yin", [128, KW * T], b2_at + KW * T * 4)
    mlo = at("mlo", [128, KD, T], b2_at, F32R)
    hit = at("hit", [128, 4, T], r.p, F32R)
    gsig = r("gsig", [128, T])
    gtm1 = r("gtm1", [128, T])
    gtm2 = r("gtm2", [128, T])
    gt = r("gt", [128, T])
    dftw = r("dftw", [128, 2, FGW])
    p128 = r("p128", [128, TT, 128])
    ssq = r("ssq", [128, 16])
    ones = r("ones", [128, 128])
    pp = at("pp", [128, 2, TT, FGW], r.p)
    gwt = r("gwt", [128, 4, GC])
    gacc = r("gacc", [128, GC])
    xr = at("xr", [128, TT, D], hx_at)
    Og = at("Og", [128, TT, D], hxl_at)
    r = Region(abr_at)
    GG = r("GG", [128, D])
    gpart = r("gpart", [128, D])
    grow = r("grow", [1, D])
    baro = r("baro", [1, D])
    gate_dram = nc.dram_tensor("gate_dram", (128, D), F32, kind="Internal").ap()
    tab_dram = nc.dram_tensor("tab_dram", (128, NB * TAB), F32, kind="Internal").ap()
    fw_dram = nc.dram_tensor("fw_dram", (W, W), F32, kind="Internal").ap()
    u_dram = nc.dram_tensor("u_dram", (128, NB * TU), F32, kind="Internal").ap()
    y_dram = nc.dram_tensor("y_dram", (128, NB * T), F32, kind="Internal").ap()

    ss = nc.alloc_psum_tensor("ss", [128, 4, 512], F32)
    ac = nc.alloc_psum_tensor("ac", [128, 4, 512], F32)

    sem = nc.alloc_semaphore

    ada_in, u_out, gw_in = ([sem(f"{name}{i}") for i in range(n)]
                            for name, n in (("ada_in", 4), ("u_out", 2), ("gw_in", 4)))
    w_in_s = [sem(f"w_in{i}") for i in range(NSLOT)]
    ac_free = [sem(f"ac_free{i}") for i in range(4)]
    dve_s, act_s, pool_s = (sem(name) for name in ("dve_steps", "act_steps", "pool_steps"))
    vec_in, x_in, ssm_in, b_in, ada_used, w_used, id_done, vec_ps, vec_cp = map(
        sem, "vec_in x_in ssm_in b_in ada_used w_used id_done vec_ps vec_cp".split())
    sg_done, cs_done, row_cp, col_ps, col_cp, zn_done, p0_ps, p0_cp, brw_done = map(
        sem, "sg_done cs_done row_cp col_ps col_cp zn_done p0_ps p0_cp brw_done".split())
    pw_tab, bb_done, var_done, rt_done, rs_done, y_done, h_ps, h_done, ac_done = map(
        sem, "pw_tab bb_done var_done rt_done rs_done y_done h_ps h_done ac_done".split())
    v_done, vt_ps, vt_cp, s_ps, s_cp, k_ps, t_cp, t_add, cp_done = map(
        sem, "v_done vt_ps vt_cp s_ps s_cp k_ps t_cp t_add cp_done".split())
    m_in, x_done, y_ps, y_pre, ph_done, sig_done, bc2, fw_out, hc_done = map(
        sem, "m_in x_done y_ps y_pre ph_done sig_done bc2 fw_out hc_done".split())
    zeroed, y128_ps, mix_done, tab_out, tab_in, u_in, us_done, y_out, y_in = map(
        sem, "zeroed y128_ps mix_done tab_out tab_in u_in us_done y_out y_in".split())
    ht_done, hh_done, w_hi, w_lo, hit_done, hl_done, hs_done, b2_done, ba_done = map(
        sem, "ht_done hh_done w_hi w_lo hit_done hl_done hs_done b2_done ba_done".split())
    ml_done, o_free, gate_used, gate_out, a_done, m_done, ge_in, ge_th, gl_sig = map(
        sem, "ml_done o_free gate_used gate_out a_done m_done ge_in ge_th gl_sig".split())
    gl_done, pw_done, p_cp, p_ps, dft_in, zc_sig, gb_ps, gg_done, gp_in = map(
        sem, "gl_done pw_done p_cp p_ps dft_in zc_sig gb_ps gg_done gp_in".split())
    sq_done, o_done, xr_in, out_s, gpr_ps = map(
        sem, "sq_done o_done xr_in out_s gpr_ps".split())

    win = lambda col, n: [(w_in, 0, col, n), (w_in, 1024, col, n)]
    ph_u = (KW // 2, lambda i: [q for j in range(2) for q in win(COL["u"], (i, 2, j))])
    ph_conv = (NB, lambda i: [q for k in ("xa", "ca", "ba", "za") for q in win(COL[k], (i, 1, 0))])

    def ph_merge(branch, mat):
        return (KD // 4, lambda i: [q for j in range(4) for q in
                                    win(COL["gl"] + branch * D, (i, 4, j)) + [(mat, 0, 0, (i, 4, j))]])
    ph_glu = (KW // 4, lambda i: [q for j in range(4) for q in win(COL["zb"], (i, 4, j))
                                  + [(glu_wa, 0, 0, (i, 4, j)), (glu_wb, 0, 0, (i, 4, j))]])
    ph_f = (KW // 4, lambda i: [q for j in range(4) for q in win(COL["f"], (i, 4, j))])
    ph_fw = (KW // 4, lambda i: [q for j in range(4) for q in win(COL["zc"], (i, 4, j))
                                 + [(fw_dram, 0, 0, (i, 4, j))]])
    stream = [ph_u, ph_conv, ph_merge(0, proj_a), ph_glu, ph_merge(1, proj_b), ph_f, ph_fw, ph_merge(2, proj_c)]
    U0, A0 = [0], [0]
    ACCS = (4, 4, 8, 12, 8, 4, 8, 8)
    for (n, units), accs in zip(stream, ACCS):
        U0.append(U0[-1] + n * len(units(0)))
        A0.append(A0[-1] + n * accs)

    MIX = FG

    def freed(eng, k, i, a):
        eng.wait_ge(ac_free[a % 4], i * (ACCS[k] // 4) + ((A0[k] + a) // 4 + 1
                                                         + (MIX if k >= 6 and a % 4 < 2 else 0)))

    def unit(k, i, j):
        per = len(stream[k][1](0)) if k < 8 else 8
        return i * per + (U0[k] + j), (U0[k] + j) % NSLOT, \
            i * (per * 16 // NSLOT) + ((U0[k] + j) // NSLOT + 1) * 16

    block = nc.Block()
    blk = block.__enter__()

    @blk.sync
    def _(sp):
        for rr, src in ((V_BADA, b_ada[0:1, 0:2 * D]), (V_GPRE, g_pre[0:1, :]), (V_CONV, conv_w),
                        (V_C, c[0:1, :]), (V_CC, c_ctx.rearrange("(a n) -> a n", a=1))):
            n = src.shape[0] * src.shape[1] // 128
            sp.dma_start(vrow[rr:rr + n, :], src.rearrange("a (r p) -> (a r) p", p=128)).then_inc(vec_in, 16)
        sp.dma_start(drow[:, :, :], ssm_d.rearrange("a (n h) -> (a n) h", h=H).unsqueeze(1).to_broadcast([G, L, H]))\
          .then_inc(vec_in, 16)

        def ada_unit(n):
            q, k = n // 4, n % 4
            col = D + q * 512 if q < 4 else (q - 4) * 512
            if n >= 4:
                sp.wait_ge(ada_used, n - 3)
            sp.dma_start(ring[:, n % 4], w_ada[k * 512:(k + 1) * 512, col:col + 512]
                         .rearrange("(k p) c -> p k c", p=128)).then_inc(ada_in[n % 4], 16)
        for n in range(2):
            ada_unit(n)
        for i, src in enumerate((lam_re, lam_im)):
            sp.dma_start(lam[:, i, :], src[0].rearrange("d g p -> (d g) p")).then_inc(ssm_in, 16)
        sp.dma_start(ldt[:, :], log_dt[0].rearrange("d (g a) -> (d g) a", a=1)).then_inc(ssm_in, 16)
        for n in range(2, 4):
            ada_unit(n)
        others = [(braw[:, i, :], src[0].rearrange("d g p h -> (d g) (p h)"), b_in)
                  for i, src in enumerate((b_re, b_im))] \
            + [(craw[:, :, i, :], src[0].rearrange("d g h p -> (d g) h p"), b_in)
               for i, src in enumerate((c_re, c_im))] \
            + [(cn[:, t, :], ctx[0, t * 128:(t + 1) * 128, :], x_in) for t in range(CT)] \
            + [(xn[:, t, :], x[0, t * 128:(t + 1) * 128, :], x_in) for t in range(TT)]
        for n in range(4, 32):
            ada_unit(n)
            if n in EXTRAS:
                dst, src, done = others.pop(0)
                sp.dma_start(dst, src).then_inc(done, 16)
        assert not others

        def gate_loads(br, i, j):
            if j == 0 and (br or not isinstance(i, int)):
                col = i * GC + (br * 4 - 1) * GC
                if not isinstance(col, int):
                    sp.compute_val(col * 4)
                sp.wait_ge(gate_used, i * KD + br * 4 * KD)
                sp.dma_start(gate_dram[:, bass.ds(i * GC + (br * 4 - 1) * GC, GC)], gacc[:, :]).then_inc(gate_out, 16)
            if j == 0 and br == 0 and isinstance(i, int):
                sp.wait_ge(a_done, NB)
                y_store(NB - 1)
                sp.wait_ge(y_out, 16 * L * NB)
                sp.wait_ge(y_ps, NB)
                sp.dma_start(yin[:, :], y_dram[:, :]).then_inc(y_in, 16)
            for r in range(4 * j, 4 * j + 4):
                if not isinstance(i, int):
                    sp.compute_val((i * GC + (2 * D + br * 4 * GC)) * 4)
                if br or not isinstance(i, int) or r > 3:
                    sp.wait_ge(gate_used, i * KD + (br * 4 * KD + r - 3))
                sp.dma_start(gwt[:, r % 4, :],
                             w_ada[r * 128:(r + 1) * 128, bass.ds(i * GC + (2 * D + br * 4 * GC), GC)])\
                    .then_inc(gw_in[r % 4], 16)

        def u_store(i, j):
            if not isinstance(i, int):
                sp.compute_val((i * 2 + j) * (TU * 4))
            sp.wait_ge(ac_free[2 * j], i + 1)
            sp.dma_start(u_dram[:, bass.ds((i * 2 + j) * TU, TU)], uS[:, j, :]).then_inc(u_out[j], 16)

        def tab_load(b):
            if not isinstance(b, int):
                sp.compute_val(b * (TAB * 4))
                sp.wait_ge(cp_done, b)
            sp.dma_start(tab[:, :], tab_dram[:, bass.ds(b * TAB, TAB)]).then_inc(tab_in, 16)

        def u_load(b):
            for l in range(L):
                if not isinstance(b, int):
                    sp.compute_val((b * TU + l * NQ) * 4)
                    sp.wait_ge(y_ps, b)
                    sp.wait_ge(us_done, b)
                sp.dma_start(U[H * l:H * l + H, :, :],
                             u_dram.rearrange("(g h) n -> h g n", h=H)[:, :, bass.ds(b * TU + l * NQ, NQ)])\
                    .then_inc(u_in, 16)

        def y_store(b):
            for l in range(L):
                if not isinstance(b, int):
                    sp.compute_val((b * T + l * NX) * 4)
                sp.wait_ge(y_pre, b + 1)
                sp.dma_start(y_dram.rearrange("(g h) n -> h g n", h=H)[:, :, bass.ds(b * T + l * NX, NX)],
                             ys[H * l:H * l + H, :, :]).then_inc(y_out, 16)

        sp.wait_ge(bb_done, 1)
        sp.wait_ge(p0_cp, 3)
        at_ = 0
        for src in (Ar[:, :, :], Ai[:, :, :]):
            for e in range(L + 1):
                sp.dma_start(tab_dram.rearrange("p (b n) -> p b n", n=TAB)[:, :, at_:at_ + 16],
                             src[:, e, :].rearrange("p (b n) -> p b n", n=16)).then_inc(tab_out, 16)
                at_ += 16
        for src in (B1, C1):
            sp.dma_start(tab_dram.rearrange("p (b n) -> p b n", n=TAB)[:, :, at_:at_ + 256],
                         src[:, :, :].rearrange("p (b c) h -> p b (c h)", c=16)).then_inc(tab_out, 16)
            at_ += 256

        for k, (turns, units) in enumerate(stream):
            per = len(units(0))
            def body(i):
                if k == 1 and not (isinstance(i, int) and i == 0):
                    tab_load(i)
                for j, (mat, row, col, (ii, m, jj)) in enumerate(units(i)):
                    u = i * per + (U0[k] + j)
                    s = (U0[k] + j) % NSLOT
                    cc = (ii * m + jj) * 128 + col
                    if not isinstance(cc, int):
                        sp.compute_val(cc * 4)
                    if not isinstance(u, int) or u >= NSLOT:
                        sp.wait_ge(w_used, u - (NSLOT - 1))
                    cc = (ii * m + jj) * 128 + col
                    sp.dma_start(wslot[:, s, :].rearrange("p (k c) -> p k c", k=UNIT),
                                 mat[row:row + 1024, bass.ds(cc, 128)]
                                 .rearrange("(k p) c -> p k c", p=128)).then_inc(w_in_s[s], 16)
                    if k == 0 and j % 2 and not (isinstance(i, int) and i == 0):
                        u_store(i - 1, j // 2)
                    if k == 1 and j == 1 and isinstance(i, int) and i == 0:
                        u_store(KW // 2 - 1, 0)
                        u_store(KW // 2 - 1, 1)
                        sp.wait_ge(tab_out, 16 * TAB_STORES)
                        for q in range(2):
                            sp.wait_ge(u_out[q], 8 * NB)
                        sp.wait_ge(w_used, U0[1])
                        tab_load(0)
                        u_load(0)
                    if k == 1 and j == 3 and not (isinstance(i, int) and i == 0):
                        u_load(i)
                        y_store(i - 1)
                    if k == 5 and j == 2 and isinstance(i, int):
                        sp.wait_ge(gate_used, D // GC * KD)
                        sp.dma_start(gate_dram[:, D - GC:D], gacc[:, :]).then_inc(gate_out, 16)
                    if k in (2, 4) and j % 3 == 2:
                        gate_loads(k // 2 - 1, i, j // 3)
            repeat(sp, turns, body, peel=(1 if k < 3 or k == 5 else 0))
            if k in (1, 2, 3, 4):
                r0 = (k - 1) * FGW
                sp.dma_start(fw_dram[r0:r0 + 129, :], fourier_w[r0:r0 + 129, :]).then_inc(fw_out, 16)
                sp.dma_start(fw_dram[r0 + 129:r0 + FGW, :].rearrange("r (a c) -> a r c", a=2),
                             fourier_w[r0 + 129:r0 + FGW, :].rearrange("r (a c) -> a r c", a=2)[:, ::-1, :])\
                    .then_inc(fw_out, 16)
            if k == 5:
                sp.wait_ge(fw_out, 32 * FG)
                sp.wait_ge(w_used, U0[5])
                sp.dma_start(dftw[:, :, :], dft_w.rearrange("(k p) c -> p k c", p=128)).then_inc(dft_in, 16)
                sp.dma_start(dftt[:, :, :, :], dft_t.rearrange("a (k p) c -> p a k c", p=128)).then_inc(dft_in, 16)
        for cb in range(4):
            for j in range(8):
                u = U0[-1] + cb * 8 + j
                sp.wait_ge(w_used, u - (NSLOT - 1))
                sp.dma_start(wslot[:, u % NSLOT, :].rearrange("p (k c) -> p k c", k=2),
                             w_out[j * 256:(j + 1) * 256, cb * 512:(cb + 1) * 512]
                             .rearrange("(k p) c -> p k c", p=128)).then_inc(w_in_s[u % NSLOT], 16)
                if cb == 0 and j == 3:
                    sp.wait_ge(w_used, U0[-1])
                    sp.wait_ge(gate_out, 16 * (D // GC))
                    sp.dma_start(grow[0:1, :], g_post[0:1, :]).then_inc(gp_in, 16)
                    sp.dma_start(baro[0:1, :], b_ada[0:1, 2 * D:3 * D]).then_inc(gp_in, 16)
                    sp.dma_start(gpart[:, :], gate_dram[:, :]).then_inc(gp_in, 16)
            if cb == 1:
                for t in range(TT):
                    sp.dma_start(xr[:, t, :], x[0, t * 128:(t + 1) * 128, :]).then_inc(xr_in, 16)
        for n in range(2 * TT):
            t, w = n // 2, slice(n % 2 * D // 2, (n % 2 + 1) * D // 2)
            sp.wait_ge(o_done, n + 1)
            sp.dma_start(out[0, t * 128:(t + 1) * 128, w], Og[:, t, w]).then_inc(out_s, 16)
        sp.wait_ge(out_s, 16 * 2 * TT)

    @blk.gpsimd
    def _(pool):
        st = Count(pool, pool_s)
        g = nc.gpsimd
        st.link(g.memset(ident[:, :], 0.0))
        g.affine_select(out=ident[:, :], in_=ident[:, :], compare_op=ALU.not_equal, fill=1.0, base=0,
                        pattern=[[-1, 128]], channel_multiplier=1).then_inc(id_done, 1)
        pool.wait_ge(pw_tab, 6)
        for k in range(KD):
            pool.wait_ge(hh_done, k + 1)
            g.tensor_tensor(hxl[:, k, :], htmp[:, k % 3, 0:T], hxh[:, k, :].bitcast(F32), ALU.subtract)\
                .then_inc(h_done, 1)

        def lo(k, i, j):
            u, s, _ = unit(k, i, j)
            pool.wait_ge(w_hi, u + 1)
            g.tensor_tensor(wlo[:, s, :], wslot[:, s, :], whi[:, (U0[k] + j) % 2, :].bitcast(F32), ALU.subtract)\
                .then_inc(w_lo, 1)

        def conv_turn(b):
            if not (isinstance(b, int) and b == 0):
                pool.wait_ge(x_done, b)
            re, im = (PH[:, ri].rearrange("p d l q -> p (d l) q") for ri in range(2))
            n, lev = 1, 0
            while n < NQ:
                m = min(n, NQ - n)
                pr, pi = (w[:, lev, sl(b, 8)].unsqueeze(2).to_broadcast([128, 8, m]) for w in (PWr, PWi))
                g.tensor_tensor(re[:, :, n:n + m], re[:, :, 0:m], pr, ALU.mult)
                g.tensor_tensor(im[:, :, n:n + m], re[:, :, 0:m], pi, ALU.mult)
                ta = gph[:, 0, :, 0:m]
                tb = gph[:, 1, :, 0:m]
                g.tensor_tensor(ta, im[:, :, 0:m], pi, ALU.mult)
                st.link(g.tensor_tensor(tb, im[:, :, 0:m], pr, ALU.mult))
                g.tensor_tensor(re[:, :, n:n + m], re[:, :, n:n + m], ta, ALU.subtract)
                last = g.tensor_tensor(im[:, :, n:n + m], im[:, :, n:n + m], tb, ALU.add)
                n, lev = n + m, lev + 1
                if n < NQ:
                    st.link(last)
                if lev == 5:
                    lo(1, b, 2)
                if lev == 6:
                    lo(1, b, 3)
            last.then_inc(ph_done, 1)
            for j in range(4, 10):
                lo(1, b, j)

        for j in range(2):
            lo(0, 0, j)
        for i in range(KW // 2):
            for j in range(2, 6):
                lo(0, i, j)
        pool.wait_ge(w_used, U0[1])
        g.memset(PH[:, 0, :, :, 0:1].rearrange("p d l q -> p (d l) q"), 1.0)
        st.link(g.memset(PH[:, 1, :, :, 0:1].rearrange("p d l q -> p (d l) q"), 0.0))
        repeat(pool, NB, conv_turn, [(st, 13)], peel=1)

        def gate_tile(br, i, r):
            n = i * KD + (br * 4 * KD + r)
            pool.wait_ge(gw_in[r % 4], i * 64 + (br * 256 + r // 4 * 16 + 16))
            scale = cs[:, r, 0:1].to_broadcast([128, GC])
            if r == 0:
                if br or not isinstance(i, int):
                    pool.wait_ge(gate_out, i * 16 + br * 64)
                g.tensor_tensor(gacc[:, :], gwt[:, 0, :], scale, ALU.mult).then_inc(gate_used, 1)
            else:
                st.link(g.tensor_tensor(gwt[:, r % 4, :], gwt[:, r % 4, :], scale, ALU.mult))
                pool.wait_ge(gate_used, n)
                g.tensor_tensor(gacc[:, :], gacc[:, :], gwt[:, r % 4, :], ALU.add).then_inc(gate_used, 1)

        def merge_turn(k):
            def body(i):
                for j in range(4):
                    lo(k, i, 3 * j + 2)
                    lo(k, i, 3 * j + 3)
                    for r in (0, 1):
                        gate_tile(k // 2 - 1, i, 4 * j + r)
                    lo(k, i, 3 * j + 4)
                    for r in (2, 3):
                        gate_tile(k // 2 - 1, i, 4 * j + r)
            return body
        pool.wait_ge(y_ps, NB)
        pool.wait_ge(a_done, NB)
        g.memset(ones[:, :], 1.0)
        for k in range(2, 9):
            turns = stream[k][0] if k < 8 else 4
            per = len(stream[k][1](0)) if k < 8 else 8
            if k in (2, 4):
                repeat(pool, turns, merge_turn(k), [(st, KD - 1)], peel=(1 if k == 2 else 0))
            elif k < 8:
                repeat(pool, turns, lambda i: [lo(k, i, j) for j in range(2, per + 2)])
            else:
                repeat(pool, turns - 1, lambda i: [lo(k, i, j) for j in range(2, per + 2)])
                for j in range(2, per):
                    lo(k, turns - 1, j)

    @blk.tensor
    def _(pe):
        mm, tr = nc.tensor.matmul, nc.tensor.transpose
        pe.wait_ge(id_done, 1)
        pe.wait_ge(vec_in, 96)
        tr(ss[:, 0, 0:V_END], vrow[:, :], ident[0:V_END, 0:V_END])
        tr(ss[:, 1, 0:G], drow[:, :, :].rearrange("n l h -> n (l h)"), ident[0:G, 0:G]).then_inc(vec_ps, 1)
        pe.wait_ge(cs_done, 1)

        def ada_half(h):
            for q in range(4 * h, 4 * h + 4):
                if q >= 4:
                    pe.wait_ge(row_cp, q - 3)
                for k in range(4):
                    n = 4 * q + k
                    pe.wait_ge(ada_in[n % 4], 16 * (n // 4 + 1))
                    for j in range(4):
                        last = mm(ac[0:2, q % 4, :], cs[:, 4 * k + j, :], ring[:, n % 4, j, :],
                                  start=(k == 0 and j == 0), stop=(k == 3 and j == 3))
                    last.then_inc(ada_used, 1)

        def cols_half(h):
            pe.wait_ge(row_cp, 4 * h + 4)
            for k in range(KD):
                n = h * KD + k
                last = tr(ss[:, 0, 2 * n:2 * n + 2], rows[:, n * 128:(n + 1) * 128], ident[0:2, 0:2])
            last.then_inc(col_ps, 1)

        ada_half(0)
        pe.wait_ge(zn_done, 1)
        for n in range(7):
            last = tr(ss[:, n // 4, (n % 4) * 128:(n % 4 + 1) * 128],
                      ZN[:, n].rearrange("q a p -> q (a p)"), ident[:, :])
        last.then_inc(p0_ps, 1)
        pe.wait_ge(b_in, 64)
        pe.wait_ge(p0_cp, 1)
        for h in range(H):
            last = tr(ss[:, h // 4, (h % 4) * 128:(h % 4 + 1) * 128],
                      braw[:, :, :].rearrange("q r (p h) -> q (r p) h", h=H)[:, :, h], ident[:, :])
        last.then_inc(p0_ps, 1)
        pe.wait_ge(p0_cp, 2)
        for h in range(H):
            last = tr(ss[:, h // 4, (h % 4) * 128:(h % 4 + 1) * 128],
                      craw[:, h].rearrange("q r p -> q (r p)"), ident[:, :])
        last.then_inc(p0_ps, 1)
        ada_half(1)
        pe.wait_ge(p0_cp, 3)
        cols_half(0)
        cols_half(1)
        pe.wait_ge(col_cp, 1)
        pe.wait_ge(y_done, 6)
        for k in range(KD):
            b = 2 * (k % 2)
            if k >= 2:
                pe.wait_ge(ht_done, k - 1)
            for t in range(TT):
                tr(ss[:, b, t * 128:(t + 1) * 128], xn[:, t, k * 128:(k + 1) * 128], ident[:, :])
            for t in range(CT):
                last = tr(ss[:, b + 1, t * 128:(t + 1) * 128], cn[:, t, k * 128:(k + 1) * 128], ident[:, :])
            last.then_inc(h_ps, 1)

        xs_of = lambda q: (hxh[:, q, :], hxl[:, q, :])
        ba_of = lambda q: (bah[:, q, :], bal[:, q, :])
        b2_of = lambda q: (b2nd[:, q, 0, :], b2nd[:, q, 1, :])

        def product(k, i, j, nu, a, rhs):
            bank = a % 4
            mix = MIX if k >= 6 and bank < 2 else 0
            if A0[k] + a >= 4 or not isinstance(i, int) or i:
                pe.wait_ge(ac_free[bank], i * (ACCS[k] // 4) + ((A0[k] + a) // 4 + mix))
            for v in range(nu):
                u, s, arrived = unit(k, i, j + v)
                h = (U0[k] + j + v) % 2
                pe.wait_ge(w_hi, u + 1)
                for q in range(UNIT):
                    w = whi[:, h, q * 128:(q + 1) * 128]
                    xh, xl = rhs(v * UNIT + q)
                    mm(ac[:, bank, :], w, xh, start=(v == 0 and q == 0), stop=False)
                    mm(ac[:, bank, :], w, xl, start=False, stop=False)
                pe.wait_ge(w_lo, u + 1)
                for q in range(UNIT):
                    last = mm(ac[:, bank, :], wlo[:, s, q * 128:(q + 1) * 128], rhs(v * UNIT + q)[0],
                              start=False, stop=(v == nu - 1 and q == UNIT - 1))
                last.then_inc(w_used, 1)

        def u_turn(i):
            for j in range(2):
                for a in (2 * j, 2 * j + 1):
                    n = i * 4 + a
                    if a >= 4 or not isinstance(n, int) or n >= 4:
                        pe.wait_ge(ac_free[a], i)
                for v in range(2):
                    u, s, _ = unit(0, i, 2 * j + v)
                    pe.wait_ge(w_hi, u + 1)
                    for q in range(UNIT):
                        n = v * UNIT + q
                        if isinstance(i, int) and i == 0 and j == 0:
                            pe.wait_ge(h_done, n + 1)
                            pe.wait_ge(hc_done, n + 1)
                        w = whi[:, v, q * 128:(q + 1) * 128]
                        f = dict(start=(n == 0), stop=False)
                        mm(ac[:, 2 * j, :], w, hxh[:, n, :], **f)
                        mm(ac[:, 2 * j, :], w, hxl[:, n, :], start=False, stop=False)
                        mm(ac[:, 2 * j + 1, 0:TC], w, hch[:, n, :], **f)
                        mm(ac[:, 2 * j + 1, 0:TC], w, hcl[:, n, :], start=False, stop=False)
                    pe.wait_ge(w_lo, u + 1)
                    for q in range(UNIT):
                        n = v * UNIT + q
                        w = wlo[:, s, q * 128:(q + 1) * 128]
                        f = dict(start=False, stop=(n == KD - 1))
                        mm(ac[:, 2 * j, :], w, hxh[:, n, :], **f)
                        last = mm(ac[:, 2 * j + 1, 0:TC], w, hch[:, n, :], **f)
                    last.then_inc(w_used, 1)
        repeat(pe, KW // 2, u_turn, peel=1)

        def conv_turn(b):
            product(1, b, 0, 2, 0, xs_of)
            pe.wait_ge(v_done, b + 1)
            if not (isinstance(b, int) and b == 0):
                pe.wait_ge(y_pre, b)
            for d in range(2):
                for g in range(GB):
                    last = tr(ss[:, 2 * d + g // 4, (g % 4) * 128:(g % 4 + 1) * 128], V[:, d, g, :], ident[:, :])
                last.then_inc(vt_ps, 1)
            product(1, b, 2, 2, 1, xs_of)
            pe.wait_ge(u_in, b * (16 * L) + 16 * L)
            for d in range(2):
                pe.wait_ge(vt_cp, 2 * b + 1 + d)
                for g in range(GB):
                    last = mm(ss[:, 2 * d + g // 4, (g % 4) * NQ:(g % 4 + 1) * NQ], VT[:, d, g, :], U[:, g, :],
                              start=True, stop=True)
                last.then_inc(s_ps, 1)
            product(1, b, 4, 2, 2, xs_of)
            pe.wait_ge(s_cp, 2 * b + 2)
            pe.wait_ge(cp_done, b + 1)
            for d in range(2):
                for g in range(GB):
                    at0 = (L - 1) * H if d == 0 else 0
                    cp0 = 0 if d == 0 else H
                    last = mm(ss[0:H, 2 * d + g // 4, (g % 4) * 128:(g % 4 + 1) * 128],
                              V[:, d, g, at0:at0 + H], Cp[:, d, g, cp0:cp0 + L * H], start=True, stop=True)
            last.then_inc(k_ps, 1)
            product(1, b, 6, 2, 3, xs_of)
            pe.wait_ge(t_add, b + 1)
            pe.wait_ge(x_done, b + 1)
            pe.wait_ge(m_in, b * 128 + 128)
            for g in range(GB):
                o = ss[:, 0, g * NX:(g + 1) * NX]
                mm(o, M[:, g, :], U[:, g, NC:NQ], start=True, stop=False)
                mm(o, Cp[:, 0, g, H:(L + 1) * H], X[:, 0, g // 2, g % 2, :], start=False, stop=False)
                last = mm(o, Cp[:, 1, g, 0:L * H], X[:, 1, g // 2, g % 2, :], start=False, stop=True)
            last.then_inc(y_ps, 1)
        repeat(pe, NB, conv_turn, peel=1)

        def merge(k, ready):
            def body(i):
                for j in range(4):
                    product(k, i, 3 * j, 2, 2 * j, xs_of)
                    if j == 0:
                        pe.wait_ge(*ready)
                    product(k, i, 3 * j + 2, 1, 2 * j + 1, ba_of)
            repeat(pe, KD // 4, body)
        merge(2, (hs_done, KW))

        def glu_turn(i):
            for j in range(4):
                product(3, i, 4 * j, 2, 3 * j, xs_of)
                if j == 0:
                    pe.wait_ge(b2_done, KW)
                for w in range(2):
                    product(3, i, 4 * j + 2 + w, 1, 3 * j + 1 + w, b2_of)
        repeat(pe, KW // 4, glu_turn)
        merge(4, (ba_done, KW))

        def f_turn(i):
            for j in range(4):
                product(5, i, 2 * j, 2, j, xs_of)
        repeat(pe, KW // 4, f_turn)
        for a in range(4):
            freed(pe, 5, 1, a)
        pe.wait_ge(dft_in, 32)
        def channels(gr):
            if gr >= 2:
                pe.wait_ge(p_cp, gr - 1)
            pair = ss[:, gr % 2 * 2:gr % 2 * 2 + 2, :].rearrange("p b (t c) -> p (b t) c", c=FGW)
            for t in range(TT):
                for q in range(2):
                    kk = 2 * gr + q
                    last = mm(pair[:, t, :], fT[:, kk * T + t * 128:kk * T + (t + 1) * 128], dftw[:, q, :],
                              start=(q == 0), stop=(q == 1))
            last.then_inc(p_ps, 1)

        channels(0)
        for gr in range(FG):
            if gr + 1 < FG:
                channels(gr + 1)
            pe.wait_ge(p_cp, gr + 1)
            if gr == FG - 1:
                for t in range(TT):
                    last = mm(ss[:, 0, :], p128[:, t, :], dftt[:, 0, t, :], start=(t == 0), stop=(t == TT - 1))
                last.then_inc(y128_ps, 1)
            for a in range(2):
                pe.wait_ge(ac_free[a], A0[6] // 4 + gr)
                for t in range(TT):
                    last = mm(ac[:, a, :], pp[:, gr % 2, t, a * 128:(a + 1) * 128], dftt[:, a, t, :],
                              start=(t == 0), stop=(t == TT - 1))
                last.then_inc(pw_done, 1)

        def fw_turn(i):
            for j in range(4):
                product(6, i, 3 * j, 2, 2 * j, xs_of)
                if j == 0:
                    pe.wait_ge(mix_done, 1)
                product(6, i, 3 * j + 2, 1, 2 * j + 1, b2_of)
        repeat(pe, KW // 4, fw_turn)
        merge(7, (ba_done, 2 * KW))

        for cb in range(4):
            acc = (ac, ss)[cb % 2]
            if cb == 1:
                pe.wait_ge(gg_done, 2)
            for j in range(8):
                u, s, _ = unit(8, cb, j)
                pe.wait_ge(w_hi, u + 1)
                pe.wait_ge(w_lo, u + 1)
                if cb == 0:
                    pe.wait_ge(ml_done, 2 * j + 2)
                for t in range(TT):
                    if j == 0 and cb == 0:
                        pe.wait_ge(ac_free[t], A0[8] // 4 + (MIX if t < 2 else 0))
                    if j == 0 and cb > 1:
                        pe.wait_ge(o_free, 4 * (cb - 2) + t + 1)
                    for q in range(2):
                        kk = 2 * j + q
                        mh, ml = (m[:, kk, t * 128:(t + 1) * 128] for m in (mhi, mlo))
                        wh, wl = whi[:, u % 2, q * 512:(q + 1) * 512], wlo[:, s, q * 512:(q + 1) * 512]
                        mm(acc[:, t, :], mh, wh, start=(kk == 0), stop=False)
                        mm(acc[:, t, :], mh, wl, start=False, stop=False)
                        last = mm(acc[:, t, :], ml, wh, start=False, stop=(kk == KD - 1))
                    if j == 7 and t < 3:
                        last.then_inc(ac_done, 1)
                last.then_inc(w_used, 1)
                if cb == 0 and j == 5:
                    pe.wait_ge(gp_in, 48)
                    for q in range(4):
                        mm(ss[:, q, :], ones[:, :], gpart[:, q * 512:(q + 1) * 512], start=True, stop=False)
                        last = mm(ss[:, q, :], ones[0:1, :], baro[0:1, q * 512:(q + 1) * 512], start=False, stop=True)
                    last.then_inc(gb_ps, 1)
                if cb == 0 and j == 6:
                    pe.wait_ge(gg_done, 1)
                    for q in range(4):
                        last = mm(ss[:, q, :], ones[0:1, :], grow[0:1, q * 512:(q + 1) * 512], start=True, stop=True)
                    last.then_inc(gpr_ps, 1)

    @blk.scalar
    def _(act):
        st = Count(act, act_s)
        a = nc.scalar.activation
        cp = lambda o, i, scale=1.0: nc.scalar.activation(o, i, ACT.Copy, scale=scale)
        act.wait_ge(vec_cp, 1)
        a(small[:, 0:32], vecs[:, V_C:V_END], ACT.Sigmoid).then_inc(sg_done, 1)
        def rows_half(h):
            for q in range(4 * h, 4 * h + 4):
                act.wait_ge(ada_used, 4 * q + 4)
                cp(rows[:, q * 512:(q + 1) * 512], ac[0:2, q % 4, :]).then_inc(row_cp, 1)
        rows_half(0)
        act.wait_ge(p0_ps, 2)
        for h in range(H):
            last = cp(Braw[:, :, h].rearrange("p (b d g) -> p d b g", b=NB, d=2),
                      ss[:, h // 4, (h % 4) * 128:(h % 4 + 1) * 128].rearrange("p (d b g) -> p d b g", b=NB, d=2))
        last.then_inc(p0_cp, 1)
        act.wait_ge(p0_cp, 2)
        cp(Brw2[0:64, :, :], Braw[64:128, :, :], -1.0)
        cp(Brw2[64:128, :, :], Braw[0:64, :, :]).then_inc(brw_done, 1)
        act.wait_ge(p0_ps, 3)
        for h in range(H):
            for ri in range(2):
                pr = slice(64 * ri, 64 * ri + 64)
                last = cp(C1[pr, :, h].rearrange("p (b d g) -> p d b g", b=NB, d=2),
                          ss[pr, h // 4, (h % 4) * 128:(h % 4 + 1) * 128]
                          .rearrange("p (d b g) -> p d b g", b=NB, d=2), 1.0 - 2.0 * ri)
        last.then_inc(p0_cp, 1)
        act.wait_ge(x_in, 96)
        toks = [xn[:, t, :] for t in range(TT)] + [cn[:, t, :] for t in range(CT)]
        for t, tok in enumerate(toks):
            st.link(a(junk[:, :], tok, ACT.Square, accum_out=small[:, 32 + t:33 + t]))
        act.wait_ge(var_done, 1)
        a(small[:, 46:52], small[:, 40:46], ACT.Sqrt).then_inc(rt_done, 1)
        act.wait_ge(rs_done, 1)
        for t, tok in enumerate(toks):
            cp(tok, tok, small[:, 52 + t:53 + t]).then_inc(y_done, 1)

        rows_half(1)

        def hi(k, i, j):
            u, s, arrived = unit(k, i, j)
            if k or j > 1 or not isinstance(i, int) or i:
                act.wait_ge(w_used, u - 1)
            act.wait_ge(w_in_s[s], arrived)
            cp(whi[:, (U0[k] + j) % 2, :], wslot[:, s, :]).then_inc(w_hi, 1)
        for k in range(KD):
            act.wait_ge(ht_done, k + 1)
            cp(hxh[:, k, :], htmp[:, k % 3, 0:T])
            cp(hch[:, k, :], htmp[:, k % 3, T:TU]).then_inc(hh_done, 1)
            if k < 2:
                act.wait_ge(bb_done, 1)
                hi(0, 0, k)

        def u_turn(i):
            for j in range(2):
                hi(0, i, 2 * j + 2)
                hi(0, i, 2 * j + 3)
                act.wait_ge(w_used, i * 4 + (2 * j + 2))
                if not (isinstance(i, int) and i == 0):
                    act.wait_ge(u_out[j], i * 16)
                places = lambda q: q.rearrange("p (c l) -> p l c", l=L)
                o = uS[:, j, :].rearrange("p (l c) -> p l c", c=NQ)
                cp(o[:, :, 0:NC], places(ac[:, 2 * j + 1, 0:TC])).then_inc(ac_free[2 * j + 1], 1)
                act.wait_ge(ac_free[2 * j + 1], i + 1)
                cp(o[:, :, NC:NQ], places(ac[:, 2 * j, :])).then_inc(ac_free[2 * j], 1)
        repeat(act, KW // 2, u_turn, peel=1)

        def conv_turn(b):
            first = isinstance(b, int) and b == 0
            if not first:
                act.wait_ge(v_done, b)
                act.wait_ge(cp_done, b)
            act.wait_ge(tab_in, b * 16 + 16)
            for T2, T1, sign in ((B2, tB1, -1.0), (C2, tC1, 1.0)):
                s1, s2 = T1[64:128], T1[0:64]
                cp(T2[0:64].rearrange("p d g h -> p (d g) h"), s1, sign)
                last = cp(T2[64:128].rearrange("p d g h -> p (d g) h"), s2, 1.0 if sign < 0 else -1.0)
            last.then_inc(bc2, 1)
            hi(1, b, 2)
            hi(1, b, 3)
            act.wait_ge(w_used, b * 8 + (U0[1] + 2))
            cp(xas[:, :], ac[:, 0, :]).then_inc(ac_free[0], 1)
            if not first:
                act.wait_ge(x_done, b)
            for d in range(2):
                act.wait_ge(vt_ps, 2 * b + (d + 1))
                for q in range(2):
                    last = cp(VT[:, d, 4 * q:4 * q + 4, :], ss[:, 2 * d + q, :].rearrange("p (g c) -> p g c", g=4))
                last.then_inc(vt_cp, 1)
            hi(1, b, 4)
            hi(1, b, 5)
            for d in range(2):
                act.wait_ge(s_ps, 2 * b + (d + 1))
                for q in range(2):
                    for ri in range(2):
                        for s in range(2):
                            src = ss[64 * ri:64 * ri + 64, 2 * d + q, 0:4 * NQ].rearrange(
                                "p (l s c) -> p l s c", l=2, s=2)[:, :, s, :]
                            dst = S[64 * s:64 * s + 64, ri, d, 2 * q:2 * q + 2, :]
                            if d == 0:
                                last = cp(dst, src)
                            else:
                                cp(dst[:, :, 0:NC], src[:, :, NC - 1::-1])
                                last = cp(dst[:, :, NC:NQ], src[:, :, NQ - 1:NC - 1:-1])
                last.then_inc(s_cp, 1)
            hi(1, b, 6)
            hi(1, b, 7)
            act.wait_ge(k_ps, b + 1)
            if not first:
                act.wait_ge(m_in, b * 128)
            for q in range(2):
                back = ss[0:H, 2 + q, :].rearrange("p (g c) -> p g c", g=4)
                forth = ss[0:H, q, :].rearrange("p (g c) -> p g c", g=4)
                cp(Tl[:, 4 * q:4 * q + 4, 0:128], back)
                last = cp(Tl[:, 4 * q:4 * q + 4, 128:240], forth[:, :, H:128])
            last.then_inc(t_cp, 1)
            act.wait_ge(t_add, b + 1)
            if not first:
                act.wait_ge(y_ps, b)
            for j in range(L):
                act.dma_start(M[H * j:H * j + H, :, :], Tl[:, :, (L - 1 - j) * H:(L - 1 - j) * H + 128])\
                   .then_inc(m_in, 16)
            hi(1, b, 8)
            hi(1, b, 9)
            act.wait_ge(w_used, b * 8 + (U0[1] + 8))
            if not first:
                act.wait_ge(a_done, b)
            a(sg[:, :], ac[:, 3, :], ACT.Sigmoid).then_inc(sig_done, 1)
        repeat(act, NB, conv_turn, peel=1)
        act.wait_ge(cp_done, NB)
        act.wait_ge(a_done, NB)
        for n in range(KW):
            if n >= 4:
                act.wait_ge(hl_done, n - 3)
            cp(hit[:, n % 4, :], Abr[:, sl(n, T)]).then_inc(hit_done, 1)
        act.wait_ge(hl_done, KW)

        def merge(k):
            def body(i):
                for j in range(4):
                    hi(k, i, 3 * j + 2)
                    hi(k, i, 3 * j + 3)
                    act.wait_ge(w_used, i * 12 + (U0[k] + 3 * j + 2))
                    if j:
                        freed(act, k, i, 2 * j - 1)
                    elif not isinstance(i, int) or i:
                        freed(act, k, i - 1, 7)
                    a(gsig[:, :], ac[:, (2 * j) % 4, :], ACT.Sigmoid).then_inc(ac_free[(2 * j) % 4], 1)
                    hi(k, i, 3 * j + 4)
                    if k == 2 and j % 2:
                        act.wait_ge(ge_in, i * 2 + (j + 1) // 2)
                        a(gtm1[:, :], gtm1[:, :], ACT.Tanh, scale=math.sqrt(2.0 / math.pi)).then_inc(ge_th, 1)
            repeat(act, KD // 4, body, peel=1)
        merge(2)

        def glu_turn(i):
            for j in range(4):
                hi(3, i, 4 * j + 2)
                hi(3, i, 4 * j + 3)
                act.wait_ge(w_used, i * 16 + (U0[3] + 4 * j + 2))
                if j or not isinstance(i, int) or i:
                    act.wait_ge(gl_done, i * 4 + j)
                a(gsig[:, :], ac[:, (3 * j) % 4, :], ACT.Sigmoid).then_inc(gl_sig, 1)
                hi(3, i, 4 * j + 4)
                hi(3, i, 4 * j + 5)
                act.wait_ge(w_used, i * 16 + (U0[3] + 4 * j + 4))
                a(gtm1[:, :], ac[:, (3 * j + 2) % 4, :], ACT.Sigmoid).then_inc(ac_free[(3 * j + 2) % 4], 1)
        freed(act, 2, 3, 7)
        act.wait_ge(b2_done, KW)
        repeat(act, KW // 4, glu_turn, peel=1)
        act.wait_ge(gl_done, 8)
        merge(4)

        def f_turn(i):
            for j in range(4):
                hi(5, i, 2 * j + 2)
                hi(5, i, 2 * j + 3)
                act.wait_ge(w_used, i * 8 + (U0[5] + 2 * j + 2))
                cp(fT[:, bass.ds(i * (4 * T) + j * T, T)], ac[:, j, :]).then_inc(ac_free[j], 1)
        repeat(act, KW // 4, f_turn)
        act.wait_ge(gate_out, 16 * (D // GC))
        act.wait_ge(zeroed, 1)
        freed(act, 4, 3, 7)
        for gr in range(FG + 1):
            if gr < FG:
                act.wait_ge(p_ps, gr + 1)
                if gr >= 2:
                    act.wait_ge(pw_done, 2 * gr - 2)
                half = ss[:, gr % 2 * 2:gr % 2 * 2 + 2, :].rearrange("p b (t c) -> p (b t) c", c=FGW)
                cp(pp[:, gr % 2, :, 0:128], half[:, :, 0:128])
                cp(pp[:, gr % 2, :, 129:FGW], half[:, :, 129:FGW])
                cp(p128[:, :, 32 * gr:32 * gr + 1], half[:, :, 128:129]).then_inc(p_cp, 1)
            if gr:
                act.wait_ge(pw_done, 2 * gr - 1)
                act.wait_ge(ac_free[1], A0[6] // 4 + gr - 1)
                cp(gsig[:, :], ac[:, 0, :]).then_inc(ac_free[0], 1)

        def fw_turn(i):
            for j in range(4):
                hi(6, i, 3 * j + 2)
                hi(6, i, 3 * j + 3)
                act.wait_ge(w_used, i * 12 + (U0[6] + 3 * j + 2))
                if j:
                    freed(act, 6, i, 2 * j - 2)
                elif not isinstance(i, int) or i:
                    freed(act, 6, i - 1, 6)
                a(gsig[:, :], ac[:, (2 * j) % 4, :], ACT.Sigmoid).then_inc(zc_sig, 1)
                hi(6, i, 3 * j + 4)
        act.wait_ge(ac_free[1], A0[6] // 4 + MIX)
        repeat(act, KW // 4, fw_turn, peel=1)
        freed(act, 6, 1, 6)
        merge(7)
        for cb in range(4):
            for j in range(2, 10):
                if cb * 8 + j < 32:
                    hi(8, cb, j)
            if cb == 0:
                act.wait_ge(ml_done, KD)
            for t in range(TT):
                if t < 3:
                    act.wait_ge(ac_done, 3 * cb + t + 1)
                else:
                    act.wait_ge(w_used, U0[-1] + 8 * cb + 8)
                if cb or t:
                    act.wait_ge(sq_done, 4 * cb + t)
                a(gtm2[:, :], (ac, ss)[cb % 2][:, t, :], ACT.Square, accum_out=ssq[:, 4 * t + cb:4 * t + cb + 1])\
                    .then_inc(sq_done, 1)
        act.wait_ge(var_done, 2)
        a(small[:, 46:50], small[:, 40:44], ACT.Sqrt).then_inc(rt_done, 1)

    @blk.vector
    def _(dve):
        st = Count(dve, dve_s)
        v = nc.vector
        tt, ts_, stt, cpy = v.tensor_tensor, v.tensor_scalar, v.scalar_tensor_tensor, v.tensor_copy
        link = st.link
        st.link(v.memset(small[:, :], 0.0))
        dve.wait_ge(vec_ps, 1)
        cpy(dtab[:, :], ss[:, 1, 0:G])
        cpy(vecs[:, :], ss[:, 0, 0:V_END]).then_inc(vec_cp, 1)
        dve.wait_ge(vec_cp, 1)
        dve.wait_ge(sg_done, 1)
        tt(cs[:, :, :].rearrange("p k two -> p two k"), vecs[:, V_C:V_END].rearrange("p (two k) -> p two k", two=2),
           small[:, 0:32].rearrange("p (two k) -> p two k", two=2), ALU.mult).then_inc(cs_done, 1)

        MAGIC = 1.5 * 2.0 ** 23

        def nearest(o, i, scale):
            link(ts_(o, i, scale, MAGIC, ALU.mult, ALU.add))
            link(ts_(o, o, MAGIC, None, ALU.subtract))

        def exp(o, i, n, rr, p, q, e):
            link(ts_(q, i, 88.0, -87.0, ALU.min, ALU.max))
            nearest(n, q, 1.0 / math.log(2.0))
            link(stt(rr, n, -0.693145751953125, q, ALU.mult, ALU.add))
            link(stt(rr, n, -1.42860682030941723e-6, rr, ALU.mult, ALU.add))
            link(ts_(p, rr, 1.0 / 5040, 1.0 / 720, ALU.mult, ALU.add))
            for cc in (1.0 / 120, 1.0 / 24, 1.0 / 6, 0.5, 1.0, 1.0):
                link(tt(p, p, rr, ALU.mult))
                link(ts_(p, p, cc, None, ALU.add))
            link(ts_(e, n, 127.0, 8388608.0, ALU.add, ALU.mult))
            link(ts_(q, i, -87.0, None, ALU.is_ge))
            link(tt(p, p, q, ALU.mult))
            link(tt(o, p, e.bitcast(F32), ALU.mult))

        dve.wait_ge(ssm_in, 48)
        a0, a1, a2, a3, a4, a5, a6, a7 = [z[:, :] for z in zt]
        lre, lim = lam[:, 0, :], lam[:, 1, :]
        exp(a7[:, 0:1], ldt[:, :], a1[:, 0:1], a2[:, 0:1], a3[:, 0:1], a4[:, 0:1], ei[:, 0:1])
        link(ts_(a0, lre, a7[:, 0:1], None, ALU.mult))
        exp(a6, a0, a1, a2, a3, a4, ei[:, :])
        link(ts_(a0, lim, a7[:, 0:1], None, ALU.mult))
        nearest(a1, a0, 1.0 / math.pi)
        link(stt(a2, a1, -3.140625, a0, ALU.mult, ALU.add))
        link(stt(a2, a1, -9.67502593994140625e-4, a2, ALU.mult, ALU.add))
        link(stt(a2, a1, -1.509957990978376432e-7, a2, ALU.mult, ALU.add))
        nearest(a3, a1, 0.5)
        link(stt(a3, a3, -2.0, a1, ALU.mult, ALU.add))
        link(tt(a3, a3, a3, ALU.mult))
        link(ts_(a3, a3, -2.0, 1.0, ALU.mult, ALU.add))
        link(tt(a1, a2, a2, ALU.mult))
        fact = [1.0 / math.factorial(n) for n in range(16)]
        link(ts_(a4, a1, fact[13], -fact[11], ALU.mult, ALU.add))
        for cc in (fact[9], -fact[7], fact[5], -fact[3], 1.0):
            link(tt(a4, a4, a1, ALU.mult))
            link(ts_(a4, a4, cc, None, ALU.add))
        link(tt(a4, a4, a2, ALU.mult))
        link(tt(a4, a4, a3, ALU.mult))
        link(ts_(a5, a1, -fact[14], fact[12], ALU.mult, ALU.add))
        for cc in (-fact[10], fact[8], -fact[6], fact[4], -fact[2], 1.0):
            link(tt(a5, a5, a1, ALU.mult))
            link(ts_(a5, a5, cc, None, ALU.add))
        link(tt(a5, a5, a3, ALU.mult))
        z = lambda n: ZN[:, n, 0, :]
        link(tt(z(0), a6, a5, ALU.mult))
        link(tt(z(1), a6, a4, ALU.mult))
        link(ts_(a0, z(0), 1.0, None, ALU.subtract))
        link(tt(a1, lre, lre, ALU.mult))
        link(tt(a2, lim, lim, ALU.mult))
        link(tt(a1, a1, a2, ALU.add))
        link(v.reciprocal(a1, a1))
        link(tt(a2, a0, lre, ALU.mult))
        link(tt(a3, z(1), lim, ALU.mult))
        link(tt(a2, a2, a3, ALU.add))
        link(tt(z(2), a2, a1, ALU.mult))
        link(tt(a2, z(1), lre, ALU.mult))
        link(tt(a3, a0, lim, ALU.mult))
        link(tt(a2, a2, a3, ALU.subtract))
        link(tt(z(3), a2, a1, ALU.mult))

        def square(re, im, s, t):
            link(tt(s, re, re, ALU.mult))
            link(tt(t, im, im, ALU.mult))
            link(tt(im, re, im, ALU.mult))
            link(tt(re, s, t, ALU.subtract))
            link(ts_(im, im, 2.0, None, ALU.mult))
        for _ in range(3):
            square(a5, a4, a0, a1)
            link(tt(a6, a6, a6, ALU.mult))
        cpy(z(4), a5)
        cpy(z(5), a4)
        link(cpy(z(6), a6))
        cpy(ZN[:, :, 1, :], ZN[:, :, 0, :]).then_inc(zn_done, 1)
        dve.wait_ge(p0_ps, 1)
        col = lambda n: ss[:, n // 4, (n % 4) * 128:(n % 4 + 1) * 128]
        dbg = lambda ap: ap.rearrange("p (d b g) -> p d b g", b=NB, d=2)
        bdg = lambda ap: ap.rearrange("p (b d g) -> p d b g", b=NB, d=2)
        cpy(bdg(Ar[:, 1, :]), dbg(col(0)))
        cpy(bdg(Ai[:, 1, :]), dbg(col(1)))
        cpy(bdg(q2[:, 0, :]), dbg(col(2)))
        cpy(bdg(q2[:, 1, :]), dbg(col(3)))
        for n, dst in ((4, PWr[:, 0, :]), (5, PWi[:, 0, :]), (6, R8[:, :])):
            for s in range(2):
                pr = slice(64 * s, 64 * s + 64)
                last = cpy(dst[pr].rearrange("p (b d l) -> p d b l", b=NB, d=2),
                           col(n)[pr].rearrange("p (d b l s) -> p d b l s", b=NB, d=2, s=2)[:, :, :, :, s])
        last.then_inc(p0_cp, 1)
        dve.wait_ge(p0_cp, 1)
        v.memset(Ar[:, 0, :], 1.0)
        link(v.memset(Ai[:, 0, :], 0.0))
        for n0, m in ((1, 1), (2, 2), (4, 4)):
            mr, mi = (A[:, n0:n0 + 1, :].to_broadcast([128, m, 128]) for A in (Ar, Ai))
            sr, si = Ar[:, 1:1 + m, :], Ai[:, 1:1 + m, :]
            dr, di = Ar[:, n0 + 1:n0 + 1 + m, :], Ai[:, n0 + 1:n0 + 1 + m, :]
            ta = tq[:, 0:8 * m, :].rearrange("p (m a) h -> p m (a h)", m=m)
            tb = tq[:, 32:32 + 8 * m, :].rearrange("p (m a) h -> p m (a h)", m=m)
            tt(dr, sr, mr, ALU.mult)
            tt(di, sr, mi, ALU.mult)
            tt(ta, si, mi, ALU.mult)
            link(tt(tb, si, mr, ALU.mult))
            tt(dr, dr, ta, ALU.subtract)
            link(tt(di, di, tb, ALU.add))
        for n in range(6):
            re, im = PWr[:, n, :], PWi[:, n, :]
            tt(PWr[:, n + 1, :], re, re, ALU.mult)
            tt(a0, im, im, ALU.mult)
            link(tt(a1, re, im, ALU.mult))
            tt(PWr[:, n + 1, :], PWr[:, n + 1, :], a0, ALU.subtract)
            ts_(PWi[:, n + 1, :], a1, 2.0, None, ALU.mult).then_inc(pw_tab, 1)
            dve.wait_ge(pw_tab, n + 1)
        dve.wait_ge(brw_done, 1)
        qb = lambda n: q2[:, n, :].unsqueeze(2).to_broadcast([128, 128, H])
        tt(tq[:, :, :], Brw2[:, :, :], qb(1), ALU.mult)
        link(tt(B1[:, :, :], Braw[:, :, :], qb(0), ALU.mult))
        tt(B1[:, :, :], B1[:, :, :], tq[:, :, :], ALU.add).then_inc(bb_done, 1)
        dve.wait_ge(act_s, 6)
        ts_(small[:, 40:46], small[:, 32:38], 1.0 / D, EPS, ALU.mult, ALU.add).then_inc(var_done, 1)
        dve.wait_ge(var_done, 1)

        def rsqrt(n, rt):
            dve.wait_ge(rt_done, rt)
            s40, s46, s52 = small[:, 40:40 + n], small[:, 46:46 + n], small[:, 52:52 + n]
            link(v.reciprocal(s52, s46))
            link(tt(s46, s52, s52, ALU.mult))
            link(tt(s46, s46, s40, ALU.mult))
            link(ts_(s46, s46, -0.5, 1.5, ALU.mult, ALU.add))
            return tt(s52, s52, s46, ALU.mult)
        rsqrt(6, 1).then_inc(rs_done, 1)

        dve.wait_ge(col_ps, 2)
        mod = vmod
        for h, vb in ((0, 16), (1, 0)):
            last = tt(mod[:, h], ss[:, 0, 32 * h:32 * h + 32].rearrange("p (k two) -> p k two", two=2),
                      vecs[:, V_BADA + vb:V_BADA + vb + 16].unsqueeze(2).to_broadcast([128, KD, 2]), ALU.add)
        link(last)
        stt(mod[:, 0], mod[:, 0], 1.0, vecs[:, V_GPRE:V_GPRE + 16].unsqueeze(2).to_broadcast([128, KD, 2]),
            ALU.add, ALU.mult).then_inc(col_cp, 1)
        dve.wait_ge(col_cp, 1)
        def context_lo(k):
            dve.wait_ge(hh_done, k + 1)
            tt(hcl[:, k, :], htmp[:, k % 3, T:TU], hch[:, k, :].bitcast(F32), ALU.subtract).then_inc(hc_done, 1)
        for k in range(KD):
            dve.wait_ge(h_ps, k + 1)
            b = 2 * (k % 2)
            o = htmp[:, k % 3, :]
            if k >= 3:
                dve.wait_ge(h_done, k - 2)
                dve.wait_ge(hc_done, k - 2)
            ts_(o[:, 0:T], ss[:, b, :], mod[:, 0, k, 0:1], mod[:, 1, k, 0:1], ALU.mult, ALU.add)
            ts_(o[:, T:TU], ss[:, b + 1, 0:TC], mod[:, 0, k, 1:2], mod[:, 1, k, 1:2], ALU.mult, ALU.add)\
                .then_inc(ht_done, 1)
            if k:
                context_lo(k - 1)
        context_lo(KD - 1)

        def powers(dst, A, e0, n, rev, b, d, T1, T2, tmp):
            shape = [128, GB, n, H]
            cols = slice(d * 8, d * 8 + 8)
            es = slice(e0, e0 + n)
            br, bi = (A_[:, es, cols].rearrange("p e g -> p g e").unsqueeze(3).to_broadcast(shape) for A_ in A)
            o = dst.rearrange("p g (m h) -> p g m h", h=H)
            if rev:
                o, tmp = o[:, :, ::-1, :], tmp[:, :, ::-1, :]
            w1, w2 = (q.unsqueeze(2).to_broadcast(shape) for q in (T1, T2))
            tt(o, br, w1, ALU.mult)
            return tt(tmp, bi, w2, ALU.mult), o

        def conv_turn(b):
            dyn = not isinstance(b, int)
            dve.wait_ge(bc2, b + 1)
            if dyn or b:
                dve.wait_ge(k_ps, b)
                dve.wait_ge(y_ps, b)
            for d in range(2):
                tmp = t1[:, d * 1152:d * 1152 + 1024].rearrange("p (g m h) -> p g m h", g=GB, m=L)
                last, o = powers(V[:, d], (tAr, tAi), 0, L, d == 0, b, d, tB1[:, d * 8:d * 8 + 8, :],
                                 B2[:, d], tmp)
            link(last)
            for d in range(2):
                tmp = t1[:, d * 1152:d * 1152 + 1024]
                o = V[:, d].rearrange("p g m -> p (g m)")
                last = tt(o, o, tmp, ALU.add)
            last.then_inc(v_done, 1)
            dve.wait_ge(v_done, b + 1)
            for d in range(2):
                tmp = t1[:, d * 1152:d * 1152 + 1152].rearrange("p (g m h) -> p g m h", g=GB, m=L + 1)
                last, o = powers(Cp[:, d], (tAr, tAi), 0, L + 1, d == 1, b, d,
                                 tC1[:, d * 8:d * 8 + 8, :], C2[:, d], tmp)
            link(last)
            for d in range(2):
                o = Cp[:, d].rearrange("p g m -> p (g m)")
                last = tt(o, o, t1[:, d * 1152:(d + 1) * 1152], ALU.add)
            last.then_inc(cp_done, 1)
            dve.wait_ge(cp_done, b + 1)
            dve.wait_ge(w_used, b * 8 + (U0[1] + 4))
            freed(dve, 1, b, 0)
            tt(cv[:, :], ac[:, 1, :], xas[:, :], ALU.mult).then_inc(ac_free[1], 1)
            freed(dve, 1, b, 1)
            dve.wait_ge(u_in, b * (16 * L) + 16 * L)
            if dyn or b:
                dve.wait_ge(y_out, b * (16 * L))
            tt(ys[:, :, :], U[:, :, NC:NQ], dtab[:, sl(b, GB)].unsqueeze(2).to_broadcast([128, GB, NX]), ALU.mult)\
                .then_inc(us_done, 1)
            cw = lambda k: vcv[:, bass.ds(b * 3 + k, 1)]
            rows_of = lambda q: q[:, :].rearrange("p (r c) -> p r c", c=GRID)
            link(ts_(cy[:, :], cv[:, :], cw(1), None, ALU.mult))
            y3, c3 = rows_of(cy), rows_of(cv)
            link(stt(y3[:, :, 1:], c3[:, :, :GRID - 1], cw(0), y3[:, :, 1:], ALU.mult, ALU.add))
            link(stt(y3[:, :, :GRID - 1], c3[:, :, 1:], cw(2), y3[:, :, :GRID - 1], ALU.mult, ALU.add))
            dve.wait_ge(s_cp, 2 * b + 2)
            dve.wait_ge(ph_done, b + 1)
            f = lambda q: q.rearrange("p d l c -> p (d l c)")
            sr, si, pr, pi, zr, zi = (f(q[:, ri]) for q in (S, PH, Z) for ri in range(2))
            n = 2 * PB * NQ
            tt(zr, pr, sr, ALU.mult)
            tt(zi, pr, si, ALU.mult)
            tt(t1[:, 0:n], pi, si, ALU.mult)
            link(tt(t1[:, n:2 * n], pi, sr, ALU.mult))
            tt(zr, zr, t1[:, 0:n], ALU.add)
            link(tt(zi, zi, t1[:, n:2 * n], ALU.subtract))
            for ri in range(2):
                for d in range(2):
                    for l in range(PB):
                        q = Z[:, ri, d, l, :]
                        rr = R8[:, bass.ds(b * 8 + d * 4 + l, 1)]
                        last = v.tensor_tensor_scan(S[:, ri, d, l, :], rr.to_broadcast([128, NQ]), q, 0.0,
                                                    ALU.mult, ALU.add)
            link(last)
            w = slice(NC - 1, NQ - 1)
            ta, tb = (t1[:, n * i:n * i + 512].rearrange("p (d l c) -> p d l c", d=2, l=PB) for i in range(2))
            g3 = lambda q: q.rearrange("p d l c -> p (d l) c")
            P_, S_ = (lambda ri: g3(PH[:, ri])[:, :, w]), (lambda ri: g3(S[:, ri])[:, :, w])
            xs = []
            for ri in range(2):
                oa, ob = (t1[:, (2 * ri + k) * 512:(2 * ri + k + 1) * 512] for k in range(2))
                oa3, ob3 = (q.rearrange("p (m c) -> p m c", c=NX) for q in (oa, ob))
                tt(oa3, P_(0), S_(ri), ALU.mult)
                last = tt(ob3, P_(1), S_(1 - ri), ALU.mult)
            link(last)
            for ri in range(2):
                op = ALU.subtract if ri == 0 else ALU.add
                for s in range(2):
                    for d in range(2):
                        oa, ob = (t1[64 * s:64 * s + 64, (2 * ri + k) * 512 + d * 256:(2 * ri + k) * 512 + d * 256 + 256]
                                  .rearrange("p (l c) -> p l c", l=PB) for k in range(2))
                        dst = X[64 * ri:64 * ri + 64, d, :, s, :]
                        last = tt(dst if d == 0 else dst[:, :, ::-1], oa, ob, op)
            last.then_inc(x_done, 1)
            dve.wait_ge(t_cp, b + 1)
            for q in range(2):
                o = Tl[:, 4 * q:4 * q + 4, 112:128]
                last = tt(o, o, ss[0:H, q, :].rearrange("p (g c) -> p g c", g=4)[:, :, 0:H], ALU.add)
            last.then_inc(t_add, 1)
            dve.wait_ge(w_used, b * 8 + (U0[1] + 8))
            dve.wait_ge(sig_done, b + 1)
            tt(cy[:, :], cy[:, :], ac[:, 2, :], ALU.mult).then_inc(ac_free[2], 1)
            tt(sg[:, :], sg[:, :], ac[:, 3, :], ALU.mult).then_inc(ac_free[3], 1)
            freed(dve, 1, b, 2)
            freed(dve, 1, b, 3)
            tt(Abr[:, sl(b, T)], cy[:, :], sg[:, :], ALU.mult).then_inc(a_done, 1)
            dve.wait_ge(y_ps, b + 1)
            dve.wait_ge(us_done, b + 1)
            yo = ys[:, :, :].rearrange("p g c -> p (g c)")
            tt(yo, yo, ss[:, 0, :], ALU.add).then_inc(y_pre, 1)
        st.add(cpy(vcv[:, :].rearrange("p (b k) -> p k b", k=3),
                   vecs[:, V_CONV:V_CONV + 24].rearrange("p (k b) -> p k b", k=3)))
        st.wait()
        dve.wait_ge(w_used, U0[1])
        dve.wait_ge(tab_out, 16 * TAB_STORES)
        for j in range(2):
            dve.wait_ge(u_out[j], 8 * NB)
        repeat(dve, NB, conv_turn, [(st, CONV_STEPS)], peel=1)
        dve.wait_ge(a_done, NB)
        dve.wait_ge(y_pre, NB)
        dve.wait_ge(y_ps, NB)
        dve.wait_ge(m_in, 128 * NB)
        dve.wait_ge(y_out, 16 * L * NB)
        for n in range(KW):
            src = Abr[:, sl(n, T)]
            dve.wait_ge(hit_done, n + 1)
            tt(bal[:, n, :], src, hit[:, n % 4, :].bitcast(F32), ALU.subtract).then_inc(hl_done, 1)
            cpy(bah[:, n, :], src).then_inc(hs_done, 1)
        dve.wait_ge(y_in, 16)

        def split(hi, lo, src=gt[:, :]):
            link(cpy(hi, src))
            return tt(lo, src, hi.bitcast(F32), ALU.subtract)

        by_place = lambda q: q.rearrange("p (c l) -> p l c", l=L)

        def gelu_in(b):
            y = yin[:, bass.ds(b * T, T)].rearrange("p (l c) -> p l c", c=NX)
            o = by_place(gtm1[:, :])
            link(tt(o, y, y, ALU.mult))
            link(ts_(gtm1[:, :], gtm1[:, :], 0.044715, 1.0, ALU.mult, ALU.add))
            tt(o, o, y, ALU.mult).then_inc(ge_in, 1)

        def gelu_out(b):
            y = yin[:, bass.ds(b * T, T)].rearrange("p (l c) -> p l c", c=NX)
            dve.wait_ge(ge_th, b + 1)
            link(stt(by_place(gt[:, :]), by_place(gtm1[:, :]), 1.0, y, ALU.add, ALU.mult))
            link(ts_(gt[:, :], gt[:, :], 0.5, None, ALU.mult))
            o = b2nd[:, bass.ds(b, 1), :, :].rearrange("p a h t -> p (a h) t")
            split(o[:, 0, :], o[:, 1, :]).then_inc(b2_done, 1)

        def merge(k, br):
            def body(i):
                for j in range(4):
                    o = mT[:, bass.ds(i * (4 * T) + j * T, T)]
                    freed(dve, k, i, 2 * j)
                    dve.wait_ge(w_used, i * 12 + (U0[k] + 3 * j + 3))
                    free = ac_free[(2 * j + 1) % 4]
                    if br and (j or not isinstance(i, int) or i):
                        dve.wait_ge(m_done, i * 4 + (16 * (br - 1) + j))
                    tt(o if br == 0 else gtm2[:, :], ac[:, (2 * j + 1) % 4, :], gsig[:, :], ALU.mult)\
                        .then_inc(free, 1)
                    if br == 0 and j % 2:
                        gelu_in(i * 2 + j // 2)
                        gelu_out(i * 2 + j // 2)
                    if br:
                        freed(dve, k, i, 2 * j + 1)
                        tt(o if br == 1 else gt[:, :], o, gtm2[:, :], ALU.add).then_inc(m_done, 1)
                    if br == 2:
                        dve.wait_ge(m_done, i * 4 + (16 + j + 1))
                        n = bass.ds(i * 4 + j, 1)
                        split(mhi[:, n, :].rearrange("p a t -> p (a t)"),
                              mlo[:, n, :].rearrange("p a t -> p (a t)")).then_inc(ml_done, 1)
            repeat(dve, KD // 4, body, [(st, (10, 0, 4)[br])], peel=(1 if br == 1 else 0))
        merge(2, 0)
        freed(dve, 2, 3, 5)
        freed(dve, 2, 3, 7)

        def glu_turn(i):
            for j in range(4):
                za, wa, wb = ((3 * j + q) % 4 for q in range(3))
                dve.wait_ge(gl_sig, i * 4 + (j + 1))
                dve.wait_ge(w_used, i * 16 + (U0[3] + 4 * j + 4))
                tt(gtm2[:, :], ac[:, za, :], gsig[:, :], ALU.mult).then_inc(ac_free[za], 1)
                freed(dve, 3, i, 3 * j + 2)
                tt(gtm1[:, :], ac[:, wa, :], gtm1[:, :], ALU.mult).then_inc(ac_free[wa], 1)
                freed(dve, 3, i, 3 * j)
                freed(dve, 3, i, 3 * j + 1)
                tt(gt[:, :], gtm1[:, :], gtm2[:, :], ALU.mult).then_inc(gl_done, 1)
                dve.wait_ge(gl_done, i * 4 + (j + 1))
                n = bass.ds(i * 4 + j, 1)
                split(bah[:, n, :].rearrange("p a t -> p (a t)"),
                      bal[:, n, :].rearrange("p a t -> p (a t)")).then_inc(ba_done, 1)
        repeat(dve, KW // 4, glu_turn, [(st, 4)])
        merge(4, 1)
        v.memset(p128[:, :, :], 0.0)
        dve.wait_ge(dft_in, 32)
        dve.wait_ge(gate_out, 16 * (D // GC))
        v.memset(pp[:, :, :, 128:129].rearrange("p a t c -> p (a t) c"), 0.0).then_inc(zeroed, 1)
        for gr in range(FG):
            dve.wait_ge(ac_free[0], A0[6] // 4 + gr + 1)
            dve.wait_ge(pw_done, 2 * gr + 2)
            link(tt(gt[:, :], ac[:, 1, :], gsig[:, :], ALU.add))
            tt(gtm2[:, :], gsig[:, :], ac[:, 1, :], ALU.subtract).then_inc(ac_free[1], 1)
            split(b2nd[:, 2 * gr, 0, :], b2nd[:, 2 * gr, 1, :])
            dve.wait_ge(ac_free[1], A0[6] // 4 + gr + 1)
            link(split(b2nd[:, 2 * gr + 1, 0, :], b2nd[:, 2 * gr + 1, 1, :], gtm2[:, :]))
        dve.wait_ge(y128_ps, 1)
        for gr in range(FG):
            link(cpy(gt[0:1, :], ss[32 * gr:32 * gr + 1, 0, :]))
            last = split(b2nd[0:1, 2 * gr + 1, 0, :], b2nd[0:1, 2 * gr + 1, 1, :], gt[0:1, :])
            if gr < FG - 1:
                link(last)
        last.then_inc(mix_done, 1)

        def fw_turn(i):
            for j in range(4):
                zc, fw = (2 * j) % 4, (2 * j + 1) % 4
                dve.wait_ge(zc_sig, i * 4 + (j + 1))
                tt(gtm2[:, :], ac[:, zc, :], gsig[:, :], ALU.mult).then_inc(ac_free[zc], 1)
                freed(dve, 6, i, 2 * j)
                dve.wait_ge(w_used, i * 12 + (U0[6] + 3 * j + 3))
                tt(gt[:, :], ac[:, fw, :], gtm2[:, :], ALU.mult).then_inc(ac_free[fw], 1)
                freed(dve, 6, i, 2 * j + 1)
                n = bass.ds(i * 4 + j, 1)
                split(bah[:, n, :].rearrange("p a t -> p (a t)"),
                      bal[:, n, :].rearrange("p a t -> p (a t)")).then_inc(ba_done, 1)
        repeat(dve, KW // 4, fw_turn, [(st, 4)])
        merge(7, 2)
        flat = ss[:, :, :].rearrange("p q c -> p (q c)")
        dve.wait_ge(gb_ps, 1)
        cpy(GG[:, :], flat).then_inc(gg_done, 1)
        dve.wait_ge(gg_done, 1)
        dve.wait_ge(gpr_ps, 1)
        tt(GG[:, :], GG[:, :], flat, ALU.mult).then_inc(gg_done, 1)
        dve.wait_ge(gg_done, 2)
        for cb in range(4):
            for t in range(TT):
                dve.wait_ge(sq_done, 4 * cb + t + 1)
                w = slice(cb * 512, cb * 512 + 512)
                tt(Og[:, t, w], (ac, ss)[cb % 2][:, t, :], GG[:, w], ALU.mult).then_inc(o_free, 1)
        link(v.tensor_reduce(small[:, 40:44], ssq[:, :].rearrange("p (t c) -> p t c", t=TT),
                             mybir.AxisListType.X, ALU.add))
        ts_(small[:, 40:44], small[:, 40:44], 1.0 / D, EPS, ALU.mult, ALU.add).then_inc(var_done, 1)
        dve.wait_ge(var_done, 2)
        link(rsqrt(4, 2))
        dve.wait_ge(o_free, 4 * TT)
        dve.wait_ge(xr_in, 64)
        for t in range(TT):
            for h in range(2):
                o = Og[:, t, h * D // 2:(h + 1) * D // 2]
                stt(o, o, small[:, 52 + t:53 + t], xr[:, t, h * D // 2:(h + 1) * D // 2], ALU.mult, ALU.add)\
                    .then_inc(o_done, 1)

    block.__exit__(None, None, None)


EXTRAS = (5, 6, 8, 9, 11, 13, 15, 17, 19, 21)
CONV_STEPS = 9
TAB_STORES = 2 * (L + 1) + 2

NAMES = ['x', 'c', 'ctx', 'c_ctx', 'w_ada', 'b_ada', 'g_pre', 'g_post', 'w_in', 'conv_w', 'ssm_lam_re',
         'ssm_lam_im', 'ssm_log_dt', 'ssm_b_re', 'ssm_b_im', 'ssm_c_re', 'ssm_c_im', 'ssm_d', 'glu_wa', 'glu_wb',
         'fourier_w', 'proj_a', 'proj_b', 'proj_c', 'w_out']


def fourier_tables():
    k = np.arange(FGW)
    w = 2 * np.pi * (np.outer(k, k) % FGW) / FGW
    dft_w = np.concatenate([np.cos(w)[:, 0:FGW // 2 + 1], np.sin(w)[:, 1:FGW // 2]], 1) / np.sqrt(FGW)
    k = np.arange(T)
    w = 2 * np.pi * (np.outer(k, k) % T) / T
    dft_t = np.stack([np.cos(w), -np.sin(w)]) / np.sqrt(T)
    return dft_w.astype(np.float32), dft_t.astype(np.float32)


def kernel(**inputs):
    import concourse.bacc as bacc
    from concourse.bass_utils import run_bass_kernel_spmd

    nc = bacc.Bacc("TRN2", target_bir_lowering=False, num_devices=1)
    dft_w, dft_t = fourier_tables()
    arrays, args = {}, []
    for name in NAMES:
        arrays[name] = np.ascontiguousarray(inputs[name])
    arrays["dft_w"], arrays["dft_t"] = dft_w, dft_t
    for name, a in arrays.items():
        args.append(nc.dram_tensor(name, a.shape, mybir.dt.from_np(a.dtype), kind="ExternalInput").ap())
    args.append(nc.dram_tensor("out", (1, T, D), F32, kind="ExternalOutput").ap())
    program(nc, *args)
    r = run_bass_kernel_spmd(nc, [arrays], core_ids=[0])
    return r.results[0]["out"]
```
